# Optimizing a Trainium2 kernel written in Bass

```python
import math
import jax, jax.numpy as jnp
from jax import lax
import numpy as np

D_MODEL = 1024
BATCH = 1
SEQ = 256
DEPTH = 2

CHUNK = 64
Q_BLOCK = 128
N_MEM = 256
H_A = 4
DQK_A = 64
DV_A = 2 * DQK_A
H_B = 4
DH_B = 64
LEFT_CHUNKS = 8
REL_MAX = 128
H_C = 4
DH_C = 64
H_IDX = 8
D_IDX = 64
TOPK_MAX = 256
D_MIX = H_A * DV_A + H_B * DH_B + H_C * DH_C
SPLITS = (H_A * 2 * DQK_A, H_A * 2 * DQK_A, H_A * DV_A,
          H_B * DH_B, H_B * DH_B, H_B * DH_B,
          H_C * DH_C, H_C * DH_C, H_C * DH_C,
          H_IDX * D_IDX, D_IDX, H_IDX)
N_IN = sum(SPLITS)
H_X = 4
DH_X = D_MODEL // H_X
D_FF = 2816
N_EXPERTS = 8
TOP_K = 2
D_FF_E = 3584
ALPHA = (2.0 * DEPTH) ** 0.25
BETA = (8.0 * DEPTH) ** -0.25
LN_EPS = 1e-5
RMS_EPS = 1e-6
NEG_INF = -1e30

kernel_name = "hybrid_chunk_causal_diff_band_dsa_moe_encoder"

def _layer_norm(x, g, b):
    xf = x.astype(jnp.float32)
    mu = jnp.mean(xf, axis=-1, keepdims=True)
    var = jnp.mean(jnp.square(xf - mu), axis=-1, keepdims=True)
    y = (xf - mu) * lax.rsqrt(var + LN_EPS) * g.astype(jnp.float32) + b.astype(jnp.float32)
    return y.astype(x.dtype)

def _alibi_slopes():
    n = H_A + H_C
    s = jnp.asarray(2.0 ** (-8.0 * np.arange(1, n + 1) / n), dtype=jnp.float32)
    return s[0::2], s[1::2]

def _chunk_allowed(qpos, kpos):
    return (kpos[None, :] // CHUNK) <= (qpos[:, None] // CHUNK)

def _diff_attention(qa, ka, va, lam, lam_init, gain, slopes):
    b, s_len = qa.shape[0], qa.shape[1]
    nb = s_len // Q_BLOCK
    q_blocks = jnp.swapaxes(qa.reshape(b, nb, Q_BLOCK, H_A, 2, DQK_A), 0, 1)
    kpos = jnp.arange(s_len)
    scale = DQK_A ** -0.5

    def block(args):
        qb, i = args
        qpos = i * Q_BLOCK + jnp.arange(Q_BLOCK)
        sc = jnp.einsum('bqhmd,bkhmd->bhmqk', qb, ka).astype(jnp.float32) * scale
        dist = jnp.abs(qpos[:, None] - kpos[None, :]).astype(jnp.float32)
        sc = sc - slopes[None, :, None, None, None] * dist
        sc = jnp.where(_chunk_allowed(qpos, kpos), sc, NEG_INF)
        p = jax.nn.softmax(sc, axis=-1)
        a = p[:, :, 0] - lam * p[:, :, 1]
        return jnp.einsum('bhqk,bkhe->bqhe', a.astype(va.dtype), va)

    o = lax.map(block, (q_blocks, jnp.arange(nb)))
    o = jnp.swapaxes(o, 0, 1).reshape(b, s_len, H_A, DV_A).astype(jnp.float32)
    o = o * lax.rsqrt(jnp.mean(jnp.square(o), axis=-1, keepdims=True) + RMS_EPS)
    o = o * gain.astype(jnp.float32) * (1.0 - lam_init)
    return o.reshape(b, s_len, H_A * DV_A).astype(va.dtype)

def _band_attention(qb, kb, vb, table):
    b, s_len = qb.shape[0], qb.shape[1]
    nc = s_len // CHUNK
    left = LEFT_CHUNKS * CHUNK
    band = (LEFT_CHUNKS + 1) * CHUNK
    qc = qb.reshape(b, nc, CHUNK, H_B, DH_B)

    def gather_band(t):
        tp = jnp.pad(t, ((0, 0), (left, 0), (0, 0), (0, 0)))
        tp = tp.reshape(b, nc + LEFT_CHUNKS, CHUNK, H_B, DH_B)
        return jnp.concatenate([tp[:, j:j + nc] for j in range(LEFT_CHUNKS + 1)], axis=2)

    kband = gather_band(kb)
    vband = gather_band(vb)
    sc = jnp.einsum('bcqhd,bckhd->bchqk', qc, kband).astype(jnp.float32) * DH_B ** -0.5
    qi = jnp.arange(CHUNK)
    kj = jnp.arange(band)
    rel = qi[:, None] - (kj[None, :] - left)
    bias = table[:, jnp.clip(rel, -REL_MAX, REL_MAX) + REL_MAX].astype(jnp.float32)
    kabs = jnp.arange(nc)[:, None] * CHUNK + kj[None, :] - left
    sc = sc + bias[None, None]
    sc = jnp.where((kabs >= 0)[None, :, None, None, :], sc, NEG_INF)
    p = jax.nn.softmax(sc, axis=-1)
    o = jnp.einsum('bchqk,bckhd->bcqhd', p.astype(vb.dtype), vband)
    return o.reshape(b, s_len, H_B * DH_B)

def _dsa_attention(qc, kc, vc, qi, ki, wi, slopes):
    b, s_len = qc.shape[0], qc.shape[1]
    nb = s_len // Q_BLOCK
    topk = min(TOPK_MAX, s_len // 4)
    kpos = jnp.arange(s_len)

    def to_blocks(t):
        return jnp.swapaxes(t.reshape((b, nb, Q_BLOCK) + t.shape[2:]), 0, 1)

    def block(args):
        qb, qib, wib, i = args
        qpos = i * Q_BLOCK + jnp.arange(Q_BLOCK)
        dots = jnp.einsum('bqhd,bsd->bqhs', qib, ki).astype(jnp.float32) * D_IDX ** -0.5
        isc = jnp.einsum('bqhs,bqh->bqs', jax.nn.relu(dots), wib.astype(jnp.float32)) * H_IDX ** -0.5
        isc = jnp.where(_chunk_allowed(qpos, kpos)[None], isc, NEG_INF)
        top_val, top_idx = lax.top_k(isc, topk)
        kg = jax.vmap(lambda t, ix: t[ix])(kc, top_idx)
        vg = jax.vmap(lambda t, ix: t[ix])(vc, top_idx)
        sc = jnp.einsum('bqhd,bqkhd->bhqk', qb, kg).astype(jnp.float32) * DH_C ** -0.5
        dist = jnp.abs(qpos[None, :, None] - top_idx).astype(jnp.float32)
        sc = sc - slopes[None, :, None, None] * dist[:, None]
        sc = jnp.where((top_val > 0.5 * NEG_INF)[:, None], sc, NEG_INF)
        p = jax.nn.softmax(sc, axis=-1)
        return jnp.einsum('bhqk,bqkhd->bqhd', p.astype(vc.dtype), vg)

    o = lax.map(block, (to_blocks(qc), to_blocks(qi), to_blocks(wi), jnp.arange(nb)))
    return jnp.swapaxes(o, 0, 1).reshape(b, s_len, H_C * DH_C)

def _hybrid_mixer(h, w_in, lq1, lk1, lq2, lk2, dgain, rel_table, w_out, layer_idx, slopes_a, slopes_c):
    b, s_len, _ = h.shape
    proj = h @ w_in
    offsets = [int(o) for o in np.cumsum(SPLITS)[:-1]]
    qa, ka, va, qb, kb, vb, qc, kc, vc, qi, ki, wi = jnp.split(proj, offsets, axis=-1)
    lam_init = 0.8 - 0.6 * math.exp(-0.3 * layer_idx)
    lam = (jnp.exp(jnp.sum(lq1.astype(jnp.float32) * lk1.astype(jnp.float32)))
           - jnp.exp(jnp.sum(lq2.astype(jnp.float32) * lk2.astype(jnp.float32))) + lam_init)
    ya = _diff_attention(qa.reshape(b, s_len, H_A, 2, DQK_A), ka.reshape(b, s_len, H_A, 2, DQK_A),
                         va.reshape(b, s_len, H_A, DV_A), lam, lam_init, dgain, slopes_a)
    yb = _band_attention(qb.reshape(b, s_len, H_B, DH_B), kb.reshape(b, s_len, H_B, DH_B),
                         vb.reshape(b, s_len, H_B, DH_B), rel_table)
    yc = _dsa_attention(qc.reshape(b, s_len, H_C, DH_C), kc.reshape(b, s_len, H_C, DH_C),
                        vc.reshape(b, s_len, H_C, DH_C), qi.reshape(b, s_len, H_IDX, D_IDX),
                        ki, wi, slopes_c)
    return jnp.concatenate([ya, yb, yc], axis=-1) @ w_out

def _mem_cross_attention(h, mem, wq, wk, wv, wo):
    b, s_len, _ = h.shape
    q = (h @ wq).reshape(b, s_len, H_X, DH_X)
    k = (mem @ wk).reshape(b, -1, H_X, DH_X)
    v = (mem @ wv).reshape(b, -1, H_X, DH_X)
    sc = jnp.einsum('bqhd,bkhd->bhqk', q, k).astype(jnp.float32) * DH_X ** -0.5
    p = jax.nn.softmax(sc, axis=-1)
    o = jnp.einsum('bhqk,bkhd->bqhd', p.astype(v.dtype), v).reshape(b, s_len, D_MODEL)
    return o @ wo

def _swiglu(h, w1, w3, w2):
    return (jax.nn.silu(h @ w1) * (h @ w3)) @ w2

def _moe(h, router, w1, w3, w2):
    b, s_len, d = h.shape
    t = h.reshape(-1, d)
    logits = (t @ router).astype(jnp.float32)
    top_val, top_idx = lax.top_k(logits, TOP_K)
    gates = jax.nn.softmax(top_val, axis=-1)
    gate_full = jnp.sum(jax.nn.one_hot(top_idx, N_EXPERTS, dtype=jnp.float32) * gates[..., None], axis=1)
    out = jnp.zeros_like(t)
    for e in range(N_EXPERTS):
        out = out + gate_full[:, e:e + 1].astype(t.dtype) * _swiglu(t, w1[e], w3[e], w2[e])
    return out.reshape(b, s_len, d)

def setup_inputs(seed: int = 0) -> dict:
    key = jax.random.key(seed)
    ks = jax.random.split(key, 27)

    def nrm(k, shape, scale):
        return jax.random.normal(k, shape, jnp.float32) * scale

    n_dense = (DEPTH + 1) // 2
    n_moe = DEPTH // 2
    return {
        'x': nrm(ks[0], (BATCH, SEQ, D_MODEL), 1.0),
        'mem': nrm(ks[1], (BATCH, N_MEM, D_MODEL), 1.0),
        'w_in': nrm(ks[2], (DEPTH, D_MODEL, N_IN), D_MODEL ** -0.5),
        'lam_q1': nrm(ks[3], (DEPTH, DQK_A), 0.1),
        'lam_k1': nrm(ks[4], (DEPTH, DQK_A), 0.1),
        'lam_q2': nrm(ks[5], (DEPTH, DQK_A), 0.1),
        'lam_k2': nrm(ks[6], (DEPTH, DQK_A), 0.1),
        'diff_norm_g': 1.0 + nrm(ks[7], (DEPTH, DV_A), 0.02),
        'rel_bias': nrm(ks[8], (DEPTH, H_B, 2 * REL_MAX + 1), 0.1),
        'w_out': nrm(ks[9], (DEPTH, D_MIX, D_MODEL), D_MIX ** -0.5 * BETA),
        'ln1_g': 1.0 + nrm(ks[10], (DEPTH, D_MODEL), 0.02),
        'ln1_b': nrm(ks[11], (DEPTH, D_MODEL), 0.02),
        'xattn_wq': nrm(ks[12], (DEPTH, D_MODEL, D_MODEL), D_MODEL ** -0.5),
        'xattn_wk': nrm(ks[13], (DEPTH, D_MODEL, D_MODEL), D_MODEL ** -0.5),
        'xattn_wv': nrm(ks[14], (DEPTH, D_MODEL, D_MODEL), D_MODEL ** -0.5),
        'xattn_wo': nrm(ks[15], (DEPTH, D_MODEL, D_MODEL), D_MODEL ** -0.5 * BETA),
        'ln2_g': 1.0 + nrm(ks[16], (DEPTH, D_MODEL), 0.02),
        'ln2_b': nrm(ks[17], (DEPTH, D_MODEL), 0.02),
        'ffn_w1': nrm(ks[18], (n_dense, D_MODEL, D_FF), D_MODEL ** -0.5),
        'ffn_w3': nrm(ks[19], (n_dense, D_MODEL, D_FF), D_MODEL ** -0.5),
        'ffn_w2': nrm(ks[20], (n_dense, D_FF, D_MODEL), D_FF ** -0.5 * BETA),
        'moe_router': nrm(ks[21], (n_moe, D_MODEL, N_EXPERTS), D_MODEL ** -0.5),
        'moe_w1': nrm(ks[22], (n_moe, N_EXPERTS, D_MODEL, D_FF_E), D_MODEL ** -0.5),
        'moe_w3': nrm(ks[23], (n_moe, N_EXPERTS, D_MODEL, D_FF_E), D_MODEL ** -0.5),
        'moe_w2': nrm(ks[24], (n_moe, N_EXPERTS, D_FF_E, D_MODEL), D_FF_E ** -0.5 * BETA),
        'ln3_g': 1.0 + nrm(ks[25], (DEPTH, D_MODEL), 0.02),
        'ln3_b': nrm(ks[26], (DEPTH, D_MODEL), 0.02),
    }

def reference(x, mem, w_in, lam_q1, lam_k1, lam_q2, lam_k2, diff_norm_g, rel_bias, w_out,
              ln1_g, ln1_b, xattn_wq, xattn_wk, xattn_wv, xattn_wo, ln2_g, ln2_b,
              ffn_w1, ffn_w3, ffn_w2, moe_router, moe_w1, moe_w3, moe_w2, ln3_g, ln3_b):
    slopes_a, slopes_c = _alibi_slopes()
    h = x
    for l in range(DEPTH):
        mix = _hybrid_mixer(h, w_in[l], lam_q1[l], lam_k1[l], lam_q2[l], lam_k2[l],
                            diff_norm_g[l], rel_bias[l], w_out[l], l, slopes_a, slopes_c)
        h = _layer_norm(ALPHA * h + mix, ln1_g[l], ln1_b[l])
        xa = _mem_cross_attention(h, mem, xattn_wq[l], xattn_wk[l], xattn_wv[l], xattn_wo[l])
        h = _layer_norm(ALPHA * h + xa, ln2_g[l], ln2_b[l])
        if l % 2 == 0:
            f = _swiglu(h, ffn_w1[l // 2], ffn_w3[l // 2], ffn_w2[l // 2])
        else:
            f = _moe(h, moe_router[l // 2], moe_w1[l // 2], moe_w3[l // 2], moe_w2[l // 2])
        h = _layer_norm(ALPHA * h + f, ln3_g[l], ln3_b[l])
    return h


_drawn_inputs = setup_inputs


def setup_inputs(seed=0):
    import zlib

    import numpy as np

    out = dict(_drawn_inputs(seed))
    spreads = {}
    factors = {'diff_norm_g': 5.533, 'rel_bias': 7.602}
    for name, (base, spread) in spreads.items():
        noise = np.random.default_rng([zlib.crc32(name.encode()), seed]).standard_normal(out[name].shape)
        drawn = base * np.exp(spread * noise) if base else spread * noise
        out[name] = __import__('jax').numpy.asarray(drawn.astype(out[name].dtype))
    for name, factor in factors.items():
        out[name] = (out[name] * factor).astype(out[name].dtype)
    return out
```

```python
import math
from contextlib import ExitStack

import numpy as np

import concourse.bass as bass
from concourse import mybir

P = 128
F32 = mybir.dt.float32
BF16 = mybir.dt.bfloat16
I32 = mybir.dt.int32
ALU = mybir.AluOpType
ACT = mybir.ActivationFunctionType
AX = mybir.AxisListType.X

CHUNK = 64
H_A, DQK_A = 4, 64
DV_A = 2 * DQK_A
H_B, DH_B = 4, 64
H_C, DH_C = 4, 64
H_IDX, D_IDX = 8, 64
H_X = 4
REL_MAX = 128
TOPK = 64
LN_EPS, RMS_EPS = 1e-5, 1e-6
NEG_INF = -1e30
DVE_LINKS = 96
GONE = -3e38
FILL = 3e38
FAR = float(2 ** 100)


class Signal:

    def __init__(self, sem, per_layer, step=1):
        self.sem, self.per_layer, self.step = sem, per_layer, step

    def wait(self, eng, layer, count):
        eng.wait_ge(self.sem, layer * (self.per_layer * self.step) + count * self.step)


class Order:

    def __init__(self, eng, sem):
        self.eng, self.sem, self.base, self.n = eng, sem, 0, 0

    def link(self, ins):
        self.n += 1
        ins.then_inc(self.sem, 1)
        self.eng.wait_ge(self.sem, self.base + self.n)


TILES = [
    ("HT0", "a"), ("HT1", "v"), ("HT2", "a"), ("HT3", "v"),
    ("KI", "v"), ("QI0", "a"), ("QI1", "v"),
    ("QA0", "a"), ("QA1", "v"), ("KA0", "a"), ("KA1", "v"),
    ("QB", "a"), ("KB", "v"), ("VB", "a"), ("QC", "v"), ("KC", "a"), ("VC", "v"),
    ("VA0", "a"), ("VA1", "v"),
    ("KX0", "a"), ("KX1", "a"), ("TA0", "v"), ("KX2", "a"), ("KX3", "a"),
    ("TA1", "v"), ("TA2", "v"), ("VX0", "a"), ("VX1", "a"),
    ("OA0", "v"), ("TB0", "a"), ("TC0", "v"), ("VX2", "a"), ("VX3", "v"),
    ("TB1", "a"), ("TB2", "v"), ("TC1", "a"), ("TC2", "v"),
    ("OA1", "v"), ("OBC0", "v"), ("OBC1", "v"),
    ("YA0", "v"), ("YB0", "a"), ("YA1", "v"), ("YB1", "a"),
    ("HX0", "a"), ("HX1", "v"), ("HX2", "a"), ("HX3", "v"),
    ("QX0", "a"), ("QX1", "v"), ("QX2", "a"), ("QX3", "v"),
    ("TX0", "a"), ("TX1", "v"), ("TX2", "a"), ("TX3", "v"),
    ("OX0", "a"), ("OX1", "v"), ("OX2", "a"), ("OX3", "v"),
    ("HF0", "a"), ("HF1", "v"), ("HF2", "a"), ("HF3", "v"),
]
TILE_AT = {name: i for i, (name, _) in enumerate(TILES)}
EVACUATIONS = {w: [n for n, x in TILES if x == w] for w in "av"}
assert len(TILES) % 2 == 0

GROUPS = ["A0", "A1", "B0", "C0", "B1", "C1", "X0", "X1"]

UNITS = [
    ("small", "KI"), ("qi", "QI1"), ("qa", "QA1"), ("ka", "KA1"), ("qkb", "KB"),
    ("vbqc", "QC"), ("kcvc", "VC"), ("va", "VA1"),
    ("wk0", "KX1"), ("wk1", "KX3"), ("wv0", "VX1"), ("wv1", "VX3"),
    ("wout0", 2), ("wout1", 4), ("wq0", "QX1"), ("wq1", "QX3"), ("wo0", 6), ("wo1", 8),
]
UNIT_AT = {name: i for i, (name, _) in enumerate(UNITS)}
SLOTS = 4
SLOT = 4096
FIRST_SLOT = 3


def through(group):
    return GROUPS.index("C0" if group == "B0" else group) + 1


def slot_of(u):
    return (u + FIRST_SLOT) % SLOTS


SLOT_USES = [sum(slot_of(u) == s for u in range(len(UNITS))) for s in range(SLOTS)]


def hybrid_encoder(nc, x, mem, w_in, lam_q1, lam_k1, lam_q2, lam_k2, diff_norm_g, rel_bias, w_out,
                   ln1_g, ln1_b, xattn_wq, xattn_wk, xattn_wv, xattn_wo, ln2_g, ln2_b,
                   ffn_w1, ffn_w3, ffn_w2, moe_router, moe_w1, moe_w3, moe_w2, ln3_g, ln3_b, out):
    _, SEQ, D = x.shape
    N_MEM = mem.shape[1]
    DEPTH = w_in.shape[0]
    N_IN = w_in.shape[2]
    D_FF = ffn_w1.shape[2]
    N_EXPERTS, D_FF_E = moe_w1.shape[1], moe_w1.shape[3]
    KT = D // P
    TB = SEQ // P
    ALPHA = (2.0 * DEPTH) ** 0.25
    assert (SEQ, N_MEM, D, TB, KT, DEPTH) == (256, 256, 1024, 2, 8, 2)
    HALF = D // 2
    NKEYS = [P, 2 * P]
    SMALL = D_IDX + H_IDX
    SCALE = DQK_A ** -0.5
    assert DQK_A == DH_B == DH_C == D_IDX == 64
    SCALE_X = float((D // H_X) ** -0.5)
    slopes = [2.0 ** (-8.0 * i / (H_A + H_C)) for i in range(1, H_A + H_C + 1)]
    lam_inits = [0.8 - 0.6 * math.exp(-0.3 * l) for l in range(DEPTH)]

    C_QA, C_KA, C_VA = 0, 512, 1024
    C_QB, C_VB, C_KC, C_QI, C_KI = 1536, 2048, 2560, 3072, 3584
    assert C_KI + SMALL == N_IN
    M_QA, M_KA, M_QB, M_KB, M_QC, M_KC, M_QI, M_KI = 0, 4, 8, 10, 12, 14, 16, 20

    FA, FB = 512, 384
    STEPS = D_FF_E // (FA + FB)
    assert STEPS * (FA + FB) == D_FF_E
    PAIRS = D_FF // (2 * P)
    assert PAIRS % 2 == 1 and PAIRS * 2 * P == D_FF
    EXTRA = (2 * SEQ - 1) // (P + 1)
    assert EXTRA == 3 and TB == 2

    with ExitStack() as ctx:
        def sb(name, shape, dt=F32):
            return ctx.enter_context(nc.sbuf_tensor(name, shape, dt))

        def sem(name):
            return ctx.enter_context(nc.semaphore(name))

        PS = ctx.enter_context(nc.psum_tensor("PS", [P, 8, 512], F32))

        BIG = sb("BIG", [P, SLOTS * SLOT + 21 * SEQ])
        QK = BIG[:, SLOTS * SLOT:].rearrange("p (m t) -> p m t", t=SEQ)
        H = sb("H", [P, TB, D])
        N = sb("N", [P, TB, D])
        HT = sb("HT", [P, KT, SEQ])
        MT = sb("MT", [P, KT, N_MEM])
        VN = sb("VN", [P, TB, D])
        WI = sb("WI", [P, TB, H_IDX])
        KX = sb("KX", [P, KT, N_MEM])
        VX = sb("VX", [P, TB, D])
        E = sb("E", [P, 6144])
        PT = sb("PT", [P, 2560])
        YT = sb("YT", [P, KT, SEQ])
        GB = sb("GB", [P, 2, D])
        HK = sb("HK", [P, 2, H_B, P])
        iden = sb("iden", [P, P])
        flip8 = sb("flip8", [P, P])
        idenb = sb("idenb", [P, P], BF16)
        slopeI = sb("slopeI", [P, H_A + H_C, P], BF16)
        dist = sb("dist", [P, 2 * P], BF16)
        maskB = sb("maskB", [P, P], BF16)
        maskI = sb("maskI", [P, 2 * P])
        isc = sb("isc", [P, 2 * P])
        work = sb("work", [P, 2 * P])
        selb = sb("selb", [P, 3 * P], BF16)
        LG = sb("LG", [P, 6, KT])
        LB = sb("LB", [P, 6, KT])
        gain = sb("gain", [P, DEPTH])
        neglam = sb("neglam", [P, DEPTH])
        st = sb("st", [P, TB, 2, 6])
        mv = sb("mv", [P, TB, 2])
        var = sb("var", [P, TB])
        rstd = sb("rstd", [P, TB])
        mhalf = sb("mhalf", [P, 8])
        top8 = sb("top8", [P, 8])
        mx = sb("mx", [P, 8, 8])
        nmx = sb("nmx", [P, 8, 8])
        sums = sb("sums", [P, 8, 8])
        rs = sb("rs", [P, 8, 8])
        mix = sb("mix", [P, 4])
        ss = sb("ss", [P, 4])
        rms = sb("rms", [P, 4])
        sq = HT[:, 0:2, :].rearrange("p t s -> p (t s)").rearrange("p (h d) -> p h d", h=4)

        EV = {
            "A0": E[:, 0:1024].rearrange("p (h k) -> p h k", k=P),
            "A1": E[:, 1024:3072].rearrange("p (h k) -> p h k", k=2 * P),
            "B0": E[:, 3072:3584].rearrange("p (h k) -> p h k", k=P),
            "C0": E[:, 3584:4096].rearrange("p (h k) -> p h k", k=P),
            "B1": E[:, 4096:5120].rearrange("p (h k) -> p h k", k=2 * P),
            "C1": E[:, 5120:6144].rearrange("p (h k) -> p h k", k=2 * P),
            "X0": E[:, 0:1024].rearrange("p (h k) -> p h k", k=2 * P),
            "X1": E[:, 1024:2048].rearrange("p (h k) -> p h k", k=2 * P),
        }
        DOT = {1: E[:, 4096:6144].rearrange("p (h k) -> p h k", k=2 * P),
               0: E[:, 3072:4096].rearrange("p (h k) -> p h k", k=P)}

        def heads(ap):
            return ap.rearrange("p (h k) -> p h k", k=P)

        PTV = {"TA0": heads(PT[:, 0:512]), "TA1": heads(PT[:, 512:1024]), "TA2": heads(PT[:, 1024:1536]),
               "TB0": heads(PT[:, 1536:2048]), "TC0": heads(PT[:, 2048:2560]),
               "TB1": heads(E[:, 0:512]), "TB2": heads(E[:, 512:1024]),
               "TC1": heads(E[:, 1024:1536]), "TC2": heads(E[:, 1536:2048])}
        PX = PT[:, 0:2048].rearrange("p (t h q) -> p t h q", t=2, h=H_X)

        def scores(group):
            bank, n, a, b, keys = {"A0": (4, 2, 0, 512, P), "A1": (0, 4, 0, 512, 2 * P),
                                   "B0": (4, 2, 0, 256, P), "C0": (4, 2, 256, 512, P),
                                   "B1": (0, 2, 0, 512, 2 * P), "C1": (2, 2, 0, 512, 2 * P),
                                   "X0": (4, 2, 0, 512, 2 * P), "X1": (0, 2, 0, 512, 2 * P)}[group]
            if n == 2:
                return PS[:, bank:bank + 2, a:b].rearrange("p b (m k) -> p b m k", k=keys)
            return PS[:, bank:bank + 4, :].rearrange("p (a b) (m k) -> p a (b m) k", a=2, k=keys)

        def score(group, i):
            S = scores(group)
            return S[:, i // S.shape[2], i % S.shape[2], :]

        def maps_of(group):
            return 8 if group[0] == "A" else 4

        def place(h, n):
            return (h % 2) * (n // 2) + h // 2

        DOTS = {1: PS[:, 0:4, :].rearrange("p b (m k) -> p (b m) k", k=2 * P),
                0: PS[:, 4:6, :].rearrange("p b (m k) -> p (b m) k", k=P)}

        def tile_bank(name):
            return PS[:, 6 + TILE_AT[name] % 2, :]

        XG = E[:, 0:1024].rearrange("p (t s) -> p t s", s=P)
        SIL = {"a": E[:, 1024:1024 + FA], "b": E[:, 1536:1536 + FB]}
        HID = {"a": E[:, 2048:2048 + FA], "b": E[:, 2560:2560 + FB]}
        HIDT = {"a": E[:, 3072:3072 + FA], "b": E[:, 3584:3584 + FB]}
        ONE = E[:, 4096:4352].rearrange("p (b s) -> p b s", b=TB)
        GATED = E[:, 4352:4608].rearrange("p (b s) -> p b s", b=TB)
        GATEDT = E[:, 4608:4864]
        YE = E[:, 4864:5888]
        FHID = E[:, 0:1024].rearrange("p (f t) -> p f t", t=SEQ)
        FSIL = E[:, 1024:2048].rearrange("p (f t) -> p f t", t=SEQ)
        iota_s = sb("iota_s", [P, 2 * P])
        before = sb("before", [P, P])
        ones = sb("ones", [P, P])
        router = sb("router", [P, KT, N_EXPERTS])
        logit = sb("logit", [P, TB, 16])
        best = sb("best", [P, TB, 8])
        take1 = sb("take1", [P, TB, 8])
        take2 = sb("take2", [P, TB, 8])
        left1 = sb("left1", [P, TB, 16])
        left2 = sb("left2", [P, TB, 16])
        chosen = sb("chosen", [P, TB, N_EXPERTS])
        gate = sb("gate", [P, TB, N_EXPERTS])
        gtmp = sb("gtmp", [P, TB, N_EXPERTS])
        gw = sb("gw", [P, TB, 4])
        rank = sb("rank", [P, TB, N_EXPERTS])
        cand = sb("cand", [1, N_EXPERTS])
        ctmp = sb("ctmp", [1, N_EXPERTS])
        full = sb("full", [1, 4])
        fulli = sb("fulli", [1, 4], I32)

        s_x = sem("s_x")
        s_mem = sem("s_mem")
        s_rows = sem("s_rows")
        s_lam = sem("s_lam")
        s_table = sem("s_table")
        s_table_out = sem("s_table_out")
        s_router = sem("s_router")
        s_out = sem("s_out")
        pool_done = sem("pool_done")
        columns_ready = sem("columns_ready")
        columns_done = sem("columns_done")
        mem_ready = sem("mem_ready")
        mem_done = sem("mem_done")
        tail_done = sem("tail_done")
        dist_done = sem("dist_done")
        lam_ready = sem("lam_ready")
        lam_exp = sem("lam_exp")
        order_pool = sem("order_pool")
        order_dve = sem("order_dve")
        order_ffn = sem("order_ffn")
        order_moe = sem("order_moe")

        gb_loaded = Signal(sem("gb_loaded"), 3, 32)
        hankel_loaded = Signal(sem("hankel_loaded"), 1, 32)
        ring_loaded = [Signal(sem(f"ring_loaded{s}"), SLOT_USES[s], 16) for s in range(SLOTS)]
        tile_ready = Signal(sem("tile_ready"), len(TILES))
        tile_taken = {"a": Signal(sem("tile_taken_act"), len(EVACUATIONS["a"])),
                      "v": Signal(sem("tile_taken_dve"), len(EVACUATIONS["v"]))}
        dots_ready = Signal(sem("dots_ready"), 2)
        relu_done = Signal(sem("relu_done"), 2)
        selected = Signal(sem("selected"), 2)
        scores_ready = Signal(sem("scores_ready"), len(GROUPS))
        max_done = Signal(sem("max_done"), len(GROUPS))
        exp_done = Signal(sem("exp_done"), len(GROUPS))
        probs_ready = Signal(sem("probs_ready"), 4)
        rows_done = Signal(sem("rows_done"), 2)
        acc_ready = Signal(sem("acc_ready"), 8)
        sum_done = Signal(sem("sum_done"), 12)
        var_ready = Signal(sem("var_ready"), 8)
        rstd_ready = Signal(sem("rstd_ready"), 8)
        norm_done = Signal(sem("norm_done"), 6)
        resid_done = Signal(sem("resid_done"), 3)

        ffn_in = [sem("ffn_in_a"), sem("ffn_in_b")]
        ffn_out_w = [sem("ffn_w2_a"), sem("ffn_w2_b")]
        ffn_up = sem("ffn_up")
        ffn_silu = sem("ffn_silu")
        ffn_hidden = sem("ffn_hidden")
        ffn_used = sem("ffn_used")

        moe_w1s = {c: sem(f"moe_w1_{c}") for c in "ab"}
        moe_w3s = {c: sem(f"moe_w3_{c}") for c in "ab"}
        moe_w2s = {c: sem(f"moe_w2_{c}") for c in "ab"}
        router_ready = sem("router_ready")
        logit_done = sem("logit_done")
        exp2_done = sem("exp2_done")
        chosen_done = sem("chosen_done")
        rank_ready = sem("rank_ready")
        table_done = sem("table_done")
        zsum_done = sem("zsum_done")
        onehot_done = sem("onehot_done")
        gather_ready = sem("gather_ready")
        gather_act = sem("gather_act")
        gather_dve = sem("gather_dve")
        gatedT_ready = sem("gatedT_ready")
        gatedT_done = sem("gatedT_done")
        g_ready = {c: sem(f"g_ready_{c}") for c in "ab"}
        u_ready = {c: sem(f"u_ready_{c}") for c in "ab"}
        silu_done = {c: sem(f"silu_done_{c}") for c in "ab"}
        hidden_done = {c: sem(f"hidden_done_{c}") for c in "ab"}
        turned_ready = {c: sem(f"turned_ready_{c}") for c in "ab"}
        turned_done = {c: sem(f"turned_done_{c}") for c in "ab"}
        w2_used = {c: sem(f"w2_used_{c}") for c in "ab"}
        y_act = sem("y_act")
        y_dve = sem("y_dve")
        scatter_ready = sem("scatter_ready")
        scatter_done = sem("scatter_done")

        scratch = nc.dram_tensor("rel_tail", [DEPTH * H_B, 2 * P], F32, kind="Internal")
        rel_rows = rel_bias.rearrange("l h r -> (l h) r")
        R = 2 * REL_MAX + 1

        block = ctx.enter_context(nc.Block())

        def extra_experts(eng, work_on):
            eng.wait_ge(table_done, 1)
            many = eng.value_load(fulli[0:1, EXTRA:EXTRA + 1], min_val=0, max_val=EXTRA)
            for j in range(EXTRA):
                e = eng.value_load(fulli[0:1, j:j + 1], min_val=0, max_val=N_EXPERTS - 1)
                with eng.If(many > j):
                    work_on(e, N_EXPERTS + j)

        def unit_done(eng, u, layer):
            last = UNITS[u][1]
            if isinstance(last, str):
                tile_ready.wait(eng, layer, TILE_AT[last] + 1)
            else:
                acc_ready.wait(eng, layer, last)

        def slot(s, a=0, b=SLOT):
            return BIG[:, s * SLOT + a:s * SLOT + b]

        def columns(w, a, n):
            return w[:, a:a + n].rearrange("(t p) n -> p t n", p=P)

        at, PLACE = 0, {}
        for c, n in (("a", FA), ("b", FB)):
            for which, size in (("w1", KT * n), ("w3", KT * n), ("w2", n // P * D)):
                PLACE[which + c] = BIG[:, at:at + size]
                at += size
        assert at <= SLOTS * SLOT + 21 * SEQ
        W1V = {c: PLACE["w1" + c].rearrange("p (t n) -> p t n", t=KT) for c in "ab"}
        W3V = {c: PLACE["w3" + c].rearrange("p (t n) -> p t n", t=KT) for c in "ab"}
        W2V = {c: PLACE["w2" + c].rearrange("p (f n) -> p f n", n=D) for c in "ab"}
        FW = [slot(s).rearrange("p (w t n) -> p w t n", w=2, t=KT) for s in (2, 1)]
        FW2 = [slot(3, a, a + SLOT // 2).rearrange("p (f n) -> p f n", n=D) for a in (0, SLOT // 2)]
        NF, FTILE = {"a": FA // P, "b": FB // P}, {"a": FA, "b": FB}

        @block.sync
        def _(sp):
            for b in range(TB):
                sp.dma_start(N[:, b, :], x[0, b * P:(b + 1) * P, :]).then_inc(s_x, 16)
            for layer in range(DEPTH):
                src = {
                    "small": (w_in, C_KI, SMALL), "qi": (w_in, C_QI, 512), "qa": (w_in, C_QA, 512),
                    "ka": (w_in, C_KA, 512), "qkb": (w_in, C_QB, 512), "vbqc": (w_in, C_VB, 512),
                    "kcvc": (w_in, C_KC, 512), "va": (w_in, C_VA, 512),
                    "wk0": (xattn_wk, 0, 512), "wk1": (xattn_wk, 512, 512),
                    "wv0": (xattn_wv, 0, 512), "wv1": (xattn_wv, 512, 512),
                    "wout0": (w_out, 0, 512), "wout1": (w_out, 512, 512),
                    "wq0": (xattn_wq, 0, 512), "wq1": (xattn_wq, 512, 512),
                    "wo0": (xattn_wo, 0, 512), "wo1": (xattn_wo, 512, 512),
                }
                for u, (name, _) in enumerate(UNITS):
                    w, a, n = src[name]
                    source = columns(w[layer], a, n)
                    s = slot_of(u)
                    if u >= SLOTS:
                        unit_done(sp, u - SLOTS, layer)
                    else:
                        sp.wait_ge(ffn_used, layer * (2 * PAIRS))
                    sp.dma_start(slot(s, 0, KT * n).rearrange("p (t n) -> p t n", t=KT),
                                 source).then_inc(ring_loaded[s].sem, 16)
                if layer == 0:
                    def load_in(place, k):
                        for which, w in ((0, ffn_w1), (1, ffn_w3)):
                            sp.dma_start(FW[place][:, which], w[0][:, k].rearrange("(t p) n -> p t n", p=P)
                                         ).then_inc(ffn_in[place], 16)

                    def load_out(place, k):
                        sp.dma_start(FW2[place], ffn_w2[0][k, :].rearrange("(f p) n -> p f n", p=P)
                                     ).then_inc(ffn_out_w[place], 16)

                    def pair(place, k, uses):
                        sp.wait_ge(ffn_used, uses)
                        load_in(place, k)
                        load_out(place, k)

                    unit_done(sp, UNIT_AT["wq0"], 0)
                    load_in(1, slice(0, 2 * P))
                    unit_done(sp, UNIT_AT["wq1"], 0)
                    load_in(0, slice(2 * P, 4 * P))
                    unit_done(sp, UNIT_AT["wo0"], 0)
                    load_out(1, slice(0, 2 * P))
                    load_out(0, slice(2 * P, 4 * P))
                    pair(1, slice(4 * P, 6 * P), 2)
                    with sp.Fori(1, PAIRS // 2) as i:
                        pair(0, bass.ds(i * (4 * P) + 2 * P, 2 * P), i * 4)
                        pair(1, bass.ds(i * (4 * P) + 4 * P, 2 * P), i * 4 + 2)
                else:
                    def expert_weights(e, n):
                        with sp.Fori(0, STEPS) as j:
                            for c, off in (("a", 0), ("b", FA)):
                                uses = n * STEPS + j
                                f = FTILE[c]
                                col = bass.ds(j * (FA + FB) + off, f)
                                s1 = moe_w1[0, e][:, col].rearrange("(t p) n -> p t n", p=P)
                                s3 = moe_w3[0, e][:, col].rearrange("(t p) n -> p t n", p=P)
                                s2 = moe_w2[0, e][col, :].rearrange("(f p) n -> p f n", p=P)
                                sp.wait_ge(g_ready[c], uses)
                                sp.dma_start(W1V[c], s1).then_inc(moe_w1s[c], 16)
                                sp.wait_ge(u_ready[c], uses)
                                sp.dma_start(W3V[c], s3).then_inc(moe_w3s[c], 16)
                                sp.wait_ge(w2_used[c], uses)
                                sp.dma_start(W2V[c], s2).then_inc(moe_w2s[c], 16)

                    for u in range(len(UNITS) - SLOTS, len(UNITS)):
                        unit_done(sp, u, DEPTH - 1)
                    with sp.Fori(0, N_EXPERTS) as e:
                        expert_weights(e, e)
                    sp.wait_ge(table_done, 1)
                    extra_experts(sp, lambda e, n: expert_weights(e, n))
            resid_done.wait(sp, DEPTH - 1, 3)
            for b in range(TB):
                sp.dma_start(out[0, b * P:(b + 1) * P, :], H[:, b, :]).then_inc(s_out, 16)
            sp.wait_ge(s_out, 16 * TB)

        @block.gpsimd
        def _(pool):
            o = Order(pool, order_pool)
            g = nc.gpsimd
            rows_g, rows_b = E[0:6 * KT, 0:P], E[0:6 * KT, P:2 * P]
            table = E[0:DEPTH * H_B, 2 * P:2 * P + R]
            tail = E[0:DEPTH * H_B, 768:768 + 2 * P]
            o.link(g.memset(rows_g, 1.0))
            o.link(g.memset(rows_b, 0.0))
            for i, (gg, bb) in enumerate([(ln3_g, ln3_b), (ln1_g, ln1_b), (ln2_g, ln2_b)]):
                r = i * 2 * KT
                first, layers = (KT, 1) if i == 0 else (0, DEPTH)
                for rows, src in ((rows_g, gg), (rows_b, bb)):
                    pool.dma_start(rows[r + first:r + 2 * KT, :],
                                   src[0:layers, :].rearrange("l (t p) -> (l t) p", p=P)).then_inc(s_rows, 16)
            pool.dma_start(E[0:DEPTH, 1024:1024 + DV_A], diff_norm_g).then_inc(s_rows, 16)
            pool.dma_start(table, rel_rows).then_inc(s_table, 16)
            for i, q in enumerate((lam_q1, lam_k1, lam_q2, lam_k2)):
                pool.dma_start(E[:, 1280 + i * 128:1280 + (i + 1) * 128],
                               q.rearrange("l d -> (l d)").partition_broadcast(P)).then_inc(s_lam, 16)
            for b in range(TB):
                pool.dma_start(E[:, 2048 + b * D:2048 + (b + 1) * D],
                               mem[0, b * P:(b + 1) * P, :]).then_inc(s_mem, 16)
            pool.dma_start(router[:], moe_router[0].rearrange("(t p) n -> p t n", p=P)).then_inc(s_router, 16)

            o.link(g.memset(iden[:], 0.0))
            o.link(g.affine_select(out=iden[:], in_=iden[:], compare_op=ALU.not_equal, fill=1.0, base=0,
                                   pattern=[[-1, P]], channel_multiplier=1))
            o.link(g.memset(flip8[:], 0.0))
            o.link(g.affine_select(out=flip8[:], in_=flip8[:], compare_op=ALU.not_equal, fill=1.0 / SCALE,
                                   base=1 - P, pattern=[[1, P]], channel_multiplier=1))
            o.link(g.memset(idenb[:], 0.0))
            o.link(g.affine_select(out=idenb[:], in_=idenb[:], compare_op=ALU.not_equal, fill=1.0, base=0,
                                   pattern=[[-1, P]], channel_multiplier=1))
            o.link(g.memset(slopeI[:], 0.0))
            for j, s in enumerate(slopes):
                o.link(g.affine_select(out=slopeI[:, j, :], in_=slopeI[:, j, :], compare_op=ALU.not_equal,
                                       fill=-s / SCALE, base=0, pattern=[[-1, P]], channel_multiplier=1))
            o.link(g.iota(isc[:], pattern=[[-1, 2 * P]], base=P, channel_multiplier=1,
                          allow_small_or_imprecise_dtypes=True))
            o.link(g.iota(iota_s[:], pattern=[[1, 2 * P]], base=0, channel_multiplier=0,
                          allow_small_or_imprecise_dtypes=True))
            o.link(g.memset(maskI[:], 0.0))
            o.link(g.memset(maskI[0:CHUNK, P + CHUNK:2 * P], NEG_INF))
            o.link(g.memset(maskB[:], 0.0))
            o.link(g.memset(maskB[0:CHUNK, CHUNK:P], -FAR))
            o.link(g.memset(mhalf[:], -0.5))
            o.link(g.memset(ones[:], 1.0))
            o.link(g.memset(before[:], 1.0))
            o.link(g.affine_select(out=before[:], in_=before[:], compare_op=ALU.is_gt, fill=0.0, base=0,
                                   pattern=[[1, P]], channel_multiplier=-1))
            g.memset(top8[:], 0.0).then_inc(pool_done, 1)

            pool.wait_ge(tail_done, 1)
            pool.dma_start(scratch.ap(), tail).then_inc(s_table_out, 16)
            pool.wait_ge(s_table_out, 16)

            lns = ((ln1_g, ln1_b), (ln2_g, ln2_b), (ln3_g, ln3_b))

            def to_rstd(n, layer, v, out_, width):
                var_ready.wait(pool, layer, n)
                g.tensor_tensor(out_, v, mhalf[:, 0:width], ALU.pow).then_inc(rstd_ready.sem, 1)

            for layer in range(DEPTH):
                exp_done.wait(pool, layer, 0)
                near = bass.AP(rel_bias.tensor, 1, [[H_B * R, DEPTH], [1, P], [R, H_B], [1, P]])
                far = bass.AP(scratch, 0, [[H_B * 2 * P, DEPTH], [1, P], [2 * P, H_B], [1, P]])
                pool.dma_start(HK[:, 0], near[layer]).then_inc(hankel_loaded.sem, 16)
                pool.dma_start(HK[:, 1], far[layer]).then_inc(hankel_loaded.sem, 16)
                for i, (gg, bb) in enumerate(lns):
                    resid_done.wait(pool, layer, i)
                    pool.dma_start(GB[:, 0, :], gg[layer].partition_broadcast(P)).then_inc(gb_loaded.sem, 16)
                    pool.dma_start(GB[:, 1, :], bb[layer].partition_broadcast(P)).then_inc(gb_loaded.sem, 16)
                    if i == 0:
                        to_rstd(1, layer, ss[:], rms[:], 4)
                        to_rstd(2, layer, ss[:], rms[:], 4)
                    for b in range(TB):
                        to_rstd(3 + 2 * i + b, layer, var[:, b:b + 1], rstd[:, b:b + 1], 1)

        @block.tensor
        def _(pe):
            mm = pe.matmul

            def turn(dst, src, n=P):
                return pe.transpose(dst, src, iden[0:n, 0:n])

            pe.wait_ge(pool_done, 1)
            pe.wait_ge(s_rows, 16 * 7)
            turn(PS[:, 0, 0:6 * KT], E[0:6 * KT, 0:P], 6 * KT)
            turn(PS[:, 0, 64:64 + 6 * KT], E[0:6 * KT, P:2 * P], 6 * KT)
            turn(PS[:, 0, 128:128 + DEPTH], E[0:DEPTH, 1024:1024 + DV_A], DEPTH).then_inc(columns_ready, 1)
            pe.wait_ge(s_mem, 16 * TB)
            for t in range(KT):
                for b in range(TB):
                    last = turn(PS[:, 1 + t // 2, (t % 2) * SEQ + b * P:(t % 2) * SEQ + (b + 1) * P],
                                E[:, 2048 + b * D + t * P:2048 + b * D + (t + 1) * P])
            last.then_inc(mem_ready, 1)
            pe.wait_ge(s_x, 16 * TB)
            pe.wait_ge(columns_done, 3)
            pe.wait_ge(mem_done, 1)
            pe.wait_ge(dist_done, 1)

            def begin(name, layer):
                i = TILE_AT[name]
                if i >= 2:
                    old, who = TILES[i - 2]
                    tile_taken[who].wait(pe, layer, EVACUATIONS[who].index(old) + 1)
                return tile_bank(name)

            def ready(ins):
                ins.then_inc(tile_ready.sem, 1)

            def unit(name, layer):
                u = UNIT_AT[name]
                s = slot_of(u)
                ring_loaded[s].wait(pe, layer, (u - (slot_of(u) - FIRST_SLOT) % SLOTS) // SLOTS + 1)
                n = SMALL if name == "small" else 512
                return slot(s, 0, KT * n).rearrange("p (t n) -> p t n", t=KT)

            def turned_rows(names, layer):
                for k, name in enumerate(names):
                    bank = begin(name, layer)
                    for t in (2 * k, 2 * k + 1):
                        for b in range(TB):
                            c = (t % 2) * SEQ + b * P
                            last = turn(bank[:, c:c + P], N[:, b, t * P:(t + 1) * P])
                    ready(last)

            def project_turned(name, w, first, count, acts, layer):
                bank = begin(name, layer)
                for m in range(count):
                    for t in range(KT):
                        last = mm(bank[:, m * SEQ:(m + 1) * SEQ], w[:, t, (first + m) * P:(first + m + 1) * P],
                                  acts[:, t, :], start=(t == 0), stop=(t == KT - 1))
                ready(last)

            def project_rows(name, w, a, n, acts, layer, blocks=range(TB)):
                bank = begin(name, layer)
                for i, b in enumerate(blocks):
                    for t in range(KT):
                        last = mm(bank[:, i * n:(i + 1) * n], acts[:, t, b * P:(b + 1) * P], w[:, t, a:a + n],
                                  start=(t == 0), stop=(t == KT - 1))
                ready(last)

            def taken(name, layer):
                who = dict(TILES)[name]
                tile_taken[who].wait(pe, layer, EVACUATIONS[who].index(name) + 1)

            def group_free(group, layer):
                if group == "A0":
                    relu_done.wait(pe, layer, 2)
                elif group == "A1":
                    relu_done.wait(pe, layer, 1)
                elif group in ("B0", "C0"):
                    exp_done.wait(pe, layer, 1)
                elif group in ("B1", "C1"):
                    exp_done.wait(pe, layer, 2)
                elif group == "X0":
                    exp_done.wait(pe, layer, 4)
                else:
                    sum_done.wait(pe, layer, 4)

            def made(ins):
                ins.then_inc(scores_ready.sem, 1)

            def scores_a(b, layer):
                group = f"A{b}"
                group_free(group, layer)
                n = NKEYS[b]
                for i in range(2 * H_A):
                    h, m = i // 2, i % 2
                    r = slice(64 * m, 64 * m + 64)
                    S = score(group, m * H_A + h)
                    mm(S, QK[r, M_QA + h, b * P:(b + 1) * P], QK[r, M_KA + h, 0:n],
                       start=True, stop=False)
                    last = mm(S, slopeI[:, 2 * h, :], dist[:, 2 * P - n:], start=False, stop=True)
                made(last)

            def scores_b(b, layer):
                group = f"B{b}"
                group_free(group, layer)
                n = NKEYS[b]
                for h in range(H_B):
                    S = score(group, place(h, H_B))
                    r = slice(64 * (h % 2), 64 * (h % 2) + 64)
                    mm(S, QK[r, M_QB + h // 2, b * P:(b + 1) * P], QK[r, M_KB + h // 2, 0:n],
                       start=True, stop=False)
                    for k in range(b + 1):
                        mm(S[:, k * P:(k + 1) * P], HK[:, b - k, h, :], flip8[:], start=False, stop=False)
                    last = mm(S[:, b * P:n], idenb[:], maskB[:], start=False, stop=True)
                made(last)

            def scores_c(b, layer):
                group = f"C{b}"
                group_free(group, layer)
                selected.wait(pe, layer, b + 1)
                n = NKEYS[b]
                chosen_keys = selb[:, 0:P] if b == 0 else selb[:, P:3 * P]
                for h in range(H_C):
                    S = score(group, place(h, H_C))
                    r = slice(64 * (h % 2), 64 * (h % 2) + 64)
                    mm(S, QK[r, M_QC + h // 2, b * P:(b + 1) * P], QK[r, M_KC + h // 2, 0:n],
                       start=True, stop=False)
                    mm(S, slopeI[:, 2 * h + 1, :], dist[:, 2 * P - n:], start=False, stop=False)
                    last = mm(S, idenb[:], chosen_keys, start=False, stop=True)
                made(last)

            def turn_probs(name, group, k, layer):
                bank = begin(name, layer)
                for h in range(4):
                    i = place(h, 4) if group[0] in "BC" else h
                    src = EV[group][:, i, k * P:(k + 1) * P]
                    last = turn(bank[:, h * P:(h + 1) * P], src)
                ready(last)

            def values_a(b, layer):
                bank = begin(f"OA{b}", layer)
                parts = ["TA0"] if b == 0 else ["TA1", "TA2"]
                for h in range(H_A):
                    for k, part in enumerate(parts):
                        last = mm(bank[:, h * P:(h + 1) * P], PTV[part][:, h, :], VN[:, k, h * P:(h + 1) * P],
                                  start=(k == 0), stop=(k == len(parts) - 1))
                ready(last)

            def values_bc(b, layer):
                bank = begin(f"OBC{b}", layer)
                for g, off in (("B", 512), ("C", 768)):
                    parts = [f"T{g}0"] if b == 0 else [f"T{g}1", f"T{g}2"]
                    for h in range(4):
                        c = off - 512 + h * 64
                        for k, part in enumerate(parts):
                            last = mm(bank[:, c:c + 64], PTV[part][:, h, :],
                                      VN[:, k, off + h * 64:off + (h + 1) * 64],
                                      start=(k == 0), stop=(k == len(parts) - 1))
                ready(last)

            def product_rows(w, half, acts):
                for b in range(TB):
                    for t in range(KT):
                        last = mm(PS[:, 2 * half + b, :], acts[:, t, b * P:(b + 1) * P], w[:, t, :],
                                  start=(t == 0), stop=(t == KT - 1))
                    last.then_inc(acc_ready.sem, 1)

            def body(layer):
                pe.wait_ge(ffn_hidden, layer * (2 * PAIRS))
                norm_done.wait(pe, layer, 0)
                turned_rows(["HT0", "HT1", "HT2", "HT3"], layer)
                taken("HT2", layer)
                taken("HT3", layer)
                w = unit("small", layer)
                bank = begin("KI", layer)
                for half in (0, 64):
                    for t in range(KT):
                        mm(bank[half:half + 64, 0:SEQ], w[:, t, 0:D_IDX], HT[:, t, :],
                           start=(t == 0), stop=(t == KT - 1))
                for b in range(TB):
                    for t in range(KT):
                        last = mm(bank[:, SEQ + b * 8:SEQ + b * 8 + 8], HT[:, t, b * P:(b + 1) * P],
                                  w[:, t, D_IDX:SMALL], start=(t == 0), stop=(t == KT - 1))
                ready(last)
                w = unit("qi", layer)
                project_turned("QI0", w, 0, 2, HT, layer)
                project_turned("QI1", w, 2, 2, HT, layer)
                taken("QI0", layer)
                taken("QI1", layer)
                sum_done.wait(pe, layer, 0)
                for b in (1, 0):
                    for h in range(H_IDX):
                        r = slice(64 * (h % 2), 64 * (h % 2) + 64)
                        last = mm(DOTS[b][:, place(h, H_IDX), :], QK[r, M_QI + h // 2, b * P:(b + 1) * P],
                                  QK[r, M_KI, 0:NKEYS[b]], start=True, stop=True)
                    last.then_inc(dots_ready.sem, 1)
                for name, a in (("qa", "QA"), ("ka", "KA")):
                    w = unit(name, layer)
                    project_turned(a + "0", w, 0, 2, HT, layer)
                    project_turned(a + "1", w, 2, 2, HT, layer)
                w = unit("qkb", layer)
                project_turned("QB", w, 0, 2, HT, layer)
                project_turned("KB", w, 2, 2, HT, layer)
                w = unit("vbqc", layer)
                project_rows("VB", w, 0, 256, HT, layer)
                project_turned("QC", w, 2, 2, HT, layer)
                w = unit("kcvc", layer)
                project_turned("KC", w, 0, 2, HT, layer)
                project_rows("VC", w, 256, 256, HT, layer)
                taken("KC", layer)
                taken("VC", layer)
                scores_a(0, layer)
                scores_a(1, layer)
                w = unit("va", layer)
                project_rows("VA0", w, 0, 512, HT, layer, [0])
                project_rows("VA1", w, 0, 512, HT, layer, [1])
                w = unit("wk0", layer)
                project_turned("KX0", w, 0, 2, MT, layer)
                project_turned("KX1", w, 2, 2, MT, layer)
                probs_ready.wait(pe, layer, 1)
                turn_probs("TA0", "A0", 0, layer)
                hankel_loaded.wait(pe, layer, 1)
                scores_b(0, layer)
                scores_c(0, layer)
                w = unit("wk1", layer)
                project_turned("KX2", w, 0, 2, MT, layer)
                project_turned("KX3", w, 2, 2, MT, layer)
                probs_ready.wait(pe, layer, 2)
                turn_probs("TA1", "A1", 0, layer)
                turn_probs("TA2", "A1", 1, layer)
                scores_b(1, layer)
                scores_c(1, layer)
                w = unit("wv0", layer)
                project_rows("VX0", w, 0, 512, MT, layer, [0])
                project_rows("VX1", w, 0, 512, MT, layer, [1])
                taken("VA1", layer)
                taken("TA0", layer)
                values_a(0, layer)
                exp_done.wait(pe, layer, 4)
                turn_probs("TB0", "B0", 0, layer)
                turn_probs("TC0", "C0", 0, layer)
                w = unit("wv1", layer)
                project_rows("VX2", w, 0, 512, MT, layer, [0])
                project_rows("VX3", w, 0, 512, MT, layer, [1])
                exp_done.wait(pe, layer, 6)
                for g in "BC":
                    turn_probs(f"T{g}1", g + "1", 0, layer)
                    turn_probs(f"T{g}2", g + "1", 1, layer)
                values_a(1, layer)
                values_bc(0, layer)
                taken("TC1", layer)
                taken("TC2", layer)
                values_bc(1, layer)
                for b in range(TB):
                    rows_done.wait(pe, layer, b + 1)
                    for name, off in ((f"YA{b}", 0), (f"YB{b}", 4)):
                        bank = begin(name, layer)
                        for m in range(4):
                            last = turn(bank[:, m * P:(m + 1) * P], N[:, b, (off + m) * P:(off + m + 1) * P])
                        ready(last)
                taken("YA1", layer)
                taken("YB1", layer)
                product_rows(unit("wout0", layer), 0, YT)
                product_rows(unit("wout1", layer), 1, YT)

                norm_done.wait(pe, layer, 2)
                turned_rows(["HX0", "HX1", "HX2", "HX3"], layer)
                taken("HX2", layer)
                taken("HX3", layer)
                w = unit("wq0", layer)
                project_turned("QX0", w, 0, 2, HT, layer)
                project_turned("QX1", w, 2, 2, HT, layer)
                w = unit("wq1", layer)
                project_turned("QX2", w, 0, 2, HT, layer)
                project_turned("QX3", w, 2, 2, HT, layer)
                taken("QX2", layer)
                taken("QX3", layer)
                for b in range(TB):
                    group_free(f"X{b}", layer)
                    for h in range(H_X):
                        for c in range(2):
                            last = mm(score(f"X{b}", h), QK[:, 2 * h + c, b * P:(b + 1) * P], KX[:, 2 * h + c, :],
                                      start=(c == 0), stop=(c == 1))
                    made(last)
                for b in range(TB):
                    probs_ready.wait(pe, layer, 3 + b)
                    for k in range(2):
                        turn_probs(f"TX{2 * b + k}", f"X{b}", k, layer)
                taken("TX2", layer)
                taken("TX3", layer)
                for h in range(H_X):
                    bank = begin(f"OX{h}", layer)
                    for c in range(2):
                        for k in range(2):
                            last = mm(bank[:, c * SEQ:(c + 1) * SEQ], VX[:, k, (2 * h + c) * P:(2 * h + c + 1) * P],
                                      PX[:, k, h, :], start=(k == 0), stop=(k == 1))
                    ready(last)
                taken("OX2", layer)
                taken("OX3", layer)
                exp_done.wait(pe, layer, 8)
                product_rows(unit("wo0", layer), 0, YT)
                product_rows(unit("wo1", layer), 1, YT)
                norm_done.wait(pe, layer, 4)
                turned_rows(["HF0", "HF1", "HF2", "HF3"], layer)
                taken("HF2", layer)
                taken("HF3", layer)
                sum_done.wait(pe, layer, 8)

            def feed_forward():
                def up(i, place, f, bank, uses):
                    if f == 0:
                        pe.wait_ge(ffn_in[place], uses * 32)
                    if i is not None:
                        pe.wait_ge(ffn_hidden, i)
                    for which in range(2):
                        for t in range(KT):
                            last = mm(PS[:, bank, which * SEQ:(which + 1) * SEQ],
                                      FW[place][:, which, t, f * P:(f + 1) * P], HT[:, t, :],
                                      start=(t == 0), stop=(t == KT - 1))
                    last.then_inc(ffn_up, 1)

                def down(i, place, f, slot_, uses, first=False, final=False):
                    if f == 0:
                        pe.wait_ge(ffn_out_w[place], uses * 16)
                    pe.wait_ge(ffn_hidden, i + 1)
                    for half in range(2):
                        for b in range(TB):
                            last = mm(PS[:, 2 * half + b, :], FHID[:, slot_, b * P:(b + 1) * P],
                                      FW2[place][:, f, half * HALF:(half + 1) * HALF],
                                      start=first, stop=final)
                    last.then_inc(ffn_used, 1)

                up(None, 1, 0, 6, 1)
                up(None, 1, 1, 7, 1)
                down(0, 1, 0, 2, 1, first=True)
                with pe.Fori(0, PAIRS // 2) as i:
                    n = i * 4 + 2
                    up(n - 2, 0, 0, 4, i + 1)
                    down(n - 1, 1, 1, 3, i + 1)
                    up(n - 1, 0, 1, 5, i + 1)
                    down(n, 0, 0, 0, i + 1)
                    up(n, 1, 0, 6, i + 2)
                    down(n + 1, 0, 1, 1, i + 1)
                    up(n + 1, 1, 1, 7, i + 2)
                    down(n + 2, 1, 0, 2, i + 2)
                down(2 * PAIRS - 1, 1, 1, 3, PAIRS // 2 + 1, final=True)

            def mixture():
                pe.wait_ge(s_router, 16)
                for b in range(TB):
                    for t in range(KT):
                        last = mm(PS[:, 4, b * 8:b * 8 + 8], HT[:, t, b * P:(b + 1) * P], router[:, t, :],
                                  start=(t == 0), stop=(t == KT - 1))
                last.then_inc(router_ready, 1)
                pe.wait_ge(chosen_done, 1)
                mm(PS[:, 5, 0:8], before[:], chosen[:, 0, :], start=True, stop=True)
                mm(PS[:, 5, 8:16], before[:], chosen[:, 1, :], start=True, stop=False)
                mm(PS[:, 5, 8:16], ones[:], chosen[:, 0, :], start=False, stop=True)
                mm(PS[:, 5, 16:24], ones[:], chosen[:, 0, :], start=True, stop=False)
                mm(PS[:, 5, 16:24], ones[:], chosen[:, 1, :], start=False, stop=True).then_inc(rank_ready, 1)
                resid_done.wait(pe, DEPTH - 1, 2)

                def item(n):
                    pe.wait_ge(onehot_done, n * 2 + 1)
                    pe.wait_ge(turned_done["a"], n * STEPS)
                    pe.wait_ge(turned_done["b"], n * STEPS)
                    for t in range(KT):
                        for b in range(TB):
                            last = mm(PS[:, 6 + t // 4, (t % 4) * P:(t % 4 + 1) * P],
                                      H[:, b, t * P:(t + 1) * P], ONE[:, b, :], start=(b == 0), stop=(b == 1))
                        if t % 4 == 3:
                            last.then_inc(gather_ready, 1)
                    pe.wait_ge(onehot_done, n * 2 + 2)
                    pe.wait_ge(y_act, n)
                    pe.wait_ge(y_dve, n)
                    for b in range(TB):
                        last = turn(PS[:, 0, b * P:(b + 1) * P], GATED[:, b, :])
                    last.then_inc(gatedT_ready, 1)
                    pe.wait_ge(gather_act, n + 1)
                    pe.wait_ge(gather_dve, n + 1)
                    pe.wait_ge(scatter_done, n * 4)

                    def part(c, which, k):
                        pe.wait_ge((moe_w1s if which == 0 else moe_w3s)[c], (k + 1) * 16)
                        W = (W1V if which == 0 else W3V)[c]
                        bank = (2 if c == "a" else 4) + which
                        if which == 0:
                            pe.wait_ge(silu_done[c], k)
                        else:
                            pe.wait_ge(hidden_done[c], k)
                        for t in range(KT):
                            last = mm(PS[:, bank, 0:FTILE[c]], XG[:, t, :], W[:, t, :],
                                      start=(t == 0), stop=(t == KT - 1))
                        last.then_inc((g_ready if which == 0 else u_ready)[c], 1)

                    def turn_hidden(c, k):
                        pe.wait_ge(hidden_done[c], k + 1)
                        pe.wait_ge(turned_done[c], k)
                        for f in range(NF[c]):
                            last = turn(PS[:, 6 if c == "a" else 7, f * P:(f + 1) * P], HID[c][:, f * P:(f + 1) * P])
                        last.then_inc(turned_ready[c], 1)

                    def down(c, k, first=False, final=False):
                        pe.wait_ge(moe_w2s[c], (k + 1) * 16)
                        pe.wait_ge(turned_done[c], k + 1)
                        for f in range(NF[c]):
                            for half in range(2):
                                last = mm(PS[:, half, :], HIDT[c][:, f * P:(f + 1) * P],
                                          W2V[c][:, f, half * HALF:(half + 1) * HALF],
                                          start=first and f == 0, stop=final and f == NF[c] - 1)
                        last.then_inc(w2_used[c], 1)

                    k0 = n * STEPS
                    part("a", 0, k0)
                    part("a", 1, k0)
                    part("b", 0, k0)
                    turn_hidden("a", k0)
                    part("b", 1, k0)
                    pe.wait_ge(gatedT_done, n + 1)
                    down("a", k0, first=True)
                    with pe.Fori(1, STEPS) as j:
                        k = k0 + j
                        part("a", 0, k)
                        turn_hidden("b", k - 1)
                        part("a", 1, k)
                        down("b", k - 1)
                        part("b", 0, k)
                        turn_hidden("a", k)
                        part("b", 1, k)
                        down("a", k)
                    k = k0 + (STEPS - 1)
                    turn_hidden("b", k)
                    down("b", k, final=True)
                    pe.wait_ge(y_act, n + 1)
                    pe.wait_ge(y_dve, n + 1)
                    for half in range(2):
                        for b in range(TB):
                            mm(PS[:, 2 + 2 * half + b, :], GATEDT[:, b * P:(b + 1) * P],
                               YE[:, half * HALF:(half + 1) * HALF], start=True, stop=True
                               ).then_inc(scatter_ready, 1)

                with pe.Fori(0, N_EXPERTS) as e:
                    item(e)
                extra_experts(pe, lambda e, n: item(n))

            for layer in range(DEPTH):
                body(layer)
                if layer == 0:
                    feed_forward()
                else:
                    mixture()

        def destination(name):
            bank = tile_bank(name)
            kind, i = name[:2], int(name[-1]) if name[-1].isdigit() else 0
            two = bank.rearrange("p (m t) -> p m t", t=SEQ)
            turned = {"QI": M_QI + 2 * i, "QA": M_QA + 2 * i, "KA": M_KA + 2 * i, "QB": M_QB, "KB": M_KB,
                      "QC": M_QC, "KC": M_KC}
            if kind in turned:
                return QK[:, turned[kind]:turned[kind] + 2, :], two
            if name == "VB":
                return VN[:, :, 512:768], two
            if name == "VC":
                return VN[:, :, 768:1024], two
            if kind == "VA":
                return VN[:, i, 0:512], bank
            if kind == "KX":
                return KX[:, 2 * i:2 * i + 2, :], two
            if kind == "QX":
                return QK[:, 2 * i:2 * i + 2, :], two
            if kind == "OX":
                return YT[:, 2 * i:2 * i + 2, :], two
            if kind == "VX":
                return VX[:, i % 2, i // 2 * HALF:(i // 2 + 1) * HALF], bank
            if kind == "TX":
                return PX[:, i % 2, :, i // 2 * P:(i // 2 + 1) * P], heads(bank)
            if kind == "YB":
                return YT[:, 4:8, i * P:(i + 1) * P], heads(bank)
            return PTV[name], heads(bank)

        def column(tile, row, layer, t):
            return tile[:].rearrange("p r t -> p (r t)")[:, bass.ds(layer * KT + (row * KT + t), 1)]

        NORM_ROW = {"HT": 0, "HX": 2, "HF": 4}

        @block.scalar
        def _(act):
            a = nc.scalar
            act.wait_ge(mem_ready, 1)
            for i in range(KT // 2):
                last = a.activation(MT[:, 2 * i:2 * i + 2, :], PS[:, 1 + i, :].rearrange("p (m t) -> p m t", t=SEQ),
                                    ACT.Copy)
            last.then_inc(mem_done, 1)
            act.wait_ge(lam_ready, 1)
            a.activation(work[:, 8:8 + 2 * DEPTH], work[:, 0:2 * DEPTH], ACT.Exp).then_inc(lam_exp, 1)
            act.wait_ge(columns_done, 3)
            act.wait_ge(s_table_out, 16)

            def take(name, layer):
                tile_ready.wait(act, layer, TILE_AT[name] + 1)
                if name[:2] in NORM_ROW:
                    row, k = NORM_ROW[name[:2]], int(name[2])
                    for t in (2 * k, 2 * k + 1):
                        last = a.activation(HT[:, t, :], tile_bank(name)[:, (t % 2) * SEQ:(t % 2 + 1) * SEQ],
                                            ACT.Identity, bias=column(LB, row, layer, t),
                                            scale=column(LG, row, layer, t))
                else:
                    dst, src = destination(name)
                    last = a.activation(dst, src, ACT.Copy)
                last.then_inc(tile_taken["a"].sem, 1)

            def exps(group, layer):
                i = GROUPS.index(group)
                max_done.wait(act, layer, through(group))
                for m in range(maps_of(group)):
                    last = a.activation(EV[group][:, m, :], score(group, m), ACT.Exp, bias=nmx[:, i, m:m + 1],
                                        scale=SCALE_X if group[0] == "X" else SCALE,
                                        accum_out=sums[:, i, m:m + 1])
                last.then_inc(exp_done.sem, 1)

            def body(layer):
                def tiles(*names):
                    for name in names:
                        take(name, layer)

                tiles("HT0", "HT2", "QI0")
                for i, b in enumerate((1, 0)):
                    dots_ready.wait(act, layer, i + 1)
                    a.activation(DOT[b], DOTS[b], ACT.Relu).then_inc(relu_done.sem, 1)
                tiles("QA0", "KA0", "QB", "VB", "KC")
                exps("A0", layer)
                exps("A1", layer)
                tiles("VA0", "KX0", "KX1")
                exps("B0", layer)
                exps("C0", layer)
                tiles("KX2", "KX3")
                exps("B1", layer)
                exps("C1", layer)
                tiles("VX0", "VX1", "TB0", "VX2", "TB1", "TC1", "YB0", "YB1")
                tiles("HX0", "HX2", "QX0", "QX2")
                exps("X0", layer)
                exps("X1", layer)
                tiles("TX0", "TX2", "OX0", "OX2", "HF0", "HF2")

            def silu_f(n, bank, s):
                act.wait_ge(ffn_up, n + 1)
                a.activation(FSIL[:, s, :], PS[:, bank, 0:SEQ], ACT.Silu).then_inc(ffn_silu, 1)

            def item(n):
                act.wait_ge(gather_ready, n * 2 + 1)
                a.activation(XG[:, 0:4, :], heads(PS[:, 6, :]), ACT.Copy).then_inc(gather_act, 1)

                def silu(c, k):
                    act.wait_ge(g_ready[c], k + 1)
                    act.wait_ge(hidden_done[c], k)
                    a.activation(SIL[c], PS[:, 2 if c == "a" else 4, 0:FTILE[c]], ACT.Silu
                                 ).then_inc(silu_done[c], 1)

                def take_turned(k):
                    act.wait_ge(turned_ready["a"], k + 1)
                    a.activation(HIDT["a"], PS[:, 6, 0:FA], ACT.Copy).then_inc(turned_done["a"], 1)

                k0 = n * STEPS
                silu("a", k0)
                silu("b", k0)
                take_turned(k0)
                with act.Fori(1, STEPS) as j:
                    k = k0 + j
                    silu("a", k)
                    silu("b", k)
                    take_turned(k)
                act.wait_ge(w2_used["b"], k0 + STEPS)
                a.activation(YE[:, 0:HALF], PS[:, 0, :], ACT.Copy).then_inc(y_act, 1)

            for layer in range(DEPTH):
                body(layer)
                if layer == 0:
                    silu_f(0, 6, 2)
                    silu_f(1, 7, 3)
                    with act.Fori(0, PAIRS // 2) as i:
                        for f, bank in enumerate((4, 5, 6, 7)):
                            n = i * 4 + (2 + f)
                            act.wait_ge(ffn_hidden, i * 4 + f)
                            silu_f(n, bank, f)
                else:
                    act.wait_ge(logit_done, 1)
                    a.activation(gw[:, :, 1:2], gw[:, :, 0:1], ACT.Exp).then_inc(exp2_done, 1)
                    with act.Fori(0, N_EXPERTS) as e:
                        item(e)
                    extra_experts(act, lambda e, n: item(n))

        @block.vector
        def _(dve):
            v = nc.vector
            o = Order(dve, order_dve)
            dve.wait_ge(s_table, 16)
            dve.wait_ge(pool_done, 1)
            t8 = slice(0, DEPTH * H_B)
            tail = E[t8, 768:768 + 2 * P]
            v.tensor_copy(tail[:, 0:P], E[t8, 2 * P + REL_MAX + 1:2 * P + R])
            v.tensor_scalar(tail[:, P:2 * P], maskI[t8, 0:P], E[t8, 2 * P + R - 1:2 * P + R], None,
                            ALU.add).then_inc(tail_done, 1)
            o.link(v.scalar_tensor_tensor(out=dist[:], in0=isc[:], scalar=-1.0, in1=isc[:], op0=ALU.mult,
                                          op1=ALU.max))
            v.memset(dist[0:CHUNK, P + CHUNK:2 * P], FAR).then_inc(dist_done, 1)
            dve.wait_ge(columns_ready, 1)
            v.tensor_copy(LG[:].rearrange("p r t -> p (r t)"), PS[:, 0, 0:6 * KT]).then_inc(columns_done, 1)
            v.tensor_copy(LB[:].rearrange("p r t -> p (r t)"), PS[:, 0, 64:64 + 6 * KT]).then_inc(columns_done, 1)
            for l in range(DEPTH):
                last = v.tensor_scalar(gain[:, l:l + 1], PS[:, 0, 128 + l:129 + l], 1.0 - lam_inits[l], None, ALU.mult)
            last.then_inc(columns_done, 1)
            dve.wait_ge(s_lam, 16 * 4)
            lq = E[:, 1280:1792].rearrange("p (i l d) -> p i l d", l=DEPTH, d=DQK_A)
            lsum = work[:, 0:2 * DEPTH].rearrange("p (i l) -> p i l", l=DEPTH)
            lexp = work[:, 8:8 + 2 * DEPTH].rearrange("p (i l) -> p i l", l=DEPTH)
            for i in range(2):
                o.link(v.tensor_tensor(sq[:, i, :].rearrange("p (l d) -> p l d", l=DEPTH), lq[:, 2 * i],
                                       lq[:, 2 * i + 1], ALU.mult))
                last = v.tensor_reduce(lsum[:, i, :], sq[:, i, :].rearrange("p (l d) -> p l d", l=DEPTH),
                                       AX, ALU.add)
            last.then_inc(lam_ready, 1)
            dve.wait_ge(lam_exp, 1)
            for l in range(DEPTH):
                o.link(v.tensor_tensor(neglam[:, l:l + 1], lexp[:, 1, l:l + 1], lexp[:, 0, l:l + 1], ALU.subtract))
                o.link(v.tensor_scalar(neglam[:, l:l + 1], neglam[:, l:l + 1], -lam_inits[l], None, ALU.add))
            dve.wait_ge(s_x, 16 * TB)
            for b in range(TB):
                o.link(v.tensor_copy(H[:, b, :], N[:, b, :]))
            setup_links = o.n

            def take(name, layer):
                tile_ready.wait(dve, layer, TILE_AT[name] + 1)
                bank = tile_bank(name)
                kind = name[:2]
                if kind in NORM_ROW:
                    row, k = NORM_ROW[kind], int(name[2])
                    for t in (2 * k, 2 * k + 1):
                        last = v.tensor_scalar(HT[:, t, :], bank[:, (t % 2) * SEQ:(t % 2 + 1) * SEQ],
                                               column(LG, row, layer, t), column(LB, row, layer, t),
                                               ALU.mult, ALU.add)
                elif name == "KI":
                    v.tensor_copy(QK[:, M_KI, :], bank[:, 0:SEQ])
                    last = v.tensor_scalar(WI[:].rearrange("p b h -> p (b h)"), bank[:, SEQ:SEQ + TB * H_IDX],
                                           float(H_IDX ** -0.5 * D_IDX ** -0.5), None, ALU.mult)
                elif kind == "YA":
                    b = int(name[2])
                    last = v.tensor_scalar(YT[:, 0:4, b * P:(b + 1) * P], heads(bank), gain[:, bass.ds(layer, 1)],
                                           None, ALU.mult)
                else:
                    dst, src = destination(name)
                    last = v.tensor_copy(dst, src)
                last.then_inc(tile_taken["v"].sem, 1)

            def select(b, layer):
                n = NKEYS[b]
                relu_done.wait(dve, layer, 2 - b)
                selected.wait(dve, layer, b)
                score, rest = isc[:, 0:n], work[:, 0:n]
                for h in range(H_IDX):
                    o.link(v.scalar_tensor_tensor(out=score, in0=DOT[b][:, place(h, H_IDX), :], scalar=WI[:, b, h:h + 1],
                                                  in1=maskI[:, 2 * P - n:] if h == 0 else score,
                                                  op0=ALU.mult, op1=ALU.add))
                for i in range(TOPK // 8):
                    o.link(v.max(top8[:], score if i == 0 else rest))
                    o.link(v.match_replace(rest, top8[:], score if i == 0 else rest, GONE))
                o.link(v.tensor_scalar(rest, rest, 0.5 * GONE, -FAR, ALU.is_gt, ALU.mult))
                o.link(v.tensor_scalar(score, score, 0.5 * NEG_INF, -FAR, ALU.is_le, ALU.mult))
                keys = selb[:, 0:P] if b == 0 else selb[:, P:3 * P]
                v.tensor_tensor(keys, rest, score, ALU.min).then_inc(selected.sem, 1)

            def maxima(group, layer):
                i = GROUPS.index(group)
                scores_ready.wait(dve, layer, through(group))
                n = maps_of(group)
                o.link(v.tensor_reduce(mx[:, i, 0:n].rearrange("p (a m) -> p a m", a=2), scores(group), AX,
                                       ALU.max))
                v.tensor_scalar(nmx[:, i, 0:n], mx[:, i, 0:n], -(SCALE_X if group[0] == "X" else SCALE), None,
                                ALU.mult).then_inc(max_done.sem, 1)

            def inverse_sums(group, layer):
                i = GROUPS.index(group)
                exp_done.wait(dve, layer, i + 1)
                n = maps_of(group)
                o.link(v.reciprocal(rs[:, i, 0:n], sums[:, i, 0:n]))
                return i

            def mix_maps(b, layer):
                group = f"A{b}"
                i = inverse_sums(group, layer)
                pair = lambda t, m: t[:, i, m * H_A:(m + 1) * H_A]
                o.link(v.scalar_tensor_tensor(out=mix[:], in0=pair(sums, 0), scalar=neglam[:, bass.ds(layer, 1)],
                                              in1=pair(rs, 1), op0=ALU.mult, op1=ALU.mult))
                for h in range(H_A):
                    e0, e1 = EV[group][:, h, :], EV[group][:, H_A + h, :]
                    last = v.scalar_tensor_tensor(out=e0, in0=e1, scalar=mix[:, h:h + 1], in1=e0,
                                                  op0=ALU.mult, op1=ALU.add)
                last.then_inc(probs_ready.sem, 1)

            def rows_a(b, layer):
                name = f"OA{b}"
                tile_ready.wait(dve, layer, TILE_AT[name] + 1)
                i = GROUPS.index(f"A{b}")
                rows = N[:, b, 0:512].rearrange("p (h d) -> p h d", h=H_A)
                r0 = rs[:, i, 0:H_A].rearrange("p (h u) -> p h u", u=1).to_broadcast([P, H_A, DV_A])
                v.tensor_tensor(rows, heads(tile_bank(name)), r0, ALU.mult).then_inc(tile_taken["v"].sem, 1)
                taken = EVACUATIONS["v"].index(name) + 1
                tile_taken["v"].wait(dve, layer, taken)
                o.link(v.tensor_tensor(sq, rows, rows, ALU.mult))
                o.link(v.tensor_reduce(ss[:], sq, AX, ALU.add))
                v.tensor_scalar(ss[:], ss[:], 1.0 / DV_A, RMS_EPS, ALU.mult, ALU.add).then_inc(var_ready.sem, 1)
                rstd_ready.wait(dve, layer, 1 + b)
                o.link(v.tensor_tensor(rows, rows, rms[:].rearrange("p (h u) -> p h u", u=1)
                                       .to_broadcast([P, H_A, DV_A]), ALU.mult))

            def rows_bc(b, layer):
                name = f"OBC{b}"
                for g in "BC":
                    inverse_sums(f"{g}{b}", layer)
                tile_ready.wait(dve, layer, TILE_AT[name] + 1)
                for g, c in (("B", 0), ("C", 256)):
                    i = GROUPS.index(f"{g}{b}")
                    r = rs[:, i, 0:4].rearrange("p (a c u) -> p c a u", a=2, u=1).to_broadcast([P, 2, 2, 64])
                    cut = lambda t: t.rearrange("p (c a d) -> p c a d", c=2, a=2)
                    last = v.tensor_tensor(cut(N[:, b, 512 + c:768 + c]), cut(tile_bank(name)[:, c:c + 256]), r,
                                           ALU.mult)
                    if g == "B":
                        o.link(last)
                last.then_inc(tile_taken["v"].sem, 1)
                tile_taken["v"].wait(dve, layer, EVACUATIONS["v"].index(name) + 1)

            def statistics(o, z, b, layer):
                for half in range(2):
                    o.link(v.bn_stats(st[:, b, half, :], z[:, b, half * HALF:(half + 1) * HALF]))
                o.link(v.bn_aggr(mv[:, b, :], st[:, b].rearrange("p c s -> p (c s)")))
                v.tensor_scalar(var[:, b:b + 1], mv[:, b, 1:2], LN_EPS, None, ALU.add).then_inc(var_ready.sem, 1)

            def normalise(z, b, which, layer):
                rstd_ready.wait(dve, layer, 3 + 2 * which + b)
                v.tensor_scalar(N[:, b, :], z[:, b, :], mv[:, b, 0:1], rstd[:, b:b + 1], ALU.subtract, ALU.mult
                                ).then_inc(norm_done.sem, 1)

            def residual_sum(half, b, first, layer):
                z = H[:, b, half * HALF:(half + 1) * HALF]
                v.scalar_tensor_tensor(out=z, in0=z, scalar=ALPHA, in1=PS[:, 2 * half + b, :], op0=ALU.mult,
                                       op1=ALU.add).then_inc(sum_done.sem, 1)

            def residual_rows(o, which, layer):
                norm_done.wait(dve, layer, 2 * which + 2)
                gb_loaded.wait(dve, layer, which + 1)
                for b in range(TB):
                    o.link(v.tensor_tensor(H[:, b, :], N[:, b, :], GB[:, 0, :], ALU.mult))
                o.link(v.tensor_tensor(H[:, 0, :], H[:, 0, :], GB[:, 1, :], ALU.add))
                v.tensor_tensor(H[:, 1, :], H[:, 1, :], GB[:, 1, :], ALU.add).then_inc(resid_done.sem, 1)
                resid_done.wait(dve, layer, which + 1)

            def sublayer_norm(which, layer):
                for half in range(2):
                    for b in range(TB):
                        acc_ready.wait(dve, layer, 4 * which + 2 * half + b + 1)
                        residual_sum(half, b, 4 * which, layer)
                sum_done.wait(dve, layer, 4 * which + 4)
                for b in range(TB):
                    statistics(o, H, b, layer)
                for b in range(TB):
                    normalise(H, b, which, layer)

            def body(layer):
                def tiles(*names):
                    for name in names:
                        take(name, layer)

                tiles("HT1", "HT3", "KI", "QI1")
                tile_taken["v"].wait(dve, layer, 4)
                select(0, layer)
                tiles("QA1")
                select(1, layer)
                tiles("KA1", "KB", "QC", "VC")
                maxima("A0", layer)
                maxima("A1", layer)
                mix_maps(0, layer)
                tiles("VA1")
                mix_maps(1, layer)
                tiles("TA0")
                maxima("B0", layer)
                maxima("C0", layer)
                tiles("TA1", "TA2")
                maxima("B1", layer)
                maxima("C1", layer)
                rows_a(0, layer)
                tiles("TC0", "VX3", "TB2", "TC2")
                rows_a(1, layer)
                rows_bc(0, layer)
                dve.sem_inc(rows_done.sem, 1)
                rows_bc(1, layer)
                dve.sem_inc(rows_done.sem, 1)
                tiles("YA0", "YA1")
                sublayer_norm(0, layer)
                tiles("HX1", "HX3")
                residual_rows(o, 0, layer)
                tiles("QX1", "QX3")
                maxima("X0", layer)
                maxima("X1", layer)
                for b in range(TB):
                    group = f"X{b}"
                    i = inverse_sums(group, layer)
                    r = rs[:, i, 0:4].rearrange("p (h u) -> p h u", u=1).to_broadcast([P, 4, N_MEM])
                    v.tensor_tensor(EV[group], EV[group], r, ALU.mult).then_inc(probs_ready.sem, 1)
                tiles("TX1", "TX3", "OX1", "OX3")
                sublayer_norm(1, layer)
                tiles("HF1", "HF3")
                residual_rows(o, 1, layer)

            def feed_forward(layer):
                o = Order(dve, order_ffn)

                def hidden(n, bank, s):
                    dve.wait_ge(ffn_silu, n + 1)
                    v.tensor_tensor(FHID[:, s, :], FSIL[:, s, :], PS[:, bank, SEQ:2 * SEQ], ALU.mult
                                    ).then_inc(ffn_hidden, 1)

                hidden(0, 6, 2)
                hidden(1, 7, 3)
                with dve.Fori(0, PAIRS // 2) as i:
                    for f, bank in enumerate((4, 5, 6, 7)):
                        dve.wait_ge(ffn_used, i * 4 + f)
                        hidden(i * 4 + (2 + f), bank, f)
                dve.wait_ge(ffn_used, 2 * PAIRS)
                for half in range(2):
                    for b in range(TB):
                        residual_sum(half, b, 8, layer)
                sum_done.wait(dve, layer, 12)
                for b in range(TB):
                    statistics(o, H, b, layer)
                for b in range(TB):
                    normalise(H, b, 2, layer)
                residual_rows(o, 2, layer)

            def mixture(layer):
                o = Order(dve, order_moe)
                EIGHT = slice(0, N_EXPERTS)
                o.link(v.memset(logit[:], FILL))
                o.link(v.memset(take1[:], FILL))
                o.link(v.memset(take2[:], FILL))
                dve.wait_ge(router_ready, 1)
                o.link(v.tensor_copy(logit[:, :, EIGHT], PS[:, 4, 0:16].rearrange("p (b e) -> p b e", b=TB)))
                for b in range(TB):
                    o.link(v.max(best[:, b, :], logit[:, b, EIGHT]))
                v.tensor_tensor(gw[:, :, 0:1], best[:, :, 1:2], best[:, :, 0:1], ALU.subtract
                                ).then_inc(logit_done, 1)
                o.link(v.tensor_copy(take1[:, :, 0:1], best[:, :, 0:1]))
                o.link(v.tensor_copy(take2[:, :, 0:2], best[:, :, 0:2]))
                for b in range(TB):
                    o.link(v.match_replace(left1[:, b, :], take1[:, b, :], logit[:, b, :], GONE))
                    o.link(v.match_replace(left2[:, b, :], take2[:, b, :], logit[:, b, :], GONE))
                o.link(v.tensor_scalar(gtmp[:], left1[:, :, EIGHT], 0.5 * GONE, None, ALU.is_le))
                v.tensor_scalar(chosen[:], left2[:, :, EIGHT], 0.5 * GONE, None, ALU.is_le).then_inc(chosen_done, 1)
                dve.wait_ge(exp2_done, 1)
                dve.wait_ge(chosen_done, 1)
                o.link(v.tensor_scalar(gw[:, :, 2:3], gw[:, :, 1:2], 1.0, None, ALU.add))
                o.link(v.reciprocal(gw[:, :, 2:3], gw[:, :, 2:3]))
                o.link(v.tensor_tensor(gw[:, :, 3:4], gw[:, :, 1:2], gw[:, :, 2:3], ALU.mult))
                for b in range(TB):
                    o.link(v.tensor_tensor(gate[:, b, :], chosen[:, b, :], gtmp[:, b, :], ALU.subtract))
                    o.link(v.tensor_scalar(gtmp[:, b, :], gtmp[:, b, :], gw[:, b, 2:3], None, ALU.mult))
                    o.link(v.scalar_tensor_tensor(out=gate[:, b, :], in0=gate[:, b, :], scalar=gw[:, b, 3:4],
                                                  in1=gtmp[:, b, :], op0=ALU.mult, op1=ALU.add))
                dve.wait_ge(rank_ready, 1)
                o.link(v.tensor_copy(rank[:].rearrange("p b e -> p (b e)"), PS[:, 5, 0:16]))
                o.link(v.tensor_scalar(ctmp[:], PS[0:1, 5, 16:24], float(P), None, ALU.is_gt))
                o.link(v.tensor_reduce(full[:, 3:4], ctmp[:], AX, ALU.add))
                o.link(v.tensor_scalar(ctmp[:], ctmp[:], -64.0, 64.0, ALU.mult, ALU.add))
                o.link(v.tensor_tensor(cand[:], ctmp[:], iota_s[0:1, EIGHT], ALU.add))
                for j in range(EXTRA):
                    o.link(v.tensor_reduce(full[:, j:j + 1], cand[:], AX, ALU.min))
                    o.link(v.tensor_scalar(ctmp[:], cand[:], full[:, j:j + 1], 64.0, ALU.is_equal, ALU.mult))
                    o.link(v.tensor_tensor(cand[:], cand[:], ctmp[:], ALU.add))
                o.link(v.tensor_scalar(full[:, 0:EXTRA], full[:, 0:EXTRA], float(N_EXPERTS - 1), None, ALU.min))
                v.tensor_copy(fulli[:], full[:]).then_inc(table_done, 1)
                norm_done.wait(dve, DEPTH - 1, 4)
                for b in range(TB):
                    o.link(v.tensor_scalar(N[:, b, :], H[:, b, :], ALPHA, None, ALU.mult))

                def item(e, n, base):
                    dve.wait_ge(gather_ready, n * 2)
                    dve.wait_ge(gatedT_ready, n)
                    for table, rows, s in ((chosen, ONE, 0), (gate, GATED, 1)):
                        for b in range(TB):
                            pick = lambda t: t[:].rearrange("p b e -> p (b e)")[:, bass.ds(e + b * N_EXPERTS, 1)]
                            last = v.tensor_scalar(rows[:, b, :], iota_s[:, base:base + P], pick(rank), pick(table),
                                                   ALU.is_equal, ALU.mult)
                        last.then_inc(onehot_done, 1)
                    dve.wait_ge(gather_ready, n * 2 + 2)
                    v.tensor_copy(XG[:, 4:8, :], heads(PS[:, 7, :])).then_inc(gather_dve, 1)
                    dve.wait_ge(gatedT_ready, n + 1)
                    v.tensor_copy(GATEDT, PS[:, 0, 0:TB * P]).then_inc(gatedT_done, 1)

                    def hidden(c, k):
                        dve.wait_ge(silu_done[c], k + 1)
                        dve.wait_ge(u_ready[c], k + 1)
                        dve.wait_ge(turned_ready[c], k)
                        v.tensor_tensor(HID[c], SIL[c], PS[:, 3 if c == "a" else 5, 0:FTILE[c]], ALU.mult
                                        ).then_inc(hidden_done[c], 1)

                    def take_turned(k):
                        dve.wait_ge(turned_ready["b"], k + 1)
                        v.tensor_copy(HIDT["b"], PS[:, 7, 0:FB]).then_inc(turned_done["b"], 1)

                    k0 = n * STEPS
                    hidden("a", k0)
                    hidden("b", k0)
                    with dve.Fori(1, STEPS) as j:
                        k = k0 + j
                        take_turned(k - 1)
                        hidden("a", k)
                        hidden("b", k)
                    take_turned(k0 + (STEPS - 1))
                    dve.wait_ge(w2_used["b"], k0 + STEPS)
                    v.tensor_copy(YE[:, HALF:D], PS[:, 1, :]).then_inc(y_dve, 1)
                    for half in range(2):
                        for b in range(TB):
                            z = N[:, b, half * HALF:(half + 1) * HALF]
                            dve.wait_ge(scatter_ready, n * 4 + (2 * half + b + 1))
                            v.tensor_tensor(z, z, PS[:, 2 + 2 * half + b, :], ALU.add).then_inc(scatter_done, 1)
                    dve.wait_ge(scatter_done, n * 4 + 4)

                with dve.Fori(0, N_EXPERTS) as e:
                    item(e, e, 0)
                extra_experts(dve, lambda e, n: item(e, n, P))
                for b in range(TB):
                    statistics(o, N, b, layer)
                for b in range(TB):
                    normalise(N, b, 2, layer)
                residual_rows(o, 2, layer)

            per_layer = DVE_LINKS
            for layer in range(DEPTH):
                o.base, o.n = layer * per_layer + setup_links, 0
                body(layer)
                assert o.n == per_layer, o.n
                if layer == 0:
                    feed_forward(layer)
                else:
                    mixture(layer)


_INS = ['x', 'mem', 'w_in', 'lam_q1', 'lam_k1', 'lam_q2', 'lam_k2', 'diff_norm_g', 'rel_bias', 'w_out',
        'ln1_g', 'ln1_b', 'xattn_wq', 'xattn_wk', 'xattn_wv', 'xattn_wo', 'ln2_g', 'ln2_b',
        'ffn_w1', 'ffn_w3', 'ffn_w2', 'moe_router', 'moe_w1', 'moe_w3', 'moe_w2', 'ln3_g', 'ln3_b']


def kernel(**inputs):
    import numpy as _np
    import concourse.bacc as _bacc
    from concourse import mybir as _mybir
    from concourse.bass_utils import run_bass_kernel_spmd as _run

    nc = _bacc.Bacc("TRN2", target_bir_lowering=False, num_devices=1)
    arrays, args = {}, []
    for name in _INS:
        a = _np.ascontiguousarray(inputs[name])
        arrays[f"in_{name}_dram"] = a
        args.append(nc.dram_tensor(f"in_{name}_dram", a.shape, _mybir.dt.from_np(a.dtype), kind="ExternalInput").ap())
    out = nc.dram_tensor("out_0_dram", inputs["x"].shape, _mybir.dt.float32, kind="ExternalOutput").ap()
    hybrid_encoder(nc, *args, out)
    r = _run(nc, [arrays], core_ids=[0])
    return r.results[0]["out_0_dram"]
```

```python
import math
from contextlib import ExitStack

import numpy as np

import concourse.bass as bass
from concourse import mybir

P = 128
F32 = mybir.dt.float32
F32R = mybir.dt.float32r
BF16 = mybir.dt.bfloat16
I32 = mybir.dt.int32
ALU = mybir.AluOpType
ACT = mybir.ActivationFunctionType
AX = mybir.AxisListType.X

CHUNK = 64
H_A, DQK_A = 4, 64
DV_A = 2 * DQK_A
H_B, DH_B = 4, 64
H_C, DH_C = 4, 64
H_IDX, D_IDX = 8, 64
H_X = 4
REL_MAX = 128
TOPK = 64
LN_EPS, RMS_EPS = 1e-5, 1e-6
NEG_INF = -1e30
DVE_LINKS = 96
GONE = -3e38
FILL = 3e38
FAR = float(2 ** 100)


class Signal:

    def __init__(self, sem, per_layer, step=1):
        self.sem, self.per_layer, self.step = sem, per_layer, step

    def wait(self, eng, layer, count):
        eng.wait_ge(self.sem, layer * (self.per_layer * self.step) + count * self.step)


class Order:

    def __init__(self, eng, sem):
        self.eng, self.sem, self.base, self.n = eng, sem, 0, 0

    def link(self, ins):
        self.n += 1
        ins.then_inc(self.sem, 1)
        self.eng.wait_ge(self.sem, self.base + self.n)


PLAN = [
    ("tile", "HT0", "a"), ("tile", "HT1", "v"), ("tile", "HT2", "a"), ("tile", "HT3", "v"),
    ("tile", "KI", "v"), ("tile", "QI0", "a"), ("tile", "QI1", "a"),
    ("dots", 1), ("dots", 0), ("select", 0, 0),
    ("tile", "QA0", "a"), ("select", 0, 1), ("tile", "QA1", "a"), ("select", 0, 2),
    ("tile", "KA0", "a"), ("select", 1, 0), ("tile", "KA1", "a"),
    ("scores", "A0"), ("max", "A0"), ("scores", "A1"), ("max", "A1"), ("exp", "A0"),
    ("tile", "QB", "a"), ("select", 1, 1), ("exp", "A1"),
    ("tile", "KB", "a"), ("mix", 0), ("select", 1, 2), ("tile", "VB", "a"), ("mix", 1),
    ("tile", "QC", "a"), ("tile", "KC", "a"), ("tile", "VC", "a"),
    ("tile", "TA0", "v"),
    ("scores", "B0"), ("scores", "C0"), ("max", "B0"), ("max", "C0"), ("exp", "B0"), ("exp", "C0"),
    ("tile", "VA0", "a"), ("tile", "TA1", "v"), ("tile", "TA2", "a"),
    ("scores", "B1"), ("scores", "C1"), ("max", "B1"), ("max", "C1"), ("exp", "B1"), ("exp", "C1"),
    ("tile", "VA1", "a"), ("tile", "OA0", "v"), ("tile", "OA1", "v"),
    ("tile", "KX0", "a"), ("tile", "TB0", "a"), ("tile", "TC0", "v"),
    ("tile", "KX1", "a"), ("tile", "TB1", "a"), ("tile", "TB2", "v"), ("tile", "TC1", "a"), ("tile", "TC2", "v"),
    ("tile", "OBC0", "v"), ("tile", "OBC1", "v"),
    ("tile", "YA0", "s"), ("tile", "YB0", "s"), ("tile", "YA1", "s"), ("tile", "YB1", "s"),
    ("acc", "WO", 0), ("acc", "WO", 1), ("acc", "WO", 2), ("acc", "WO", 3), ("sums", 0),
    ("tile", "KX2", "a"), ("tile", "KX3", "a"), ("norm", 0),
    ("tile", "HX0", "a"), ("tile", "HX1", "v"), ("tile", "HX2", "a"), ("tile", "HX3", "v"),
    ("tile", "QX0", "a"), ("tile", "QX1", "a"), ("residual", 0), ("tile", "QX2", "a"), ("tile", "QX3", "a"),
    ("scores", "X0"), ("scores", "X1"), ("max", "X0"), ("max", "X1"), ("exp", "X0"), ("exp", "X1"),
    ("tile", "VX0", "a"), ("over", 0), ("tile", "VX1", "a"), ("over", 1),
    ("tile", "TX0", "a"), ("tile", "TX1", "v"), ("tile", "VX2", "a"), ("tile", "TX2", "a"), ("tile", "TX3", "v"),
    ("tile", "VX3", "a"),
    ("tile", "OX0", "s"), ("tile", "OX1", "s"), ("tile", "OX2", "s"), ("tile", "OX3", "s"),
    ("acc", "WX", 0), ("acc", "WX", 1), ("acc", "WX", 2), ("acc", "WX", 3), ("sums", 1), ("norm", 1),
    ("tile", "HF0", "a"), ("tile", "HF1", "v"), ("tile", "HF2", "a"), ("tile", "HF3", "v"),
    ("residual", 1),
]
TILES = [(x[1], x[2]) for x in PLAN if x[0] == "tile"]
TILE_AT = {name: i for i, (name, _) in enumerate(TILES)}
LAST = {name: "v" if who == "s" else who for name, who in TILES}
TAKEN = {w: [n for n, _ in TILES if LAST[n] == w] for w in "av"}
PARTED = [n for n, who in TILES if who == "s" or n[:2] in ("HT", "HX", "HF")]

GROUPS = [x[1] for x in PLAN if x[0] == "scores"]

PIECES = [x[1] if x[0] == "tile" else f"{x[1]}{x[2]}" for x in PLAN
          if x[0] == "acc" or x[0] == "tile" and x[1][0] in "QKV"]
PIECE_AT = {name: i for i, name in enumerate(PIECES)}
PIECE = 2048
SLOTS = 3


def through(group):
    return GROUPS.index("C0" if group == "B0" else group) + 1


def hybrid_encoder(nc, x, mem, w_in, lam_q1, lam_k1, lam_q2, lam_k2, diff_norm_g, rel_bias, w_out,
                   ln1_g, ln1_b, xattn_wq, xattn_wk, xattn_wv, xattn_wo, ln2_g, ln2_b,
                   ffn_w1, ffn_w3, ffn_w2, moe_router, moe_w1, moe_w3, moe_w2, ln3_g, ln3_b, out):
    _, SEQ, D = x.shape
    N_MEM = mem.shape[1]
    DEPTH = w_in.shape[0]
    N_IN = w_in.shape[2]
    D_FF = ffn_w1.shape[2]
    N_EXPERTS, D_FF_E = moe_w1.shape[1], moe_w1.shape[3]
    KT = D // P
    TB = SEQ // P
    ALPHA = (2.0 * DEPTH) ** 0.25
    assert (SEQ, N_MEM, D, TB, KT, DEPTH) == (256, 256, 1024, 2, 8, 2)
    HALF = D // 2
    NKEYS = [P, 2 * P]
    SMALL = D_IDX + H_IDX
    SCALE = DQK_A ** -0.5
    assert DQK_A == DH_B == DH_C == D_IDX == 64
    SCALE_X = float((D // H_X) ** -0.5)
    slopes = [2.0 ** (-8.0 * i / (H_A + H_C)) for i in range(1, H_A + H_C + 1)]
    lam_inits = [0.8 - 0.6 * math.exp(-0.3 * l) for l in range(DEPTH)]

    C_QA, C_KA, C_VA = 0, 512, 1024
    C_QB, C_KB, C_VB, C_QC, C_KC, C_VC, C_QI, C_KI = 1536, 1792, 2048, 2304, 2560, 2816, 3072, 3584
    assert C_KI + SMALL == N_IN
    M_QA, M_KA, M_QB, M_KB, M_QC, M_KC, M_QI, M_KI = 0, 4, 8, 10, 12, 14, 12, 16
    M_ALL = 17

    FE = 2 * P
    STEPS = D_FF_E // (2 * FE)
    assert STEPS * 2 * FE == D_FF_E
    PAIRS = D_FF // (2 * P)
    assert PAIRS % 2 == 1 and PAIRS * 2 * P == D_FF
    FIRST = [0, len(PIECES) + 3 * PAIRS]
    ALL = FIRST[1] + len(PIECES)
    EXTRA = (2 * SEQ - 1) // (P + 1)
    assert EXTRA == 3 and TB == 2

    with ExitStack() as ctx:
        def sb(name, shape, dt=F32):
            return ctx.enter_context(nc.sbuf_tensor(name, shape, dt))

        def sem(name):
            return ctx.enter_context(nc.semaphore(name))

        PS = ctx.enter_context(nc.psum_tensor("PS", [P, 8, 512], F32))

        floats = {}
        arena_at = 0
        for name, n in (("RAW", SLOTS * PIECE), ("SPH", SLOTS * PIECE), ("SPL", SLOTS * PIECE),
                        ("QK", M_ALL * SEQ), ("VN", TB * D), ("KX", KT * N_MEM), ("VX", TB * D),
                        ("XTH", KT * SEQ), ("XTL", KT * SEQ), ("YMH", KT * N_MEM), ("YML", KT * N_MEM),
                        ("E", 3072), ("PT", 3072)):
            floats[name] = arena_at
            arena_at += n
        sb("arena", [P, arena_at])
        arena_base = nc.sbuf_base - 4 * arena_at

        def over(name, shape, dt=F32, region=None, at=0):
            return nc.alloc_sbuf_tensor_at(name, shape, dt, offset=arena_base + 4 * (floats[region or name] + at))

        RAW = over("RAW", [P, SLOTS * PIECE])
        SPH = over("SPH", [P, SLOTS * PIECE], F32R)
        SPL = over("SPL", [P, SLOTS * PIECE], F32R)
        QK = over("QK", [P, M_ALL, SEQ])
        H = sb("H", [P, TB, D])
        N = sb("N", [P, TB, D])
        VN = over("VN", [P, TB, D])
        KX = over("KX", [P, KT, N_MEM])
        VX = over("VX", [P, TB, D])
        XTH = over("XTH", [P, KT, SEQ], F32R)
        XTL = over("XTL", [P, KT, SEQ], F32R)
        YMH = over("YMH", [P, KT, N_MEM], F32R)
        YML = over("YML", [P, KT, N_MEM], F32R)
        E = over("E", [P, 3072])
        PT = over("PT", [P, 3072])
        WI = sb("WI", [P, TB, H_IDX])
        GB = sb("GB", [P, 2, D])
        HK = sb("HK", [P, 2, H_B, P])
        iden = sb("iden", [P, P])
        flip8 = sb("flip8", [P, P])
        idenb = sb("idenb", [P, P], BF16)
        slopeI = sb("slopeI", [P, H_A + H_C, P], BF16)
        dist = sb("dist", [P, 2 * P], BF16)
        maskB = sb("maskB", [P, P], BF16)
        maskI = sb("maskI", [P, 2 * P])
        selb = sb("selb", [P, 3 * P], BF16)
        LG = sb("LG", [P, 6, KT])
        LB = sb("LB", [P, 6, KT])
        gain = sb("gain", [P, DEPTH])
        neglam = sb("neglam", [P, DEPTH])
        lam_work = sb("lam_work", [P, 4 * DEPTH])
        st = sb("st", [P, TB, 2, 6])
        mv = sb("mv", [P, TB, 2])
        var = sb("var", [P, TB])
        rstd = sb("rstd", [P, TB])
        mhalf = sb("mhalf", [P, 4])
        top8 = sb("top8", [P, 8])
        mx = sb("mx", [P, 8, 8])
        nmx = sb("nmx", [P, 8, 8])
        sums = sb("sums", [P, 8, 8])
        rs = sb("rs", [P, 8, 8])
        mix = sb("mix", [P, 4])
        ss = sb("ss", [P, 4])
        rms = sb("rms", [P, 4])
        isc = PT[:, 2048:2048 + 2 * P]
        work = PT[:, 2304:2304 + 2 * P]
        sq = PT[:, 2560:3072].rearrange("p (h d) -> p h d", h=4)
        TURN = [PT[:, 1024 + 512 * k:1536 + 512 * k] for k in range(4)]

        EV = {
            "A0": E[:, 0:1024].rearrange("p (h k) -> p h k", k=P),
            "A1": E[:, 1024:3072].rearrange("p (h k) -> p h k", k=2 * P),
            "B0": E[:, 0:512].rearrange("p (h k) -> p h k", k=P),
            "C0": E[:, 512:1024].rearrange("p (h k) -> p h k", k=P),
            "B1": E[:, 1024:2048].rearrange("p (h k) -> p h k", k=2 * P),
            "C1": E[:, 2048:3072].rearrange("p (h k) -> p h k", k=2 * P),
            "X0": E[:, 0:1024].rearrange("p (h k) -> p h k", k=2 * P),
            "X1": E[:, 1024:2048].rearrange("p (h k) -> p h k", k=2 * P),
        }
        DOT = {1: E[:, 1024:3072].rearrange("p (h k) -> p h k", k=2 * P),
               0: E[:, 0:1024].rearrange("p (h k) -> p h k", k=P)}

        def heads(ap):
            return ap.rearrange("p (h k) -> p h k", k=P)

        PTV = {"TB0": heads(PT[:, 0:512]), "TC0": heads(PT[:, 512:1024]),
               "TA0": heads(PT[:, 1024:1536]), "TA1": heads(PT[:, 1536:2048]), "TA2": heads(PT[:, 2048:2560]),
               "TB1": heads(PT[:, 1024:1536]), "TB2": heads(PT[:, 1536:2048]),
               "TC1": heads(PT[:, 2048:2560]), "TC2": heads(PT[:, 2560:3072])}
        PX = PT[:, 0:2048].rearrange("p (t h q) -> p t h q", t=2, h=H_X)

        def scores(group):
            bank, n, a, b, keys = {"A0": (4, 2, 0, 512, P), "A1": (0, 4, 0, 512, 2 * P),
                                   "B0": (4, 2, 0, 256, P), "C0": (4, 2, 256, 512, P),
                                   "B1": (0, 2, 0, 512, 2 * P), "C1": (2, 2, 0, 512, 2 * P),
                                   "X0": (4, 2, 0, 512, 2 * P), "X1": (0, 2, 0, 512, 2 * P)}[group]
            if n == 2:
                return PS[:, bank:bank + 2, a:b].rearrange("p b (m k) -> p b m k", k=keys)
            return PS[:, bank:bank + 4, :].rearrange("p (a b) (m k) -> p a (b m) k", a=2, k=keys)

        def score(group, i):
            S = scores(group)
            return S[:, i // S.shape[2], i % S.shape[2], :]

        def maps_of(group):
            return 8 if group[0] == "A" else 4

        def place(h, n):
            return (h % 2) * (n // 2) + h // 2

        DOTS = {1: PS[:, 0:4, :].rearrange("p b (m k) -> p (b m) k", k=2 * P),
                0: PS[:, 4:6, :].rearrange("p b (m k) -> p (b m) k", k=P)}

        def tile_bank(name):
            return PS[:, 6 + TILE_AT[name] % 2, :]

        R1 = {"a": VN, "b": KX}
        R3 = {"a": VX, "b": over("R3b", [P, PIECE], F32, "QK", 0)}
        R2 = {"a": over("R2a", [P, PIECE], F32, "QK", PIECE), "b": over("R2b", [P, PIECE], F32, "RAW", 0)}
        flat = {"R1a": over("R1a_flat", [P, PIECE], F32, "VN"), "R1b": over("R1b_flat", [P, PIECE], F32, "KX"),
                "R3a": over("R3a_flat", [P, PIECE], F32, "VX"), "R3b": R3["b"]}
        S1H = {"a": SPH[:, 0:PIECE], "b": SPH[:, PIECE:2 * PIECE]}
        S1L = {"a": SPL[:, 0:PIECE], "b": SPL[:, PIECE:2 * PIECE]}
        S3H = {"a": SPH[:, 2 * PIECE:3 * PIECE], "b": over("S3bh", [P, PIECE], F32R, "E")[:]}
        S3L = {"a": SPL[:, 2 * PIECE:3 * PIECE], "b": over("S3bl", [P, PIECE], F32R, "PT")[:]}
        HRH = over("HRH", [P, TB, D], F32R, "YMH")
        HRL = over("HRL", [P, TB, D], F32R, "YML")
        XGH = over("XGH", [P, KT, P], F32R, "XTH")
        XGL = over("XGL", [P, KT, P], F32R, "XTL")
        ONE = over("ONE", [P, TB, P], F32R, "RAW", PIECE)
        small = over("small", [P, 2 * PIECE - 256], F32, "RAW", PIECE + 256)
        SIL = {"a": small[:, 0:256], "b": small[:, 256:512]}
        HID = {"a": small[:, 512:768], "b": small[:, 768:1024]}
        HIDT = {"a": small[:, 1024:1280], "b": small[:, 1280:1536]}
        GATED = small[:, 1536:1792].rearrange("p (b s) -> p b s", b=TB)
        GATEDT = small[:, 1792:2048]
        YE = small[:, 2048:3072]
        FSIL = E[:, 0:512]
        FHID = E[:, 512:1024]
        FHH = over("FHH", [P, 2, SEQ], F32R, "E", 1024)
        FHL = over("FHL", [P, 2, SEQ], F32R, "E", 1536)
        iota_s = sb("iota_s", [P, 2 * P])
        before = sb("before", [P, P])
        ones = sb("ones", [P, P])
        router = sb("router", [P, KT, N_EXPERTS])
        routerh = sb("routerh", [P, KT, N_EXPERTS], F32R)
        routerl = sb("routerl", [P, KT, N_EXPERTS], F32R)
        logit = over("logit", [P, TB, 16], F32, "PT", 2048)
        best = over("best", [P, TB, 8], F32, "PT", 2080)
        take1 = over("take1", [P, TB, 8], F32, "PT", 2096)
        take2 = over("take2", [P, TB, 8], F32, "PT", 2112)
        left1 = over("left1", [P, TB, 16], F32, "PT", 2128)
        left2 = over("left2", [P, TB, 16], F32, "PT", 2160)
        chosen = sb("chosen", [P, TB, N_EXPERTS])
        gate = sb("gate", [P, TB, N_EXPERTS])
        gtmp = sb("gtmp", [P, TB, N_EXPERTS])
        gw = sb("gw", [P, TB, 4])
        rank = sb("rank", [P, TB, N_EXPERTS])
        cand = sb("cand", [1, N_EXPERTS])
        ctmp = sb("ctmp", [1, N_EXPERTS])
        full = sb("full", [1, 4])
        fulli = sb("fulli", [1, 4], I32)

        s_x = sem("s_x")
        s_mem = sem("s_mem")
        s_rows = sem("s_rows")
        s_lam = sem("s_lam")
        s_table = sem("s_table")
        s_table_out = sem("s_table_out")
        s_router = sem("s_router")
        s_out = sem("s_out")
        pool_done = sem("pool_done")
        columns_ready = sem("columns_ready")
        columns_done = sem("columns_done")
        mem_ready = sem("mem_ready")
        mem_done = sem("mem_done")
        tail_done = sem("tail_done")
        dist_done = sem("dist_done")
        lam_ready = sem("lam_ready")
        lam_exp = sem("lam_exp")
        order_pool = sem("order_pool")
        order_dve = sem("order_dve")
        order_ffn = sem("order_ffn")
        order_moe = sem("order_moe")

        gb_loaded = Signal(sem("gb_loaded"), 3, 32)
        hankel_loaded = Signal(sem("hankel_loaded"), 1, 32)
        raw_loaded = [sem(f"raw_loaded{s}") for s in range(SLOTS)]
        hi_done = sem("hi_done")
        lo_done = sem("lo_done")
        router_hi = sem("router_hi")
        router_lo = sem("router_lo")
        mem_hi = sem("mem_hi")
        tile_ready = Signal(sem("tile_ready"), len(TILES))
        tile_taken = {"a": Signal(sem("tile_taken_act"), len(TAKEN["a"])),
                      "v": Signal(sem("tile_taken_dve"), len(TAKEN["v"]))}
        part_hi = Signal(sem("part_hi"), len(PARTED))
        turned_lo = Signal(sem("turned_lo"), 12)
        dots_ready = Signal(sem("dots_ready"), 2)
        relu_done = Signal(sem("relu_done"), 2)
        selected = Signal(sem("selected"), 2)
        scores_ready = Signal(sem("scores_ready"), len(GROUPS))
        max_done = Signal(sem("max_done"), len(GROUPS))
        exp_done = Signal(sem("exp_done"), len(GROUPS))
        probs_ready = Signal(sem("probs_ready"), 4)
        rows_done = Signal(sem("rows_done"), 2)
        acc_ready = Signal(sem("acc_ready"), 16)
        sum_done = Signal(sem("sum_done"), 12)
        var_ready = Signal(sem("var_ready"), 8)
        rstd_ready = Signal(sem("rstd_ready"), 8)
        norm_done = Signal(sem("norm_done"), 6)
        resid_done = Signal(sem("resid_done"), 3)

        ffn_g = sem("ffn_g")
        ffn_silu = sem("ffn_silu")
        ffn_u = sem("ffn_u")
        ffn_hidden = sem("ffn_hidden")
        ffn_hi = sem("ffn_hi")
        ffn_lo = sem("ffn_lo")
        ffn_down = sem("ffn_down")

        def by_place(name):
            return {c: sem(f"{name}_{c}") for c in "ab"}

        loaded1, loaded3, loaded2 = by_place("loaded1"), by_place("loaded3"), by_place("loaded2")
        hi1, hi3 = by_place("hi1"), by_place("hi3")
        lo1, lo3 = by_place("lo1"), by_place("lo3")
        g_ready, u_ready = by_place("g_ready"), by_place("u_ready")
        silu_done, hidden_done = by_place("silu_done"), by_place("hidden_done")
        turned_ready, turned_done = by_place("turned_ready"), by_place("turned_done")
        w2_used = by_place("w2_used")
        router_ready = sem("router_ready")
        logit_done = sem("logit_done")
        exp2_done = sem("exp2_done")
        chosen_done = sem("chosen_done")
        rank_ready = sem("rank_ready")
        table_done = sem("table_done")
        rows_hi = sem("rows_hi")
        rows_lo = sem("rows_lo")
        onehot_done = sem("onehot_done")
        gather_ready = sem("gather_ready")
        gather_hi = sem("gather_hi")
        gather_lo = sem("gather_lo")
        gatedT_ready = sem("gatedT_ready")
        gatedT_done = sem("gatedT_done")
        y_act = sem("y_act")
        y_dve = sem("y_dve")
        scatter_ready = sem("scatter_ready")
        scatter_done = sem("scatter_done")

        scratch = nc.dram_tensor("rel_tail", [DEPTH * H_B, 2 * P], F32, kind="Internal")
        rel_rows = rel_bias.rearrange("l h r -> (l h) r")
        R = 2 * REL_MAX + 1

        block = ctx.enter_context(nc.Block())

        def extra_experts(eng, work_on):
            eng.wait_ge(table_done, 1)
            many = eng.value_load(fulli[0:1, EXTRA:EXTRA + 1], min_val=0, max_val=EXTRA)
            for j in range(EXTRA):
                e = eng.value_load(fulli[0:1, j:j + 1], min_val=0, max_val=N_EXPERTS - 1)
                with eng.If(many > j):
                    work_on(e, N_EXPERTS + j)

        def used(eng, g):
            layer = g >= FIRST[1]
            i = g - FIRST[layer]
            if i >= len(PIECES):
                p, part = (i - len(PIECES) + 1) // 3, (i - len(PIECES) + 1) % 3
                if i == FIRST[1] - 1:
                    eng.wait_ge(ffn_down, PAIRS)
                elif i == len(PIECES):
                    eng.wait_ge(ffn_g, 1)
                elif i == len(PIECES) + 1:
                    eng.wait_ge(ffn_u, 1)
                elif part == 0:
                    eng.wait_ge(ffn_g, p + 1)
                elif part == 1:
                    eng.wait_ge(ffn_down, p)
                else:
                    eng.wait_ge(ffn_u, p + 1)
            elif PIECES[i][0] == "W":
                acc_ready.wait(eng, layer, (0 if PIECES[i][1] == "O" else 8) + 2 * int(PIECES[i][2]) + 2)
            else:
                tile_ready.wait(eng, layer, TILE_AT[PIECES[i]] + 1)

        def cut(t, g):
            s = g % SLOTS
            return t[:, s * PIECE:(s + 1) * PIECE]

        def is_small(g):
            return g in FIRST

        def columns(w, a, n):
            return w[:, a:a + n].rearrange("(t p) n -> p t n", p=P)

        def by_tiles(ap):
            return ap.rearrange("p (t n) -> p t n", t=KT)

        def by_rows(ap):
            return ap.rearrange("p (f n) -> p f n", n=D)

        @block.sync
        def _(sp):
            for b in range(TB):
                sp.dma_start(N[:, b, :], x[0, b * P:(b + 1) * P, :]).then_inc(s_x, 16)

            def load(slot, dst, src):
                sp.dma_start(dst, src).then_inc(raw_loaded[slot], 16)

            def layer_pieces(layer):
                where = {"QI": (w_in, C_QI), "QA": (w_in, C_QA), "KA": (w_in, C_KA), "QB": (w_in, C_QB),
                         "KB": (w_in, C_KB), "VB": (w_in, C_VB), "QC": (w_in, C_QC), "KC": (w_in, C_KC),
                         "VC": (w_in, C_VC), "VA": (w_in, C_VA), "KX": (xattn_wk, 0), "VX": (xattn_wv, 0),
                         "WO": (w_out, 0), "QX": (xattn_wq, 0), "WX": (xattn_wo, 0)}
                for i, name in enumerate(PIECES):
                    g = FIRST[layer] + i
                    if g >= SLOTS:
                        sp.wait_ge(lo_done, g - SLOTS + 1)
                    if name == "KI":
                        load(g % SLOTS, by_tiles(cut(RAW, g)[:, 0:KT * SMALL]), columns(w_in[layer], C_KI, SMALL))
                    else:
                        w, a = where[name[:2]]
                        a += 256 * int(name[2]) if name[2:] else 0
                        load(g % SLOTS, by_tiles(cut(RAW, g)), columns(w[layer], a, 256))

            def feed_forward():
                def piece(slot, w, k, held):
                    sp.wait_ge(lo_done, held)
                    dst = RAW[:, slot * PIECE:(slot + 1) * PIECE]
                    if w is ffn_w2:
                        load(slot, by_rows(dst), w[0][k, :].rearrange("(f p) n -> p f n", p=P))
                    else:
                        load(slot, by_tiles(dst), w[0][:, k].rearrange("(t p) n -> p t n", p=P))

                g = len(PIECES)
                piece(g % SLOTS, ffn_w1, slice(0, 2 * P), g - 2)
                piece((g + 1) % SLOTS, ffn_w3, slice(0, 2 * P), g - 1)
                with sp.Fori(1, PAIRS) as p:
                    now, one_before = bass.ds(p * (2 * P), 2 * P), bass.ds((p - 1) * (2 * P), 2 * P)
                    piece((g + 2) % SLOTS, ffn_w1, now, p * 3 + (g - 3))
                    piece((g + 3) % SLOTS, ffn_w2, one_before, p * 3 + (g - 2))
                    piece((g + 4) % SLOTS, ffn_w3, now, p * 3 + (g - 1))
                g = FIRST[1] - 1
                piece(g % SLOTS, ffn_w2, slice(D_FF - 2 * P, D_FF), g - 2)

            layer_pieces(0)
            feed_forward()
            layer_pieces(1)

            def expert_weights(e, n):
                def up(c, j):
                    col = bass.ds(j * (2 * FE) + (0 if c == "a" else FE), FE)
                    sp.wait_ge(lo1[c], n * STEPS + j)
                    sp.dma_start(by_tiles(flat["R1" + c][:]), moe_w1[0, e][:, col].rearrange("(t p) n -> p t n", p=P)
                                 ).then_inc(loaded1[c], 16)
                    sp.wait_ge(lo3[c], n * STEPS + j)
                    sp.dma_start(by_tiles(flat["R3" + c][:]), moe_w3[0, e][:, col].rearrange("(t p) n -> p t n", p=P)
                                 ).then_inc(loaded3[c], 16)

                def down(c, j):
                    col = bass.ds(j * (2 * FE) + (0 if c == "a" else FE), FE)
                    sp.wait_ge(w2_used[c], n * STEPS + j)
                    sp.dma_start(by_rows(R2[c][:]), moe_w2[0, e][col, :].rearrange("(f p) n -> p f n", p=P)
                                 ).then_inc(loaded2[c], 16)

                up("a", 0)
                with sp.Fori(0, STEPS - 1) as j:
                    up("b", j)
                    down("a", j)
                    up("a", j + 1)
                    down("b", j)
                up("b", STEPS - 1)
                down("a", STEPS - 1)
                down("b", STEPS - 1)

            tile_ready.wait(sp, 1, TILE_AT["OX3"] + 1)
            scores_ready.wait(sp, 1, len(GROUPS))
            sp.wait_ge(lo_done, ALL)
            with sp.Fori(0, N_EXPERTS) as e:
                expert_weights(e, e)
            sp.wait_ge(table_done, 1)
            extra_experts(sp, lambda e, n: expert_weights(e, n))
            resid_done.wait(sp, DEPTH - 1, 3)
            for b in range(TB):
                sp.dma_start(out[0, b * P:(b + 1) * P, :], H[:, b, :]).then_inc(s_out, 16)
            sp.wait_ge(s_out, 16 * TB)

        @block.gpsimd
        def _(pool):
            o = Order(pool, order_pool)
            g = nc.gpsimd
            rows_g, rows_b = PT[0:6 * KT, 0:P], PT[0:6 * KT, P:2 * P]
            table = PT[0:DEPTH * H_B, 2 * P:2 * P + R]
            tail = PT[0:DEPTH * H_B, 768:768 + 2 * P]
            o.link(g.memset(rows_g, 1.0))
            o.link(g.memset(rows_b, 0.0))
            for i, (gg, bb) in enumerate([(ln3_g, ln3_b), (ln1_g, ln1_b), (ln2_g, ln2_b)]):
                r = i * 2 * KT
                first, layers = (KT, 1) if i == 0 else (0, DEPTH)
                for rows, src in ((rows_g, gg), (rows_b, bb)):
                    pool.dma_start(rows[r + first:r + 2 * KT, :],
                                   src[0:layers, :].rearrange("l (t p) -> (l t) p", p=P)).then_inc(s_rows, 16)
            pool.dma_start(PT[0:DEPTH, 1024:1024 + DV_A], diff_norm_g).then_inc(s_rows, 16)
            pool.dma_start(table, rel_rows).then_inc(s_table, 16)
            for i, q in enumerate((lam_q1, lam_k1, lam_q2, lam_k2)):
                pool.dma_start(PT[:, 1152 + i * 128:1152 + (i + 1) * 128],
                               q.rearrange("l d -> (l d)").partition_broadcast(P)).then_inc(s_lam, 16)
            for b in range(TB):
                pool.dma_start(E[:, b * D:(b + 1) * D],
                               mem[0, b * P:(b + 1) * P, :]).then_inc(s_mem, 16)
            pool.dma_start(router[:], moe_router[0].rearrange("(t p) n -> p t n", p=P)).then_inc(s_router, 16)

            o.link(g.memset(iden[:], 0.0))
            o.link(g.affine_select(out=iden[:], in_=iden[:], compare_op=ALU.not_equal, fill=1.0, base=0,
                                   pattern=[[-1, P]], channel_multiplier=1))
            o.link(g.memset(flip8[:], 0.0))
            o.link(g.affine_select(out=flip8[:], in_=flip8[:], compare_op=ALU.not_equal, fill=1.0 / SCALE,
                                   base=1 - P, pattern=[[1, P]], channel_multiplier=1))
            o.link(g.memset(idenb[:], 0.0))
            o.link(g.affine_select(out=idenb[:], in_=idenb[:], compare_op=ALU.not_equal, fill=1.0, base=0,
                                   pattern=[[-1, P]], channel_multiplier=1))
            o.link(g.memset(slopeI[:], 0.0))
            for j, s in enumerate(slopes):
                o.link(g.affine_select(out=slopeI[:, j, :], in_=slopeI[:, j, :], compare_op=ALU.not_equal,
                                       fill=-s / SCALE, base=0, pattern=[[-1, P]], channel_multiplier=1))
            o.link(g.iota(isc, pattern=[[-1, 2 * P]], base=P, channel_multiplier=1,
                          allow_small_or_imprecise_dtypes=True))
            o.link(g.iota(iota_s[:], pattern=[[1, 2 * P]], base=0, channel_multiplier=0,
                          allow_small_or_imprecise_dtypes=True))
            o.link(g.memset(maskI[:], 0.0))
            o.link(g.memset(maskI[0:CHUNK, P + CHUNK:2 * P], NEG_INF))
            o.link(g.memset(maskB[:], 0.0))
            o.link(g.memset(maskB[0:CHUNK, CHUNK:P], -FAR))
            o.link(g.memset(mhalf[:], -0.5))
            o.link(g.memset(ones[:], 1.0))
            o.link(g.memset(before[:], 1.0))
            o.link(g.affine_select(out=before[:], in_=before[:], compare_op=ALU.is_gt, fill=0.0, base=0,
                                   pattern=[[1, P]], channel_multiplier=-1))
            g.memset(top8[:], 0.0).then_inc(pool_done, 1)

            pool.wait_ge(tail_done, 1)
            pool.dma_start(scratch.ap(), tail).then_inc(s_table_out, 16)
            pool.wait_ge(s_table_out, 16)

            lns = ((ln1_g, ln1_b), (ln2_g, ln2_b), (ln3_g, ln3_b))

            def to_rstd(n, layer, v, out_, width):
                var_ready.wait(pool, layer, n)
                g.tensor_tensor(out_, v, mhalf[:, 0:width], ALU.pow).then_inc(rstd_ready.sem, 1)

            for layer in range(DEPTH):
                exp_done.wait(pool, layer, 0)
                near = bass.AP(rel_bias.tensor, 1, [[H_B * R, DEPTH], [1, P], [R, H_B], [1, P]])
                far = bass.AP(scratch, 0, [[H_B * 2 * P, DEPTH], [1, P], [2 * P, H_B], [1, P]])
                pool.dma_start(HK[:, 0], near[layer]).then_inc(hankel_loaded.sem, 16)
                pool.dma_start(HK[:, 1], far[layer]).then_inc(hankel_loaded.sem, 16)
                for i, (gg, bb) in enumerate(lns):
                    resid_done.wait(pool, layer, i)
                    pool.dma_start(GB[:, 0, :], gg[layer].partition_broadcast(P)).then_inc(gb_loaded.sem, 16)
                    pool.dma_start(GB[:, 1, :], bb[layer].partition_broadcast(P)).then_inc(gb_loaded.sem, 16)
                    if i == 0:
                        to_rstd(1, layer, ss[:], rms[:], 4)
                        to_rstd(2, layer, ss[:], rms[:], 4)
                    for b in range(TB):
                        to_rstd(3 + 2 * i + b, layer, var[:, b:b + 1], rstd[:, b:b + 1], 1)

        @block.tensor
        def _(pe):
            mm = pe.matmul

            def turn(dst, src, n=P):
                return pe.transpose(dst, src, iden[0:n, 0:n])

            def mm3(dst, wh, wl, xh, xl, start, stop):
                mm(dst, wh, xh, start=start, stop=False)
                mm(dst, wh, xl, start=False, stop=False)
                return mm(dst, wl, xh, start=False, stop=stop)

            pe.wait_ge(pool_done, 1)
            pe.wait_ge(s_rows, 16 * 7)
            turn(PS[:, 0, 0:6 * KT], PT[0:6 * KT, 0:P], 6 * KT)
            turn(PS[:, 0, 64:64 + 6 * KT], PT[0:6 * KT, P:2 * P], 6 * KT)
            turn(PS[:, 0, 128:128 + DEPTH], PT[0:DEPTH, 1024:1024 + DV_A], DEPTH).then_inc(columns_ready, 1)
            pe.wait_ge(s_mem, 16 * TB)
            for t in range(KT):
                for b in range(TB):
                    last = turn(PS[:, 1 + t // 2, (t % 2) * SEQ + b * P:(t % 2) * SEQ + (b + 1) * P],
                                E[:, b * D + t * P:b * D + (t + 1) * P])
            last.then_inc(mem_ready, 1)
            pe.wait_ge(s_x, 16 * TB)
            pe.wait_ge(columns_done, 3)
            pe.wait_ge(mem_done, 1)
            pe.wait_ge(dist_done, 1)

            def begin(name, layer):
                i = TILE_AT[name]
                if i >= 2:
                    taken(TILES[i - 2][0], layer)
                return tile_bank(name)

            def taken(name, layer):
                who = LAST[name]
                tile_taken[who].wait(pe, layer, TAKEN[who].index(name) + 1)

            def ready(ins):
                ins.then_inc(tile_ready.sem, 1)

            def parts(g):
                pe.wait_ge(lo_done, g + 1)
                return cut(SPH, g), cut(SPL, g)

            def turned_rows(name, layer):
                bank = begin(name, layer)
                k = int(name[2])
                for t in (2 * k, 2 * k + 1):
                    for b in range(TB):
                        c = (t % 2) * SEQ + b * P
                        last = turn(bank[:, c:c + P], N[:, b, t * P:(t + 1) * P])
                ready(last)

            def project_small(g, layer):
                bank = begin("KI", layer)
                WH, WL = [w[:, 0:KT * (P + 8)].rearrange("p (t n) -> p t n", t=KT) for w in parts(g)]
                for t in range(KT):
                    mm3(bank[:, 0:SEQ], WH[:, t, 0:P], WL[:, t, 0:P], XTH[:, t, :], XTL[:, t, :],
                        t == 0, t == KT - 1)
                for b in range(TB):
                    r = slice(b * P, (b + 1) * P)
                    for t in range(KT):
                        last = mm3(bank[:, SEQ + b * 8:SEQ + b * 8 + 8], XTH[:, t, r], XTL[:, t, r],
                                   WH[:, t, P:P + 8], WL[:, t, P:P + 8], t == 0, t == KT - 1)
                ready(last)

            def project_turned(name, g, XH, XL, layer):
                bank = begin(name, layer)
                WH, WL = [by_tiles(w) for w in parts(g)]
                for m in range(2):
                    c = slice(m * P, (m + 1) * P)
                    for t in range(KT):
                        last = mm3(bank[:, m * SEQ:(m + 1) * SEQ], WH[:, t, c], WL[:, t, c], XH[:, t, :], XL[:, t, :],
                                   t == 0, t == KT - 1)
                ready(last)

            def rows_product(dsts, g, XH, XL):
                WH, WL = [by_tiles(w) for w in parts(g)]
                for b in range(TB):
                    r = slice(b * P, (b + 1) * P)
                    for t in range(KT):
                        last = mm3(dsts[b], XH[:, t, r], XL[:, t, r], WH[:, t, :], WL[:, t, :], t == 0, t == KT - 1)
                    yield last

            def project_rows(name, g, XH, XL, layer):
                bank = begin(name, layer)
                for last in rows_product([bank[:, 0:256], bank[:, 256:512]], g, XH, XL):
                    pass
                ready(last)

            def accumulate(name, layer):
                j = int(name[2])
                if name == "WO0":
                    for tile in ("YA0", "YB0", "YA1", "YB1"):
                        taken(tile, layer)
                if name == "WX0":
                    taken("OX2", layer)
                    taken("OX3", layer)
                    exp_done.wait(pe, layer, 8)
                c = slice((j % 2) * 256, (j % 2) * 256 + 256)
                dsts = [PS[:, 2 * (j // 2) + b, c] for b in range(TB)]
                for last in rows_product(dsts, FIRST[layer] + PIECE_AT[name], XTH, XTL):
                    last.then_inc(acc_ready.sem, 1)

            def group_free(group, layer):
                if group == "A0":
                    relu_done.wait(pe, layer, 2)
                elif group == "A1":
                    relu_done.wait(pe, layer, 1)
                elif group in ("B0", "C0"):
                    exp_done.wait(pe, layer, 1)
                elif group in ("B1", "C1"):
                    exp_done.wait(pe, layer, 2)
                elif group == "X0":
                    exp_done.wait(pe, layer, 4)
                else:
                    sum_done.wait(pe, layer, 4)

            def made(ins):
                ins.then_inc(scores_ready.sem, 1)

            def index_dots(b, layer):
                if b == 1:
                    for name in ("KI", "QI0", "QI1"):
                        taken(name, layer)
                    sum_done.wait(pe, layer, 0)
                for h in range(H_IDX):
                    r = slice(64 * (h % 2), 64 * (h % 2) + 64)
                    last = mm(DOTS[b][:, place(h, H_IDX), :], QK[r, M_QI + h // 2, b * P:(b + 1) * P],
                              QK[r, M_KI, 0:NKEYS[b]], start=True, stop=True)
                last.then_inc(dots_ready.sem, 1)

            def scores_a(b, layer):
                group = f"A{b}"
                if b == 0:
                    taken("KA0", layer)
                    taken("KA1", layer)
                group_free(group, layer)
                n = NKEYS[b]
                for i in range(2 * H_A):
                    h, m = i // 2, i % 2
                    r = slice(64 * m, 64 * m + 64)
                    S = score(group, m * H_A + h)
                    mm(S, QK[r, M_QA + h, b * P:(b + 1) * P], QK[r, M_KA + h, 0:n],
                       start=True, stop=False)
                    last = mm(S, slopeI[:, 2 * h, :], dist[:, 2 * P - n:], start=False, stop=True)
                made(last)

            def scores_b(b, layer):
                group = f"B{b}"
                if b == 0:
                    hankel_loaded.wait(pe, layer, 1)
                    taken("KB", layer)
                group_free(group, layer)
                n = NKEYS[b]
                for h in range(H_B):
                    S = score(group, place(h, H_B))
                    r = slice(64 * (h % 2), 64 * (h % 2) + 64)
                    mm(S, QK[r, M_QB + h // 2, b * P:(b + 1) * P], QK[r, M_KB + h // 2, 0:n],
                       start=True, stop=False)
                    for k in range(b + 1):
                        mm(S[:, k * P:(k + 1) * P], HK[:, b - k, h, :], flip8[:], start=False, stop=False)
                    last = mm(S[:, b * P:n], idenb[:], maskB[:], start=False, stop=True)
                made(last)

            def scores_c(b, layer):
                group = f"C{b}"
                group_free(group, layer)
                selected.wait(pe, layer, b + 1)
                if b == 0:
                    taken("KC", layer)
                n = NKEYS[b]
                chosen_keys = selb[:, 0:P] if b == 0 else selb[:, P:3 * P]
                for h in range(H_C):
                    S = score(group, place(h, H_C))
                    r = slice(64 * (h % 2), 64 * (h % 2) + 64)
                    mm(S, QK[r, M_QC + h // 2, b * P:(b + 1) * P], QK[r, M_KC + h // 2, 0:n],
                       start=True, stop=False)
                    mm(S, slopeI[:, 2 * h + 1, :], dist[:, 2 * P - n:], start=False, stop=False)
                    last = mm(S, idenb[:], chosen_keys, start=False, stop=True)
                made(last)

            def scores_x(b, layer):
                if b == 0:
                    for name in ("QX2", "QX3", "KX3"):
                        taken(name, layer)
                group_free(f"X{b}", layer)
                for h in range(H_X):
                    for c in range(2):
                        last = mm(score(f"X{b}", h), QK[:, 2 * h + c, b * P:(b + 1) * P], KX[:, 2 * h + c, :],
                                  start=(c == 0), stop=(c == 1))
                made(last)

            def turn_probs(name, group, k, layer):
                if group[0] == "A":
                    probs_ready.wait(pe, layer, 1 + int(group[1]))
                elif group[0] == "X":
                    probs_ready.wait(pe, layer, 3 + int(group[1]))
                else:
                    exp_done.wait(pe, layer, 4 if group[1] == "0" else 6)
                bank = begin(name, layer)
                for h in range(4):
                    i = place(h, 4) if group[0] in "BC" else h
                    src = EV[group][:, i, k * P:(k + 1) * P]
                    last = turn(bank[:, h * P:(h + 1) * P], src)
                ready(last)

            def values_a(b, layer):
                bank = begin(f"OA{b}", layer)
                halves = ["TA0"] if b == 0 else ["TA1", "TA2"]
                for name in ["VA0", "VA1"] + halves:
                    taken(name, layer)
                for h in range(H_A):
                    for k, part in enumerate(halves):
                        last = mm(bank[:, h * P:(h + 1) * P], PTV[part][:, h, :], VN[:, k, h * P:(h + 1) * P],
                                  start=(k == 0), stop=(k == len(halves) - 1))
                ready(last)

            def values_bc(b, layer):
                bank = begin(f"OBC{b}", layer)
                for name in ["VC"] + (["TB0", "TC0"] if b == 0 else ["TB1", "TB2", "TC1", "TC2"]):
                    taken(name, layer)
                for g, off in (("B", 512), ("C", 768)):
                    halves = [f"T{g}0"] if b == 0 else [f"T{g}1", f"T{g}2"]
                    for h in range(4):
                        c = off - 512 + h * 64
                        for k, part in enumerate(halves):
                            last = mm(bank[:, c:c + 64], PTV[part][:, h, :],
                                      VN[:, k, off + h * 64:off + (h + 1) * 64],
                                      start=(k == 0), stop=(k == len(halves) - 1))
                ready(last)

            def values_x(h, layer):
                if h == 0:
                    for name in ("TX2", "TX3", "VX2", "VX3"):
                        taken(name, layer)
                bank = begin(f"OX{h}", layer)
                for c in range(2):
                    for k in range(2):
                        last = mm(bank[:, c * SEQ:(c + 1) * SEQ], VX[:, k, (2 * h + c) * P:(2 * h + c + 1) * P],
                                  PX[:, k, h, :], start=(k == 0), stop=(k == 1))
                ready(last)

            def turn_outputs(name, layer):
                b, off = int(name[2]), 0 if name[1] == "A" else 4
                rows_done.wait(pe, layer, b + 1)
                bank = begin(name, layer)
                for m in range(4):
                    last = turn(bank[:, m * P:(m + 1) * P], N[:, b, (off + m) * P:(off + m + 1) * P])
                ready(last)

            def tile(name, layer):
                kind, i = name[:2], int(name[-1]) if name[-1].isdigit() else 0
                g = FIRST[layer] + PIECE_AT[name] if name in PIECE_AT else None
                if name in ("KI", "QX0"):
                    turned_lo.wait(pe, layer, 4 if name == "KI" else 8)
                if kind in ("HT", "HX", "HF"):
                    if i == 0:
                        norm_done.wait(pe, layer, {"HT": 0, "HX": 2, "HF": 4}[kind])
                    turned_rows(name, layer)
                elif name == "KI":
                    project_small(g, layer)
                elif kind == "KX":
                    project_turned(name, g, YMH, YML, layer)
                elif kind in ("QI", "QA", "KA", "QB", "KB", "QC", "KC", "QX"):
                    project_turned(name, g, XTH, XTL, layer)
                elif kind == "VX":
                    project_rows(name, g, YMH, YML, layer)
                elif kind[0] == "V":
                    project_rows(name, g, XTH, XTL, layer)
                elif kind[0] == "T":
                    if kind == "TX":
                        turn_probs(name, f"X{i // 2}", i % 2, layer)
                    else:
                        turn_probs(name, f"{kind[1]}{min(i, 1)}", max(i - 1, 0), layer)
                elif kind == "OA":
                    values_a(i, layer)
                elif name[:3] == "OBC":
                    values_bc(i, layer)
                elif kind == "OX":
                    values_x(i, layer)
                else:
                    turn_outputs(name, layer)

            def body(layer):
                pe.wait_ge(ffn_hidden, layer * PAIRS)
                for step in PLAN:
                    kind, name = step[0], step[1]
                    if kind == "tile":
                        tile(name, layer)
                    elif kind == "dots":
                        index_dots(name, layer)
                    elif kind == "scores":
                        {"A": scores_a, "B": scores_b, "C": scores_c, "X": scores_x}[name[0]](int(name[1]), layer)
                    elif kind == "acc":
                        accumulate(f"{name}{step[2]}", layer)
                turned_lo.wait(pe, layer, 12)
                sum_done.wait(pe, layer, 8)

            def feed_forward():
                FIRST_FFN = len(PIECES)

                def up(slot, split, bank, signal):
                    pe.wait_ge(lo_done, split)
                    r = slice(slot * PIECE, (slot + 1) * PIECE)
                    WH, WL = by_tiles(SPH[:, r]), by_tiles(SPL[:, r])
                    for m in range(2):
                        c = slice(m * P, (m + 1) * P)
                        for t in range(KT):
                            last = mm3(PS[:, bank, m * SEQ:(m + 1) * SEQ], WH[:, t, c], WL[:, t, c],
                                       XTH[:, t, :], XTL[:, t, :], t == 0, t == KT - 1)
                    last.then_inc(signal, 1)

                def down(slot, split, made_, first=False, final=False):
                    pe.wait_ge(lo_done, split)
                    pe.wait_ge(ffn_lo, made_)
                    r = slice(slot * PIECE, (slot + 1) * PIECE)
                    WH, WL = by_rows(SPH[:, r]), by_rows(SPL[:, r])
                    for f in range(2):
                        for b in range(TB):
                            for half in range(2):
                                c = slice(half * HALF, (half + 1) * HALF)
                                q = slice(b * P, (b + 1) * P)
                                last = mm3(PS[:, 2 * half + b, :], FHH[:, f, q], FHL[:, f, q], WH[:, f, c],
                                           WL[:, f, c], first and f == 0, final and f == 1)
                    last.then_inc(ffn_down, 1)

                g = FIRST_FFN
                up(g % SLOTS, g + 1, 4, ffn_g)
                up((g + 1) % SLOTS, g + 2, 5, ffn_u)
                pe.wait_ge(ffn_silu, 1)
                up((g + 2) % SLOTS, g + 3, 4, ffn_g)
                down((g + 3) % SLOTS, g + 4, 1, first=True)
                pe.wait_ge(ffn_hidden, 1)
                up((g + 4) % SLOTS, g + 5, 5, ffn_u)
                with pe.Fori(2, PAIRS) as p:
                    pe.wait_ge(ffn_silu, p)
                    up((g + 2) % SLOTS, p * 3 + g, 4, ffn_g)
                    down((g + 3) % SLOTS, p * 3 + (g + 1), p)
                    pe.wait_ge(ffn_hidden, p)
                    up((g + 4) % SLOTS, p * 3 + (g + 2), 5, ffn_u)
                g = FIRST[1] - 1
                down(g % SLOTS, g + 1, PAIRS, final=True)

            def mixture():
                pe.wait_ge(router_lo, 1)
                for b in range(TB):
                    r = slice(b * P, (b + 1) * P)
                    for t in range(KT):
                        last = mm3(PS[:, 4, b * 8:b * 8 + 8], XTH[:, t, r], XTL[:, t, r],
                                   routerh[:, t, :], routerl[:, t, :], t == 0, t == KT - 1)
                last.then_inc(router_ready, 1)
                pe.wait_ge(chosen_done, 1)
                mm(PS[:, 5, 0:8], before[:], chosen[:, 0, :], start=True, stop=True)
                mm(PS[:, 5, 8:16], before[:], chosen[:, 1, :], start=True, stop=False)
                mm(PS[:, 5, 8:16], ones[:], chosen[:, 0, :], start=False, stop=True)
                mm(PS[:, 5, 16:24], ones[:], chosen[:, 0, :], start=True, stop=False)
                mm(PS[:, 5, 16:24], ones[:], chosen[:, 1, :], start=False, stop=True).then_inc(rank_ready, 1)
                pe.wait_ge(table_done, 1)
                pe.wait_ge(rows_lo, 1)

                def gather(n, part):
                    rows = HRH if part == 0 else HRL
                    if part == 0:
                        pe.wait_ge(onehot_done, n * 2 + 1)
                    for q, bank in enumerate((2, 4) if part == 0 else (6, 3)):
                        if bank == 2:
                            pe.wait_ge(silu_done["a"], n * STEPS)
                        elif bank == 4:
                            pe.wait_ge(hidden_done["a"], n * STEPS)
                        elif bank == 6:
                            pe.wait_ge(turned_done["a"], n * STEPS)
                        else:
                            pe.wait_ge(silu_done["b"], n * STEPS)
                        for t in range(4):
                            c = slice((4 * q + t) * P, (4 * q + t + 1) * P)
                            for b in range(TB):
                                last = mm(PS[:, bank, t * P:(t + 1) * P], rows[:, b, c], ONE[:, b, :],
                                          start=(b == 0), stop=(b == 1))
                        last.then_inc(gather_ready, 1)

                def item(n, ahead):
                    def up(c, which, k):
                        pe.wait_ge((lo1 if which == 0 else lo3)[c], k + 1)
                        if which == 0:
                            pe.wait_ge(silu_done[c], k)
                        else:
                            pe.wait_ge(hidden_done[c], k)
                        WH, WL = (S1H, S1L) if which == 0 else (S3H, S3L)
                        WH, WL = by_tiles(WH[c]), by_tiles(WL[c])
                        bank = 2 + 2 * which + (c == "b")
                        for t in range(KT):
                            last = mm3(PS[:, bank, 0:FE], XGH[:, t, :], XGL[:, t, :], WH[:, t, :], WL[:, t, :],
                                       t == 0, t == KT - 1)
                        last.then_inc((g_ready if which == 0 else u_ready)[c], 1)

                    def turn_hidden(c, k):
                        pe.wait_ge(hidden_done[c], k + 1)
                        pe.wait_ge(turned_done[c], k)
                        for f in range(2):
                            last = turn(PS[:, 6 + (c == "b"), f * P:(f + 1) * P], HID[c][:, f * P:(f + 1) * P])
                        last.then_inc(turned_ready[c], 1)

                    def down(c, k, first=False, final=False):
                        pe.wait_ge(loaded2[c], (k + 1) * 16)
                        pe.wait_ge(turned_done[c], k + 1)
                        for f in range(2):
                            for half in range(2):
                                last = mm(PS[:, half, :], HIDT[c][:, f * P:(f + 1) * P],
                                          by_rows(R2[c][:])[:, f, half * HALF:(half + 1) * HALF],
                                          start=first and f == 0, stop=final and f == 1)
                        last.then_inc(w2_used[c], 1)

                    k0 = n * STEPS
                    pe.wait_ge(gather_hi, n + 1)
                    pe.wait_ge(gather_lo, n + 1)
                    up("a", 0, k0)
                    up("a", 1, k0)
                    up("b", 0, k0)
                    pe.wait_ge(scatter_done, n * 4)
                    turn_hidden("a", k0)
                    pe.wait_ge(onehot_done, n * 2 + 2)
                    for b in range(TB):
                        last = turn(PS[:, 7, b * P:(b + 1) * P], GATED[:, b, :])
                    last.then_inc(gatedT_ready, 1)
                    up("b", 1, k0)
                    pe.wait_ge(gatedT_done, n + 1)
                    down("a", k0, first=True)
                    with pe.Fori(1, STEPS) as j:
                        k = k0 + j
                        up("a", 0, k)
                        turn_hidden("b", k - 1)
                        up("a", 1, k)
                        down("b", k - 1)
                        up("b", 0, k)
                        turn_hidden("a", k)
                        up("b", 1, k)
                        down("a", k)
                    k = k0 + (STEPS - 1)
                    if ahead:
                        gather(n + 1, 0)
                    turn_hidden("b", k)
                    down("b", k, final=True)
                    if ahead:
                        gather(n + 1, 1)
                    pe.wait_ge(y_act, n + 1)
                    pe.wait_ge(y_dve, n + 1)
                    for i, bank in enumerate((7, 0, 1, 6)):
                        half, b = i // 2, i % 2
                        if bank == 6:
                            if ahead:
                                pe.wait_ge(gather_lo, n + 2)
                        mm(PS[:, bank, :], GATEDT[:, b * P:(b + 1) * P],
                           YE[:, half * HALF:(half + 1) * HALF], start=True, stop=True
                           ).then_inc(scatter_ready, 1)

                gather(0, 0)
                gather(0, 1)
                with pe.Fori(0, N_EXPERTS - 1) as e:
                    item(e, True)
                item(N_EXPERTS - 1, False)

                def extra(e, n):
                    gather(n, 0)
                    pe.wait_ge(scatter_done, n * 4)
                    gather(n, 1)
                    item(n, False)

                extra_experts(pe, extra)

            for layer in range(DEPTH):
                body(layer)
                if layer == 0:
                    feed_forward()
                else:
                    mixture()

        def destination(name):
            bank = tile_bank(name)
            kind, i = name[:2], int(name[-1]) if name[-1].isdigit() else 0
            two = bank.rearrange("p (m t) -> p m t", t=SEQ)
            turned = {"QI": M_QI + 2 * i, "QA": M_QA + 2 * i, "KA": M_KA + 2 * i, "QB": M_QB, "KB": M_KB,
                      "QC": M_QC, "KC": M_KC}
            if kind in turned:
                return QK[:, turned[kind]:turned[kind] + 2, :], two
            if name == "VB":
                return VN[:, :, 512:768], two
            if name == "VC":
                return VN[:, :, 768:1024], two
            if kind == "VA":
                return VN[:, :, 256 * i:256 * (i + 1)], two
            if kind == "KX":
                return KX[:, 2 * i:2 * i + 2, :], two
            if kind == "QX":
                return QK[:, 2 * i:2 * i + 2, :], two
            if kind == "VX":
                return VX[:, :, 256 * i:256 * (i + 1)], two
            if kind == "TX":
                return PX[:, i % 2, :, i // 2 * P:(i // 2 + 1) * P], heads(bank)
            return PTV[name], heads(bank)

        def column(tile, row, layer, t):
            return tile[:].rearrange("p r t -> p (r t)")[:, bass.ds(layer * KT + (row * KT + t), 1)]

        NORM_ROW = {"HT": 0, "HX": 2, "HF": 4}

        def split_places(name):
            bank, kind, i = tile_bank(name), name[:2], int(name[2])
            if kind == "OX":
                return XTH[:, 2 * i:2 * i + 2, :], XTL[:, 2 * i:2 * i + 2, :], bank.rearrange("p (m t) -> p m t", t=SEQ)
            m = slice(0, 4) if kind == "YA" else slice(4, 8)
            q = slice(i * P, (i + 1) * P)
            return XTH[:, m, q], XTL[:, m, q], heads(bank)

        def turned_places(name):
            k = int(name[2])
            return [t[:, 2 * k:2 * k + 2, :].rearrange("p m t -> p (m t)") for t in (XTH, XTL)]

        def small_places(ring, g):
            w = cut(ring, g)[:, 0:KT * (P + 8)].rearrange("p (t n) -> p t n", t=KT)
            return w[:, :, 0:D_IDX], w[:, :, D_IDX:P + 8]

        def small_raw(g):
            w = cut(RAW, g)[:, 0:KT * SMALL].rearrange("p (t n) -> p t n", t=KT)
            return w[:, :, 0:D_IDX], w

        @block.scalar
        def _(act):
            a = nc.scalar

            def high(dst, src):
                return a.activation(dst, src, ACT.Copy)

            def split(g):
                act.wait_ge(raw_loaded[g % SLOTS], 16 * (g // SLOTS + 1))
                if g >= SLOTS:
                    used(act, g - SLOTS)
                if is_small(g):
                    for dst, src in zip(small_places(SPH, g), small_raw(g)):
                        last = high(dst, src)
                else:
                    last = high(cut(SPH, g), cut(RAW, g))
                last.then_inc(hi_done, 1)

            act.wait_ge(mem_ready, 1)
            for i in range(KT // 2):
                last = high(YMH[:, 2 * i:2 * i + 2, :].rearrange("p m t -> p (m t)"), PS[:, 1 + i, :])
            last.then_inc(mem_hi, 1)
            act.wait_ge(lam_ready, 1)
            a.activation(lam_work[:, 2 * DEPTH:4 * DEPTH], lam_work[:, 0:2 * DEPTH], ACT.Exp).then_inc(lam_exp, 1)
            for g in range(SLOTS):
                split(g)
            act.wait_ge(s_router, 16)
            high(routerh[:], router[:]).then_inc(router_hi, 1)
            act.wait_ge(columns_done, 3)
            act.wait_ge(dist_done, 1)
            act.wait_ge(s_table_out, 16)

            def turned(kind, layer):
                def affine(k):
                    name = f"{kind}{k}"
                    tile_ready.wait(act, layer, TILE_AT[name] + 1)
                    for t in range(2):
                        last = a.activation(TURN[k][:, t * SEQ:(t + 1) * SEQ],
                                            tile_bank(name)[:, t * SEQ:(t + 1) * SEQ],
                                            ACT.Identity, bias=column(LB, NORM_ROW[kind], layer, 2 * k + t),
                                            scale=column(LG, NORM_ROW[kind], layer, 2 * k + t))
                    last.then_inc(tile_taken["a"].sem, 1)

                def split_rows(k):
                    name = f"{kind}{k}"
                    who = LAST[name]
                    tile_taken[who].wait(act, layer, TAKEN[who].index(name) + 1)
                    high(turned_places(name)[0], TURN[k]).then_inc(part_hi.sem, 1)

                affine(0)
                split_rows(0)
                affine(2)
                split_rows(1)
                split_rows(2)
                split_rows(3)

            def take(name, layer):
                if name == "TA2":
                    selected.wait(act, layer, 2)
                tile_ready.wait(act, layer, TILE_AT[name] + 1)
                dst, src = destination(name)
                a.activation(dst, src, ACT.Copy).then_inc(tile_taken["a"].sem, 1)

            def take_high(name, layer):
                tile_ready.wait(act, layer, TILE_AT[name] + 1)
                dst, _, src = split_places(name)
                if name[:2] == "YA":
                    last = a.activation(dst, src, ACT.Copy, scale=gain[:, bass.ds(layer, 1)])
                else:
                    last = a.activation(dst, src, ACT.Copy)
                last.then_inc(part_hi.sem, 1)

            def exps(group, layer):
                i = GROUPS.index(group)
                max_done.wait(act, layer, max(through(group), i + 1))
                for m in range(maps_of(group)):
                    last = a.activation(EV[group][:, m, :], score(group, m), ACT.Exp, bias=nmx[:, i, m:m + 1],
                                        scale=SCALE_X if group[0] == "X" else SCALE,
                                        accum_out=sums[:, i, m:m + 1])
                last.then_inc(exp_done.sem, 1)

            def body(layer):
                for step in PLAN:
                    kind, name = step[0], step[1]
                    piece = None
                    if kind == "tile":
                        piece = name
                        if name[:2] in NORM_ROW:
                            if name[2] == "0":
                                turned(name[:2], layer)
                        elif step[2] == "a":
                            take(name, layer)
                        elif step[2] == "s":
                            take_high(name, layer)
                    elif kind == "dots":
                        dots_ready.wait(act, layer, 2 - name)
                        a.activation(DOT[name], DOTS[name], ACT.Relu).then_inc(relu_done.sem, 1)
                    elif kind == "exp":
                        exps(name, layer)
                    elif kind == "acc":
                        piece = f"{name}{step[2]}"
                    if piece in PIECE_AT:
                        g = FIRST[layer] + PIECE_AT[piece] + SLOTS
                        if g < ALL:
                            split(g)

            def feed_forward():
                def split_ring(slot, loads, held, uses):
                    act.wait_ge(raw_loaded[slot], loads)
                    act.wait_ge(held, uses)
                    r = slice(slot * PIECE, (slot + 1) * PIECE)
                    high(SPH[:, r], RAW[:, r]).then_inc(hi_done, 1)

                def silu(p):
                    act.wait_ge(ffn_g, p + 1)
                    act.wait_ge(ffn_hidden, p)
                    a.activation(FSIL, PS[:, 4, :], ACT.Silu).then_inc(ffn_silu, 1)

                def split_hidden(p):
                    act.wait_ge(ffn_hidden, p + 1)
                    act.wait_ge(ffn_down, p)
                    high(FHH[:].rearrange("p f t -> p (f t)"), FHID).then_inc(ffn_hi, 1)

                g = len(PIECES)
                silu(0)
                split(g + 3)
                split_hidden(0)
                split(g + 4)
                assert (g + 2) // SLOTS == (g + 3) // SLOTS == (g + 4) // SLOTS - 1
                first = 16 * ((g + 2) // SLOTS + 1)
                with act.Fori(1, PAIRS - 1) as p:
                    silu(p)
                    split_ring((g + 2) % SLOTS, p * 16 + first, ffn_g, p + 1)
                    split_ring((g + 3) % SLOTS, p * 16 + first, ffn_down, p)
                    split_hidden(p)
                    split_ring((g + 4) % SLOTS, p * 16 + (first + 16), ffn_u, p + 1)
                silu(PAIRS - 1)
                split(FIRST[1] - 1)
                split(FIRST[1])
                split_hidden(PAIRS - 1)
                split(FIRST[1] + 1)
                split(FIRST[1] + 2)

            def mixture():
                act.wait_ge(logit_done, 1)
                a.activation(gw[:, :, 1:2], gw[:, :, 0:1], ACT.Exp).then_inc(exp2_done, 1)
                resid_done.wait(act, 1, 2)
                for b in range(TB):
                    last = high(HRH[:, b, :], H[:, b, :])
                last.then_inc(rows_hi, 1)

                def split1(c, k):
                    act.wait_ge(loaded1[c], (k + 1) * 16)
                    act.wait_ge(g_ready[c], k)
                    high(S1H[c], flat["R1" + c][:]).then_inc(hi1[c], 1)

                def split3(c, k):
                    act.wait_ge(loaded3[c], (k + 1) * 16)
                    act.wait_ge(u_ready[c], k)
                    high(S3H[c], flat["R3" + c][:]).then_inc(hi3[c], 1)

                def gather(n):
                    for q, bank in enumerate((2, 4)):
                        act.wait_ge(gather_ready, n * 4 + q + 1)
                        last = high(XGH[:, 4 * q:4 * q + 4, :], heads(PS[:, bank, :]))
                    last.then_inc(gather_hi, 1)

                def item(n, ahead):
                    def silu(c, k):
                        act.wait_ge(g_ready[c], k + 1)
                        act.wait_ge(hidden_done[c], k)
                        a.activation(SIL[c], PS[:, 2 + (c == "b"), 0:FE], ACT.Silu).then_inc(silu_done[c], 1)

                    def take_turned(c, k):
                        act.wait_ge(turned_ready[c], k + 1)
                        act.wait_ge(w2_used[c], k)
                        a.activation(HIDT[c], PS[:, 6 + (c == "b"), 0:FE], ACT.Copy).then_inc(turned_done[c], 1)

                    k0 = n * STEPS
                    split1("b", k0)
                    silu("a", k0)
                    split3("b", k0)
                    split1("a", k0 + 1)
                    silu("b", k0)
                    take_turned("a", k0)
                    act.wait_ge(gatedT_ready, n + 1)
                    a.activation(GATEDT, PS[:, 7, 0:TB * P], ACT.Copy).then_inc(gatedT_done, 1)
                    split3("a", k0 + 1)

                    def steps(k, more):
                        split1("b", k)
                        silu("a", k)
                        take_turned("b", k - 1)
                        split3("b", k)
                        if more:
                            split1("a", k + 1)
                        silu("b", k)
                        take_turned("a", k)
                        if more:
                            split3("a", k + 1)

                    with act.Fori(1, STEPS if ahead else STEPS - 1) as j:
                        steps(k0 + j, True)
                    k = k0 + (STEPS - 1)
                    if ahead:
                        gather(n + 1)
                    else:
                        steps(k, False)
                    take_turned("b", k)
                    act.wait_ge(w2_used["b"], k0 + STEPS)
                    a.activation(YE[:, 0:HALF], PS[:, 0, :], ACT.Copy).then_inc(y_act, 1)

                split1("a", 0)
                split3("a", 0)
                gather(0)
                with act.Fori(0, N_EXPERTS - 1) as e:
                    item(e, True)
                item(N_EXPERTS - 1, False)

                def extra(e, n):
                    split1("a", n * STEPS)
                    split3("a", n * STEPS)
                    gather(n)
                    item(n, False)

                extra_experts(act, extra)

            for layer in range(DEPTH):
                body(layer)
                if layer == 0:
                    feed_forward()
                else:
                    mixture()

        @block.vector
        def _(dve):
            v = nc.vector
            o = Order(dve, order_dve)
            dve.wait_ge(s_table, 16)
            dve.wait_ge(pool_done, 1)
            t8 = slice(0, DEPTH * H_B)
            tail = PT[t8, 768:768 + 2 * P]
            v.tensor_copy(tail[:, 0:P], PT[t8, 2 * P + REL_MAX + 1:2 * P + R])
            v.tensor_scalar(tail[:, P:2 * P], maskI[t8, 0:P], PT[t8, 2 * P + R - 1:2 * P + R], None,
                            ALU.add).then_inc(tail_done, 1)
            o.link(v.scalar_tensor_tensor(out=dist[:], in0=isc, scalar=-1.0, in1=isc, op0=ALU.mult,
                                          op1=ALU.max))
            v.memset(dist[0:CHUNK, P + CHUNK:2 * P], FAR).then_inc(dist_done, 1)
            dve.wait_ge(columns_ready, 1)
            v.tensor_copy(LG[:].rearrange("p r t -> p (r t)"), PS[:, 0, 0:6 * KT]).then_inc(columns_done, 1)
            v.tensor_copy(LB[:].rearrange("p r t -> p (r t)"), PS[:, 0, 64:64 + 6 * KT]).then_inc(columns_done, 1)
            for l in range(DEPTH):
                last = v.tensor_scalar(gain[:, l:l + 1], PS[:, 0, 128 + l:129 + l], 1.0 - lam_inits[l], None, ALU.mult)
            last.then_inc(columns_done, 1)
            dve.wait_ge(s_lam, 16 * 4)
            lq = PT[:, 1152:1664].rearrange("p (i l d) -> p i l d", l=DEPTH, d=DQK_A)
            lsum = lam_work[:, 0:2 * DEPTH].rearrange("p (i l) -> p i l", l=DEPTH)
            lexp = lam_work[:, 2 * DEPTH:4 * DEPTH].rearrange("p (i l) -> p i l", l=DEPTH)
            for i in range(2):
                o.link(v.tensor_tensor(sq[:, i, :].rearrange("p (l d) -> p l d", l=DEPTH), lq[:, 2 * i],
                                       lq[:, 2 * i + 1], ALU.mult))
                last = v.tensor_reduce(lsum[:, i, :], sq[:, i, :].rearrange("p (l d) -> p l d", l=DEPTH),
                                       AX, ALU.add)
            last.then_inc(lam_ready, 1)
            dve.wait_ge(lam_exp, 1)
            for l in range(DEPTH):
                o.link(v.tensor_tensor(neglam[:, l:l + 1], lexp[:, 1, l:l + 1], lexp[:, 0, l:l + 1], ALU.subtract))
                o.link(v.tensor_scalar(neglam[:, l:l + 1], neglam[:, l:l + 1], -lam_inits[l], None, ALU.add))
            def low(dst, src, hi):
                return v.tensor_tensor(dst, src, hi, ALU.subtract)

            def split(g):
                dve.wait_ge(hi_done, g + 1)
                if is_small(g):
                    for dst, src, hi in zip(small_places(SPL, g), small_raw(g), small_places(SPH, g)):
                        last = low(dst, src, hi)
                else:
                    last = low(cut(SPL, g), cut(RAW, g), cut(SPH, g))
                last.then_inc(lo_done, 1)

            dve.wait_ge(mem_hi, 1)
            for i in range(KT // 2):
                m = slice(2 * i, 2 * i + 2)
                last = low(YML[:, m, :].rearrange("p m t -> p (m t)"), PS[:, 1 + i, :],
                           YMH[:, m, :].rearrange("p m t -> p (m t)"))
            last.then_inc(mem_done, 1)
            for g in range(SLOTS):
                split(g)
            dve.wait_ge(router_hi, 1)
            low(routerl[:], router[:], routerh[:]).then_inc(router_lo, 1)
            dve.wait_ge(s_x, 16 * TB)
            for b in range(TB):
                o.link(v.tensor_copy(H[:, b, :], N[:, b, :]))
            setup_links = o.n

            def turned(kind, layer):
                def affine(k):
                    name = f"{kind}{k}"
                    tile_ready.wait(dve, layer, TILE_AT[name] + 1)
                    for t in range(2):
                        last = v.tensor_scalar(TURN[k][:, t * SEQ:(t + 1) * SEQ],
                                               tile_bank(name)[:, t * SEQ:(t + 1) * SEQ],
                                               column(LG, NORM_ROW[kind], layer, 2 * k + t),
                                               column(LB, NORM_ROW[kind], layer, 2 * k + t), ALU.mult, ALU.add)
                    last.then_inc(tile_taken["v"].sem, 1)

                def split_rows(k):
                    name = f"{kind}{k}"
                    part_hi.wait(dve, layer, PARTED.index(name) + 1)
                    hi, lo = turned_places(name)
                    low(lo, TURN[k], hi).then_inc(turned_lo.sem, 1)

                affine(1)
                split_rows(0)
                affine(3)
                split_rows(1)
                split_rows(2)
                split_rows(3)

            def take(name, layer):
                tile_ready.wait(dve, layer, TILE_AT[name] + 1)
                bank = tile_bank(name)
                if name == "KI":
                    v.tensor_copy(QK[:, M_KI, :], bank[:, 0:SEQ])
                    last = v.tensor_scalar(WI[:].rearrange("p b h -> p (b h)"), bank[:, SEQ:SEQ + TB * H_IDX],
                                           float(H_IDX ** -0.5 * D_IDX ** -0.5), None, ALU.mult)
                else:
                    dst, src = destination(name)
                    last = v.tensor_copy(dst, src)
                last.then_inc(tile_taken["v"].sem, 1)

            def take_low(name, layer):
                part_hi.wait(dve, layer, PARTED.index(name) + 1)
                hi, lo, src = split_places(name)
                if name[:2] == "YA":
                    last = v.scalar_tensor_tensor(out=lo, in0=src, scalar=gain[:, bass.ds(layer, 1)], in1=hi,
                                                  op0=ALU.mult, op1=ALU.subtract)
                else:
                    last = low(lo, src, hi)
                last.then_inc(tile_taken["v"].sem, 1)

            def select(b, part, layer):
                n = NKEYS[b]
                score, rest = isc[:, 0:n], work[:, 0:n]
                if part == 0:
                    relu_done.wait(dve, layer, 2 - b)
                    tile_taken["v"].wait(dve, layer, TAKEN["v"].index("KI") + 1)
                    selected.wait(dve, layer, b)
                    for h in range(H_IDX):
                        o.link(v.scalar_tensor_tensor(out=score, in0=DOT[b][:, place(h, H_IDX), :],
                                                      scalar=WI[:, b, h:h + 1],
                                                      in1=maskI[:, 2 * P - n:] if h == 0 else score,
                                                      op0=ALU.mult, op1=ALU.add))
                    return
                rounds = TOPK // 16
                for i in range((part - 1) * rounds, part * rounds):
                    o.link(v.max(top8[:], score if i == 0 else rest))
                    o.link(v.match_replace(rest, top8[:], score if i == 0 else rest, GONE))
                if part == 1:
                    return
                o.link(v.tensor_scalar(rest, rest, 0.5 * GONE, -FAR, ALU.is_gt, ALU.mult))
                o.link(v.tensor_scalar(score, score, 0.5 * NEG_INF, -FAR, ALU.is_le, ALU.mult))
                keys = selb[:, 0:P] if b == 0 else selb[:, P:3 * P]
                v.tensor_tensor(keys, rest, score, ALU.min).then_inc(selected.sem, 1)

            def maxima(group, layer):
                i = GROUPS.index(group)
                scores_ready.wait(dve, layer, max(through(group), i + 1))
                n = maps_of(group)
                o.link(v.tensor_reduce(mx[:, i, 0:n].rearrange("p (a m) -> p a m", a=2), scores(group), AX,
                                       ALU.max))
                v.tensor_scalar(nmx[:, i, 0:n], mx[:, i, 0:n], -(SCALE_X if group[0] == "X" else SCALE), None,
                                ALU.mult).then_inc(max_done.sem, 1)

            def inverse_sums(group, layer):
                i = GROUPS.index(group)
                exp_done.wait(dve, layer, i + 1)
                n = maps_of(group)
                o.link(v.reciprocal(rs[:, i, 0:n], sums[:, i, 0:n]))
                return i

            def mix_maps(b, layer):
                group = f"A{b}"
                i = inverse_sums(group, layer)
                pair = lambda t, m: t[:, i, m * H_A:(m + 1) * H_A]
                o.link(v.scalar_tensor_tensor(out=mix[:], in0=pair(sums, 0), scalar=neglam[:, bass.ds(layer, 1)],
                                              in1=pair(rs, 1), op0=ALU.mult, op1=ALU.mult))
                for h in range(H_A):
                    e0, e1 = EV[group][:, h, :], EV[group][:, H_A + h, :]
                    last = v.scalar_tensor_tensor(out=e0, in0=e1, scalar=mix[:, h:h + 1], in1=e0,
                                                  op0=ALU.mult, op1=ALU.add)
                last.then_inc(probs_ready.sem, 1)

            def rows_a(b, layer):
                name = f"OA{b}"
                tile_ready.wait(dve, layer, TILE_AT[name] + 1)
                i = GROUPS.index(f"A{b}")
                rows = N[:, b, 0:512].rearrange("p (h d) -> p h d", h=H_A)
                r0 = rs[:, i, 0:H_A].rearrange("p (h u) -> p h u", u=1).to_broadcast([P, H_A, DV_A])
                v.tensor_tensor(rows, heads(tile_bank(name)), r0, ALU.mult).then_inc(tile_taken["v"].sem, 1)
                taken = TAKEN["v"].index(name) + 1
                tile_taken["v"].wait(dve, layer, taken)
                o.link(v.tensor_tensor(sq, rows, rows, ALU.mult))
                o.link(v.tensor_reduce(ss[:], sq, AX, ALU.add))
                v.tensor_scalar(ss[:], ss[:], 1.0 / DV_A, RMS_EPS, ALU.mult, ALU.add).then_inc(var_ready.sem, 1)
                rstd_ready.wait(dve, layer, 1 + b)
                o.link(v.tensor_tensor(rows, rows, rms[:].rearrange("p (h u) -> p h u", u=1)
                                       .to_broadcast([P, H_A, DV_A]), ALU.mult))

            def rows_bc(b, layer):
                name = f"OBC{b}"
                for g in "BC":
                    inverse_sums(f"{g}{b}", layer)
                tile_ready.wait(dve, layer, TILE_AT[name] + 1)
                for g, c in (("B", 0), ("C", 256)):
                    i = GROUPS.index(f"{g}{b}")
                    r = rs[:, i, 0:4].rearrange("p (a c u) -> p c a u", a=2, u=1).to_broadcast([P, 2, 2, 64])
                    cut = lambda t: t.rearrange("p (c a d) -> p c a d", c=2, a=2)
                    last = v.tensor_tensor(cut(N[:, b, 512 + c:768 + c]), cut(tile_bank(name)[:, c:c + 256]), r,
                                           ALU.mult)
                    if g == "B":
                        o.link(last)
                last.then_inc(tile_taken["v"].sem, 1)
                tile_taken["v"].wait(dve, layer, TAKEN["v"].index(name) + 1)

            def statistics(o, z, b, layer):
                for half in range(2):
                    o.link(v.bn_stats(st[:, b, half, :], z[:, b, half * HALF:(half + 1) * HALF]))
                o.link(v.bn_aggr(mv[:, b, :], st[:, b].rearrange("p c s -> p (c s)")))
                v.tensor_scalar(var[:, b:b + 1], mv[:, b, 1:2], LN_EPS, None, ALU.add).then_inc(var_ready.sem, 1)

            def normalise(z, b, which, layer):
                rstd_ready.wait(dve, layer, 3 + 2 * which + b)
                v.tensor_scalar(N[:, b, :], z[:, b, :], mv[:, b, 0:1], rstd[:, b:b + 1], ALU.subtract, ALU.mult
                                ).then_inc(norm_done.sem, 1)

            def residual_sum(half, b, first, layer):
                z = H[:, b, half * HALF:(half + 1) * HALF]
                v.scalar_tensor_tensor(out=z, in0=z, scalar=ALPHA, in1=PS[:, 2 * half + b, :], op0=ALU.mult,
                                       op1=ALU.add).then_inc(sum_done.sem, 1)

            def residual_rows(o, which, layer):
                norm_done.wait(dve, layer, 2 * which + 2)
                gb_loaded.wait(dve, layer, which + 1)
                for b in range(TB):
                    o.link(v.tensor_tensor(H[:, b, :], N[:, b, :], GB[:, 0, :], ALU.mult))
                o.link(v.tensor_tensor(H[:, 0, :], H[:, 0, :], GB[:, 1, :], ALU.add))
                v.tensor_tensor(H[:, 1, :], H[:, 1, :], GB[:, 1, :], ALU.add).then_inc(resid_done.sem, 1)
                resid_done.wait(dve, layer, which + 1)

            def sublayer_sums(which, layer):
                for half in range(2):
                    for b in range(TB):
                        acc_ready.wait(dve, layer, 8 * which + 4 * half + 2 + b + 1)
                        residual_sum(half, b, 4 * which, layer)

            def sublayer_norm(which, layer):
                sum_done.wait(dve, layer, 4 * which + 4)
                for b in range(TB):
                    statistics(o, H, b, layer)
                for b in range(TB):
                    normalise(H, b, which, layer)

            def normalise_probs(b, layer):
                group = f"X{b}"
                i = inverse_sums(group, layer)
                r = rs[:, i, 0:4].rearrange("p (h u) -> p h u", u=1).to_broadcast([P, 4, N_MEM])
                v.tensor_tensor(EV[group], EV[group], r, ALU.mult).then_inc(probs_ready.sem, 1)

            def body(layer):
                for step in PLAN:
                    kind, name = step[0], step[1]
                    piece = None
                    if kind == "tile":
                        piece = name
                        if name[:2] in NORM_ROW:
                            if name[2] == "0":
                                turned(name[:2], layer)
                        elif name[:2] == "OA":
                            rows_a(int(name[2]), layer)
                        elif name[:3] == "OBC":
                            rows_bc(int(name[3]), layer)
                            dve.sem_inc(rows_done.sem, 1)
                        elif step[2] == "v":
                            take(name, layer)
                        elif step[2] == "s":
                            take_low(name, layer)
                    elif kind == "select":
                        select(name, step[2], layer)
                    elif kind == "max":
                        maxima(name, layer)
                    elif kind == "mix":
                        mix_maps(name, layer)
                    elif kind == "over":
                        normalise_probs(name, layer)
                    elif kind == "sums":
                        sublayer_sums(name, layer)
                    elif kind == "norm":
                        sublayer_norm(name, layer)
                    elif kind == "residual":
                        residual_rows(o, name, layer)
                    elif kind == "acc":
                        piece = f"{name}{step[2]}"
                    if piece in PIECE_AT:
                        g = FIRST[layer] + PIECE_AT[piece] + SLOTS
                        if g < ALL:
                            split(g)

            def feed_forward(layer):
                o = Order(dve, order_ffn)

                def split_ring(slot, made_):
                    dve.wait_ge(hi_done, made_)
                    r = slice(slot * PIECE, (slot + 1) * PIECE)
                    low(SPL[:, r], RAW[:, r], SPH[:, r]).then_inc(lo_done, 1)

                def hidden(p):
                    dve.wait_ge(ffn_silu, p + 1)
                    dve.wait_ge(ffn_u, p + 1)
                    dve.wait_ge(ffn_lo, p)
                    v.tensor_tensor(FHID, FSIL, PS[:, 5, :], ALU.mult).then_inc(ffn_hidden, 1)
                    dve.wait_ge(ffn_hi, p + 1)
                    low(FHL[:].rearrange("p f t -> p (f t)"), FHID, FHH[:].rearrange("p f t -> p (f t)")
                        ).then_inc(ffn_lo, 1)

                g = len(PIECES)
                split(g + 3)
                hidden(0)
                split(g + 4)
                with dve.Fori(1, PAIRS - 1) as p:
                    split_ring((g + 2) % SLOTS, p * 3 + (g + 3))
                    split_ring((g + 3) % SLOTS, p * 3 + (g + 4))
                    hidden(p)
                    split_ring((g + 4) % SLOTS, p * 3 + (g + 5))
                split(FIRST[1] - 1)
                split(FIRST[1])
                hidden(PAIRS - 1)
                split(FIRST[1] + 1)
                dve.wait_ge(ffn_down, PAIRS)
                for half in range(2):
                    for b in range(TB):
                        residual_sum(half, b, 8, layer)
                sum_done.wait(dve, layer, 12)
                for b in range(TB):
                    statistics(o, H, b, layer)
                for b in range(TB):
                    normalise(H, b, 2, layer)
                split(FIRST[1] + 2)
                residual_rows(o, 2, layer)

            def mixture(layer):
                o = Order(dve, order_moe)
                EIGHT = slice(0, N_EXPERTS)
                o.link(v.memset(logit[:], FILL))
                o.link(v.memset(take1[:], FILL))
                o.link(v.memset(take2[:], FILL))
                dve.wait_ge(router_ready, 1)
                o.link(v.tensor_copy(logit[:, :, EIGHT], PS[:, 4, 0:16].rearrange("p (b e) -> p b e", b=TB)))
                for b in range(TB):
                    o.link(v.max(best[:, b, :], logit[:, b, EIGHT]))
                v.tensor_tensor(gw[:, :, 0:1], best[:, :, 1:2], best[:, :, 0:1], ALU.subtract
                                ).then_inc(logit_done, 1)
                o.link(v.tensor_copy(take1[:, :, 0:1], best[:, :, 0:1]))
                o.link(v.tensor_copy(take2[:, :, 0:2], best[:, :, 0:2]))
                for b in range(TB):
                    o.link(v.match_replace(left1[:, b, :], take1[:, b, :], logit[:, b, :], GONE))
                    o.link(v.match_replace(left2[:, b, :], take2[:, b, :], logit[:, b, :], GONE))
                o.link(v.tensor_scalar(gtmp[:], left1[:, :, EIGHT], 0.5 * GONE, None, ALU.is_le))
                v.tensor_scalar(chosen[:], left2[:, :, EIGHT], 0.5 * GONE, None, ALU.is_le).then_inc(chosen_done, 1)
                dve.wait_ge(exp2_done, 1)
                dve.wait_ge(chosen_done, 1)
                o.link(v.tensor_scalar(gw[:, :, 2:3], gw[:, :, 1:2], 1.0, None, ALU.add))
                o.link(v.reciprocal(gw[:, :, 2:3], gw[:, :, 2:3]))
                o.link(v.tensor_tensor(gw[:, :, 3:4], gw[:, :, 1:2], gw[:, :, 2:3], ALU.mult))
                for b in range(TB):
                    o.link(v.tensor_tensor(gate[:, b, :], chosen[:, b, :], gtmp[:, b, :], ALU.subtract))
                    o.link(v.tensor_scalar(gtmp[:, b, :], gtmp[:, b, :], gw[:, b, 2:3], None, ALU.mult))
                    o.link(v.scalar_tensor_tensor(out=gate[:, b, :], in0=gate[:, b, :], scalar=gw[:, b, 3:4],
                                                  in1=gtmp[:, b, :], op0=ALU.mult, op1=ALU.add))
                dve.wait_ge(rank_ready, 1)
                o.link(v.tensor_copy(rank[:].rearrange("p b e -> p (b e)"), PS[:, 5, 0:16]))
                o.link(v.tensor_scalar(ctmp[:], PS[0:1, 5, 16:24], float(P), None, ALU.is_gt))
                o.link(v.tensor_reduce(full[:, 3:4], ctmp[:], AX, ALU.add))
                o.link(v.tensor_scalar(ctmp[:], ctmp[:], -64.0, 64.0, ALU.mult, ALU.add))
                o.link(v.tensor_tensor(cand[:], ctmp[:], iota_s[0:1, EIGHT], ALU.add))
                for j in range(EXTRA):
                    o.link(v.tensor_reduce(full[:, j:j + 1], cand[:], AX, ALU.min))
                    o.link(v.tensor_scalar(ctmp[:], cand[:], full[:, j:j + 1], 64.0, ALU.is_equal, ALU.mult))
                    o.link(v.tensor_tensor(cand[:], cand[:], ctmp[:], ALU.add))
                o.link(v.tensor_scalar(full[:, 0:EXTRA], full[:, 0:EXTRA], float(N_EXPERTS - 1), None, ALU.min))
                v.tensor_copy(fulli[:], full[:]).then_inc(table_done, 1)
                norm_done.wait(dve, DEPTH - 1, 4)
                for b in range(TB):
                    o.link(v.tensor_scalar(N[:, b, :], H[:, b, :], ALPHA, None, ALU.mult))

                dve.wait_ge(rows_hi, 1)
                for b in range(TB):
                    last = low(HRL[:, b, :], H[:, b, :], HRH[:, b, :])
                last.then_inc(rows_lo, 1)

                def split1(c, k):
                    dve.wait_ge(hi1[c], k + 1)
                    low(S1L[c], flat["R1" + c][:], S1H[c]).then_inc(lo1[c], 1)

                def split3(c, k):
                    dve.wait_ge(hi3[c], k + 1)
                    low(S3L[c], flat["R3" + c][:], S3H[c]).then_inc(lo3[c], 1)

                def onehots(e, n, base):
                    dve.wait_ge(gather_ready, n * 4)
                    dve.wait_ge(gatedT_ready, n)
                    for table, rows in ((chosen, ONE), (gate, GATED)):
                        for b in range(TB):
                            pick = lambda t: t[:].rearrange("p b e -> p (b e)")[:, bass.ds(e + b * N_EXPERTS, 1)]
                            last = v.tensor_scalar(rows[:, b, :], iota_s[:, base:base + P], pick(rank), pick(table),
                                                   ALU.is_equal, ALU.mult)
                        last.then_inc(onehot_done, 1)

                def gather(n):
                    for q, bank in enumerate((6, 3)):
                        dve.wait_ge(gather_ready, n * 4 + 2 + q + 1)
                        last = v.tensor_copy(XGL[:, 4 * q:4 * q + 4, :], heads(PS[:, bank, :]))
                    last.then_inc(gather_lo, 1)

                def item(e, n, ahead):
                    def hidden(c, k):
                        dve.wait_ge(silu_done[c], k + 1)
                        dve.wait_ge(u_ready[c], k + 1)
                        dve.wait_ge(turned_ready[c], k)
                        v.tensor_tensor(HID[c], SIL[c], PS[:, 4 + (c == "b"), 0:FE], ALU.mult
                                        ).then_inc(hidden_done[c], 1)

                    def steps(k, more):
                        split1("b", k)
                        split3("b", k)
                        hidden("a", k)
                        if more:
                            split1("a", k + 1)
                            split3("a", k + 1)
                        hidden("b", k)

                    k0 = n * STEPS
                    steps(k0, True)
                    if ahead:
                        onehots(e + 1, n + 1, 0)
                    with dve.Fori(1, STEPS if ahead else STEPS - 1) as j:
                        steps(k0 + j, True)
                    if not ahead:
                        steps(k0 + (STEPS - 1), False)
                    dve.wait_ge(w2_used["b"], k0 + STEPS)
                    v.tensor_copy(YE[:, HALF:D], PS[:, 1, :]).then_inc(y_dve, 1)
                    if ahead:
                        gather(n + 1)
                    for i, bank in enumerate((7, 0, 1, 6)):
                        half, b = i // 2, i % 2
                        z = N[:, b, half * HALF:(half + 1) * HALF]
                        dve.wait_ge(scatter_ready, n * 4 + (i + 1))
                        v.tensor_tensor(z, z, PS[:, bank, :], ALU.add).then_inc(scatter_done, 1)
                    dve.wait_ge(scatter_done, n * 4 + 4)

                onehots(0, 0, 0)
                split1("a", 0)
                split3("a", 0)
                gather(0)
                with dve.Fori(0, N_EXPERTS - 1) as e:
                    item(e, e, True)
                item(N_EXPERTS - 1, N_EXPERTS - 1, False)

                def extra(e, n):
                    onehots(e, n, P)
                    split1("a", n * STEPS)
                    split3("a", n * STEPS)
                    gather(n)
                    item(e, n, False)

                extra_experts(dve, extra)
                for b in range(TB):
                    statistics(o, N, b, layer)
                for b in range(TB):
                    normalise(N, b, 2, layer)
                residual_rows(o, 2, layer)

            per_layer = DVE_LINKS
            for layer in range(DEPTH):
                o.base, o.n = layer * per_layer + setup_links, 0
                body(layer)
                assert o.n == per_layer, o.n
                if layer == 0:
                    feed_forward(layer)
                else:
                    mixture(layer)


_INS = ['x', 'mem', 'w_in', 'lam_q1', 'lam_k1', 'lam_q2', 'lam_k2', 'diff_norm_g', 'rel_bias', 'w_out',
        'ln1_g', 'ln1_b', 'xattn_wq', 'xattn_wk', 'xattn_wv', 'xattn_wo', 'ln2_g', 'ln2_b',
        'ffn_w1', 'ffn_w3', 'ffn_w2', 'moe_router', 'moe_w1', 'moe_w3', 'moe_w2', 'ln3_g', 'ln3_b']


def kernel(**inputs):
    import numpy as _np
    import concourse.bacc as _bacc
    from concourse import mybir as _mybir
    from concourse.bass_utils import run_bass_kernel_spmd as _run

    nc = _bacc.Bacc("TRN2", target_bir_lowering=False, num_devices=1)
    arrays, args = {}, []
    for name in _INS:
        a = _np.ascontiguousarray(inputs[name])
        arrays[f"in_{name}_dram"] = a
        args.append(nc.dram_tensor(f"in_{name}_dram", a.shape, _mybir.dt.from_np(a.dtype), kind="ExternalInput").ap())
    out = nc.dram_tensor("out_0_dram", inputs["x"].shape, _mybir.dt.float32, kind="ExternalOutput").ap()
    hybrid_encoder(nc, *args, out)
    r = _run(nc, [arrays], core_ids=[0])
    return r.results[0]["out_0_dram"]
```

```python
import math
from contextlib import ExitStack

import numpy as np

import concourse.bass as bass
from concourse import mybir

P = 128
F32 = mybir.dt.float32
F32R = mybir.dt.float32r
BF16 = mybir.dt.bfloat16
I32 = mybir.dt.int32
ALU = mybir.AluOpType
ACT = mybir.ActivationFunctionType
AX = mybir.AxisListType.X

CHUNK = 64
H_A, DQK_A = 4, 64
DV_A = 2 * DQK_A
H_B, DH_B = 4, 64
H_C, DH_C = 4, 64
H_IDX, D_IDX = 8, 64
H_X = 4
REL_MAX = 128
TOPK = 64
LN_EPS, RMS_EPS = 1e-5, 1e-6
NEG_INF = -1e30
GONE = -3e38
FILL = 3e38
FAR = float(2 ** 100)


class Signal:

    def __init__(self, sem, per_layer, step=1):
        self.sem, self.per_layer, self.step = sem, per_layer, step

    def wait(self, eng, layer, count):
        eng.wait_ge(self.sem, layer * (self.per_layer * self.step) + count * self.step)


def after(eng, sem, count):
    eng.wait_ge(sem, count + 1)


class Order:

    def __init__(self, eng, sem):
        self.eng, self.sem, self.base, self.n = eng, sem, 0, 0

    def link(self, ins):
        self.n += 1
        ins.then_inc(self.sem, 1)
        self.eng.wait_ge(self.sem, self.base + self.n)


PLAN = [
    ("tile", "HT0", "a"), ("tile", "HT1", "v"), ("tile", "HT2", "a"), ("tile", "HT3", "v"),
    ("tile", "KI", "v"), ("tile", "QI0", "a"), ("tile", "QI1", "a"),
    ("dots", 1), ("dots", 0), ("select", 0, 0),
    ("tile", "QA0", "a"), ("select", 0, 1), ("tile", "QA1", "a"), ("select", 0, 2),
    ("tile", "KA0", "a"), ("select", 1, 0), ("tile", "KA1", "a"),
    ("scores", "A0"), ("max", "A0"), ("scores", "A1"), ("max", "A1"), ("exp", "A0"),
    ("tile", "QB", "a"), ("select", 1, 1), ("exp", "A1"),
    ("tile", "KB", "a"), ("mix", 0), ("select", 1, 2), ("tile", "VB", "a"), ("mix", 1),
    ("tile", "QC", "a"), ("tile", "KC", "a"), ("tile", "VC", "a"),
    ("tile", "TA0", "v"),
    ("scores", "B0"), ("scores", "C0"), ("max", "B0"), ("max", "C0"), ("exp", "B0"), ("exp", "C0"),
    ("tile", "VA0", "a"), ("tile", "TA1", "v"), ("tile", "TA2", "a"),
    ("scores", "B1"), ("scores", "C1"), ("max", "B1"), ("max", "C1"), ("exp", "B1"), ("exp", "C1"),
    ("tile", "VA1", "a"), ("tile", "OA0", "v"), ("tile", "OA1", "v"),
    ("tile", "KX0", "a"), ("tile", "TB0", "a"), ("tile", "TC0", "v"),
    ("tile", "KX1", "a"), ("tile", "TB1", "a"), ("tile", "TB2", "v"), ("tile", "TC1", "a"), ("tile", "TC2", "v"),
    ("tile", "OBC0", "v"), ("tile", "OBC1", "v"),
    ("tile", "YA0", "s"), ("tile", "YB0", "s"), ("tile", "YA1", "s"), ("tile", "YB1", "s"),
    ("acc", "WO", 0), ("acc", "WO", 1), ("acc", "WO", 2), ("acc", "WO", 3), ("norm", 0),
    ("tile", "KX2", "a"), ("tile", "KX3", "a"),
    ("tile", "HX0", "a"), ("tile", "HX1", "v"), ("tile", "HX2", "a"), ("tile", "HX3", "v"),
    ("tile", "QX0", "a"), ("tile", "QX1", "a"), ("residual", 0), ("tile", "QX2", "a"), ("tile", "QX3", "a"),
    ("scores", "X0"), ("scores", "X1"), ("max", "X0"), ("max", "X1"), ("exp", "X0"), ("exp", "X1"),
    ("tile", "VX0", "a"), ("over", 0), ("tile", "VX1", "a"), ("over", 1),
    ("tile", "TX0", "a"), ("tile", "TX1", "v"), ("tile", "VX2", "a"), ("tile", "TX2", "a"), ("tile", "TX3", "v"),
    ("tile", "VX3", "a"),
    ("tile", "OX0", "s"), ("tile", "OX1", "s"), ("tile", "OX2", "s"), ("tile", "OX3", "s"),
    ("acc", "WX", 0), ("acc", "WX", 1), ("acc", "WX", 2), ("acc", "WX", 3), ("norm", 1),
    ("tile", "HF0", "a"), ("tile", "HF1", "v"), ("tile", "HF2", "a"), ("tile", "HF3", "v"),
    ("residual", 1),
]
TILES = [(x[1], x[2]) for x in PLAN if x[0] == "tile"]
TILE_AT = {name: i for i, (name, _) in enumerate(TILES)}
LAST = {name: "v" if who == "s" else who for name, who in TILES}
TAKEN = {w: [n for n, _ in TILES if LAST[n] == w] for w in "av"}
PARTED = [n for n, who in TILES if who == "s" or n[:2] in ("HT", "HX", "HF")]

GROUPS = [x[1] for x in PLAN if x[0] == "scores"]

PIECES = [x[1] if x[0] == "tile" else f"{x[1]}{x[2]}" for x in PLAN
          if x[0] == "acc" or x[0] == "tile" and x[1][0] in "QKV"]
PIECE_AT = {name: i for i, name in enumerate(PIECES)}
PIECE = 2048
SLOTS = 3


def through(group):
    return GROUPS.index("C0" if group == "B0" else group) + 1


def hybrid_encoder(nc, x, mem, w_in, lam_q1, lam_k1, lam_q2, lam_k2, diff_norm_g, rel_bias, w_out,
                   ln1_g, ln1_b, xattn_wq, xattn_wk, xattn_wv, xattn_wo, ln2_g, ln2_b,
                   ffn_w1, ffn_w3, ffn_w2, moe_router, moe_w1, moe_w3, moe_w2, ln3_g, ln3_b, out):
    _, SEQ, D = x.shape
    N_MEM = mem.shape[1]
    DEPTH = w_in.shape[0]
    N_IN = w_in.shape[2]
    D_FF = ffn_w1.shape[2]
    N_EXPERTS, D_FF_E = moe_w1.shape[1], moe_w1.shape[3]
    KT = D // P
    TB = SEQ // P
    ALPHA = (2.0 * DEPTH) ** 0.25
    assert (SEQ, N_MEM, D, TB, KT, DEPTH) == (256, 256, 1024, 2, 8, 2)
    HALF = D // 2
    NKEYS = [P, 2 * P]
    SMALL = D_IDX + H_IDX
    SCALE = DQK_A ** -0.5
    assert DQK_A == DH_B == DH_C == D_IDX == 64
    SCALE_X = float((D // H_X) ** -0.5)
    slopes = [2.0 ** (-8.0 * i / (H_A + H_C)) for i in range(1, H_A + H_C + 1)]
    lam_inits = [0.8 - 0.6 * math.exp(-0.3 * l) for l in range(DEPTH)]

    C_QA, C_KA, C_VA = 0, 512, 1024
    C_QB, C_KB, C_VB, C_QC, C_KC, C_VC, C_QI, C_KI = 1536, 1792, 2048, 2304, 2560, 2816, 3072, 3584
    assert C_KI + SMALL == N_IN
    M_QA, M_KA, M_QB, M_KB, M_QC, M_KC, M_QI, M_KI = 0, 4, 8, 10, 12, 14, 12, 16
    M_ALL = 17

    FE = 2 * P
    STEPS = D_FF_E // (2 * FE)
    assert STEPS * 2 * FE == D_FF_E
    PAIRS = D_FF // (2 * P)
    assert PAIRS % 2 == 1 and PAIRS * 2 * P == D_FF
    FIRST = [0, len(PIECES) + 3 * PAIRS]
    ALL = FIRST[1] + len(PIECES)
    EXTRA = (2 * SEQ - 1) // (P + 1)
    assert EXTRA == 3 and TB == 2

    with ExitStack() as ctx:
        def sb(name, shape, dt=F32):
            return ctx.enter_context(nc.sbuf_tensor(name, shape, dt))

        def sem(name):
            return ctx.enter_context(nc.semaphore(name))

        PS = ctx.enter_context(nc.psum_tensor("PS", [P, 8, 512], F32))

        floats = {}
        arena_at = 0
        for name, n in (("RAW", SLOTS * PIECE), ("SPH", SLOTS * PIECE), ("SPL", SLOTS * PIECE),
                        ("QK", M_ALL * SEQ), ("VN", TB * D), ("KX", KT * N_MEM), ("VX", TB * D),
                        ("XTH", KT * SEQ), ("XTL", KT * SEQ), ("YMH", KT * N_MEM), ("YML", KT * N_MEM),
                        ("E", 3072), ("PT", 3072), ("H", TB * D)):
            floats[name] = arena_at
            arena_at += n
        sb("arena", [P, arena_at])
        arena_base = nc.sbuf_base - 4 * arena_at

        def over(name, shape, dt=F32, region=None, at=0):
            return nc.alloc_sbuf_tensor_at(name, shape, dt, offset=arena_base + 4 * (floats[region or name] + at))

        RAW = over("RAW", [P, SLOTS * PIECE])
        SPH = over("SPH", [P, SLOTS * PIECE], F32R)
        SPL = over("SPL", [P, SLOTS * PIECE], F32R)
        QK = over("QK", [P, M_ALL, SEQ])
        H = over("H", [P, TB, D])
        N = sb("N", [P, TB, D])
        VN = over("VN", [P, TB, D])
        KX = over("KX", [P, KT, N_MEM])
        VX = over("VX", [P, TB, D])
        XTH = over("XTH", [P, KT, SEQ], F32R)
        XTL = over("XTL", [P, KT, SEQ], F32R)
        YMH = over("YMH", [P, KT, N_MEM], F32R)
        YML = over("YML", [P, KT, N_MEM], F32R)
        E = over("E", [P, 3072])
        PT = over("PT", [P, 3072])
        WI = sb("WI", [P, TB, H_IDX])
        GB = sb("GB", [P, 2, D])
        HK = sb("HK", [P, 2, H_B, P])
        iden = sb("iden", [P, P])
        flip8 = sb("flip8", [P, P])
        idenb = sb("idenb", [P, P], BF16)
        slopeI = sb("slopeI", [P, H_A + H_C, P], BF16)
        dist = sb("dist", [P, 2 * P], BF16)
        maskB = sb("maskB", [P, P], BF16)
        maskI = sb("maskI", [P, 2 * P])
        selb = sb("selb", [P, 3 * P], BF16)
        LG = sb("LG", [P, 6, KT])
        LB = sb("LB", [P, 6, KT])
        gain = sb("gain", [P, DEPTH])
        neglam = sb("neglam", [P, DEPTH])
        lam_work = sb("lam_work", [P, 4 * DEPTH])
        st = sb("st", [P, TB, 2, 6])
        mv = sb("mv", [P, TB, 2])
        var = sb("var", [P, TB])
        rstd = sb("rstd", [P, TB])
        mhalf = sb("mhalf", [P, 4])
        top8 = sb("top8", [P, 8])
        mx = sb("mx", [P, 8, 8])
        nmx = sb("nmx", [P, 8, 8])
        sums = sb("sums", [P, 8, 8])
        rs = sb("rs", [P, 8, 8])
        mix = sb("mix", [P, 4])
        ss = sb("ss", [P, 4])
        rms = sb("rms", [P, 4])
        isc = PT[:, 2048:2048 + 2 * P]
        work = PT[:, 2304:2304 + 2 * P]
        sq = PT[:, 2560:3072].rearrange("p (h d) -> p h d", h=4)
        stage = over("stage", [P, KT * N_MEM], F32, "KX")
        stage_lam, stage_iota, stage_gain, stage_sq = (stage[:, 0:512], stage[:, 512:768], stage[:, 768:768 + DV_A],
                                                       stage[:, 1024:1280])
        rows_g, rows_b = PT[0:6 * KT, 0:P], PT[0:6 * KT, P:2 * P]
        TURN = [PT[:, 1024 + 512 * k:1536 + 512 * k] for k in range(4)]

        EV = {
            "A0": E[:, 0:1024].rearrange("p (h k) -> p h k", k=P),
            "A1": E[:, 1024:3072].rearrange("p (h k) -> p h k", k=2 * P),
            "B0": E[:, 0:512].rearrange("p (h k) -> p h k", k=P),
            "C0": E[:, 512:1024].rearrange("p (h k) -> p h k", k=P),
            "B1": E[:, 1024:2048].rearrange("p (h k) -> p h k", k=2 * P),
            "C1": E[:, 2048:3072].rearrange("p (h k) -> p h k", k=2 * P),
            "X0": E[:, 0:1024].rearrange("p (h k) -> p h k", k=2 * P),
            "X1": E[:, 1024:2048].rearrange("p (h k) -> p h k", k=2 * P),
        }
        DOT = {1: E[:, 1024:3072].rearrange("p (h k) -> p h k", k=2 * P),
               0: E[:, 0:1024].rearrange("p (h k) -> p h k", k=P)}

        def heads(ap):
            return ap.rearrange("p (h k) -> p h k", k=P)

        PTV = {"TB0": heads(PT[:, 0:512]), "TC0": heads(PT[:, 512:1024]),
               "TA0": heads(PT[:, 1024:1536]), "TA1": heads(PT[:, 1536:2048]), "TA2": heads(PT[:, 2048:2560]),
               "TB1": heads(PT[:, 1024:1536]), "TB2": heads(PT[:, 1536:2048]),
               "TC1": heads(PT[:, 2048:2560]), "TC2": heads(PT[:, 2560:3072])}
        PX = PT[:, 0:2048].rearrange("p (t h q) -> p t h q", t=2, h=H_X)

        def scores(group):
            bank, n, a, b, keys = {"A0": (4, 2, 0, 512, P), "A1": (0, 4, 0, 512, 2 * P),
                                   "B0": (4, 2, 0, 256, P), "C0": (4, 2, 256, 512, P),
                                   "B1": (0, 2, 0, 512, 2 * P), "C1": (2, 2, 0, 512, 2 * P),
                                   "X0": (4, 2, 0, 512, 2 * P), "X1": (0, 2, 0, 512, 2 * P)}[group]
            if n == 2:
                return PS[:, bank:bank + 2, a:b].rearrange("p b (m k) -> p b m k", k=keys)
            return PS[:, bank:bank + 4, :].rearrange("p (a b) (m k) -> p a (b m) k", a=2, k=keys)

        def score(group, i):
            S = scores(group)
            return S[:, i // S.shape[2], i % S.shape[2], :]

        def maps_of(group):
            return 8 if group[0] == "A" else 4

        def place(h, n):
            return (h % 2) * (n // 2) + h // 2

        DOTS = {1: PS[:, 0:4, :].rearrange("p b (m k) -> p (b m) k", k=2 * P),
                0: PS[:, 4:6, :].rearrange("p b (m k) -> p (b m) k", k=P)}

        def tile_bank(name):
            return PS[:, 6 + TILE_AT[name] % 2, :]

        R1 = {"a": VN, "b": KX}
        R3 = {"a": VX, "b": over("R3b", [P, PIECE], F32, "QK", 0)}
        R2 = {"a": over("R2a", [P, PIECE], F32, "QK", PIECE), "b": over("R2b", [P, PIECE], F32, "RAW", 0)}
        flat = {"R1a": over("R1a_flat", [P, PIECE], F32, "VN"), "R1b": over("R1b_flat", [P, PIECE], F32, "KX"),
                "R3a": over("R3a_flat", [P, PIECE], F32, "VX"), "R3b": R3["b"]}
        S1H = {"a": SPH[:, 0:PIECE], "b": SPH[:, PIECE:2 * PIECE]}
        S1L = {"a": SPL[:, 0:PIECE], "b": SPL[:, PIECE:2 * PIECE]}
        S3H = {"a": SPH[:, 2 * PIECE:3 * PIECE], "b": over("S3bh", [P, PIECE], F32R, "E")[:]}
        S3L = {"a": SPL[:, 2 * PIECE:3 * PIECE], "b": over("S3bl", [P, PIECE], F32R, "PT", 1024)[:]}
        S2H = {"a": over("S2ah", [P, PIECE], F32R, "H")[:], "b": over("S2bh", [P, PIECE], F32R, "E", PIECE)[:]}
        S2L = {"a": over("S2al", [P, PIECE], F32R, "QK", PIECE)[:], "b": over("S2bl", [P, PIECE], F32R, "RAW", 0)[:]}
        HRH = over("HRH", [P, TB, D], F32R, "YMH")
        HRL = over("HRL", [P, TB, D], F32R, "YML")
        XGH = over("XGH", [P, KT, P], F32R, "XTH")
        XGL = over("XGL", [P, KT, P], F32R, "XTL")
        ONE = over("ONE", [P, TB, P], F32R, "RAW", PIECE)
        TURNED = over("TURNED", [P, 4, FE], F32R, "RAW", PIECE + TB * P)
        HTH = {"a": TURNED[:, 0, :], "b": TURNED[:, 1, :]}
        HTL = {"a": TURNED[:, 2, :], "b": TURNED[:, 3, :]}
        after_turned = PIECE + TB * P + 4 * FE
        small = over("small", [P, 4 * FE + 4 * P + D], F32, "RAW", after_turned)
        SIL = {"a": small[:, 0:FE], "b": small[:, FE:2 * FE]}
        HID = {"a": small[:, 2 * FE:3 * FE], "b": small[:, 3 * FE:4 * FE]}
        GATED = small[:, 1024:1280].rearrange("p (b s) -> p b s", b=TB)
        GATEDT = small[:, 1280:1536]
        YE = small[:, 1536:2560]
        tables_at = after_turned + 4 * FE + 4 * P + D
        FSIL = E[:, 0:512]
        FHID = E[:, 512:1024]
        FHH = over("FHH", [P, 2, SEQ], F32R, "E", 1024)
        FHL = over("FHL", [P, 2, SEQ], F32R, "E", 1536)
        iota_s = sb("iota_s", [P, 2 * P])
        before = sb("before", [P, P])
        ones = sb("ones", [P, P])
        router = sb("router", [P, KT, N_EXPERTS])
        routerh = sb("routerh", [P, KT, N_EXPERTS], F32R)
        routerl = sb("routerl", [P, KT, N_EXPERTS], F32R)
        logit = over("logit", [P, TB, 16], F32, "RAW", tables_at)
        best = over("best", [P, TB, 8], F32, "RAW", tables_at + 32)
        take1 = over("take1", [P, TB, 8], F32, "RAW", tables_at + 48)
        take2 = over("take2", [P, TB, 8], F32, "RAW", tables_at + 64)
        left1 = over("left1", [P, TB, 16], F32, "RAW", tables_at + 80)
        left2 = over("left2", [P, TB, 16], F32, "RAW", tables_at + 112)
        chosen = sb("chosen", [P, TB, N_EXPERTS])
        gate = sb("gate", [P, TB, N_EXPERTS])
        gtmp = sb("gtmp", [P, TB, N_EXPERTS])
        gw = sb("gw", [P, TB, 4])
        rank = sb("rank", [P, TB, N_EXPERTS])
        cand = sb("cand", [1, N_EXPERTS])
        ctmp = sb("ctmp", [1, N_EXPERTS])
        full = sb("full", [1, 4])
        fulli = sb("fulli", [1, 4], I32)

        s_x = sem("s_x")
        s_mem = sem("s_mem")
        s_rows = sem("s_rows")
        s_lam = sem("s_lam")
        s_table = sem("s_table")
        s_table_out = sem("s_table_out")
        s_router = sem("s_router")
        s_out = sem("s_out")
        out_ready = sem("out_ready")
        pool_done = sem("pool_done")
        iden_ready = sem("iden_ready")
        rows_blank = sem("rows_blank")
        columns_ready = sem("columns_ready")
        columns_done = sem("columns_done")
        mem_ready = sem("mem_ready")
        mem_done = sem("mem_done")
        tail_done = sem("tail_done")
        dist_done = sem("dist_done")
        lam_ready = sem("lam_ready")
        lam_exp = sem("lam_exp")
        order_pool = sem("order_pool")
        order_dve = sem("order_dve")
        order_ffn = sem("order_ffn")
        order_moe = sem("order_moe")

        gb_loaded = Signal(sem("gb_loaded"), 3, 32)
        hankel_loaded = Signal(sem("hankel_loaded"), 1, 32)
        raw_loaded = [sem(f"raw_loaded{s}") for s in range(SLOTS)]
        hi_done = sem("hi_done")
        lo_done = sem("lo_done")
        router_hi = sem("router_hi")
        router_lo = sem("router_lo")
        mem_hi = sem("mem_hi")
        tile_ready = Signal(sem("tile_ready"), len(TILES))
        tile_taken = {"a": Signal(sem("tile_taken_act"), len(TAKEN["a"])),
                      "v": Signal(sem("tile_taken_dve"), len(TAKEN["v"]))}
        part_hi = Signal(sem("part_hi"), len(PARTED))
        turned_lo = Signal(sem("turned_lo"), 12)
        dots_ready = Signal(sem("dots_ready"), 2)
        relu_done = Signal(sem("relu_done"), 2)
        selected = Signal(sem("selected"), 2)
        scores_ready = Signal(sem("scores_ready"), len(GROUPS))
        max_done = Signal(sem("max_done"), len(GROUPS))
        exp_done = Signal(sem("exp_done"), len(GROUPS))
        probs_ready = Signal(sem("probs_ready"), 4)
        rows_done = Signal(sem("rows_done"), 2)
        acc_ready = Signal(sem("acc_ready"), 16)
        sum_done = Signal(sem("sum_done"), 12)
        var_ready = Signal(sem("var_ready"), 8)
        rstd_ready = Signal(sem("rstd_ready"), 8)
        norm_done = Signal(sem("norm_done"), 6)
        resid_done = Signal(sem("resid_done"), 3)

        ffn_g = sem("ffn_g")
        ffn_silu = sem("ffn_silu")
        ffn_u = sem("ffn_u")
        ffn_hidden = sem("ffn_hidden")
        ffn_hi = sem("ffn_hi")
        ffn_lo = sem("ffn_lo")
        ffn_down = sem("ffn_down")
        ffn_first_rows = sem("ffn_first_rows")

        def by_place(name):
            return {c: sem(f"{name}_{c}") for c in "ab"}

        loaded1, loaded3, loaded2 = by_place("loaded1"), by_place("loaded3"), by_place("loaded2")
        hi1, hi3 = by_place("hi1"), by_place("hi3")
        lo1, lo3 = by_place("lo1"), by_place("lo3")
        g_ready, u_ready = by_place("g_ready"), by_place("u_ready")
        silu_done, hidden_done = by_place("silu_done"), by_place("hidden_done")
        hi2, lo2 = by_place("hi2"), by_place("lo2")
        turned_ready, turned_hi, turned_done = by_place("turned_ready"), by_place("turned_hi"), by_place("turned_done")
        w2_used = by_place("w2_used")
        router_ready = sem("router_ready")
        logit_done = sem("logit_done")
        exp2_done = sem("exp2_done")
        chosen_done = sem("chosen_done")
        rank_ready = sem("rank_ready")
        table_done = sem("table_done")
        rows_hi = sem("rows_hi")
        rows_lo = sem("rows_lo")
        total_begun = sem("total_begun")
        onehot_done = sem("onehot_done")
        gather_ready = sem("gather_ready")
        gather_hi = sem("gather_hi")
        gather_lo = sem("gather_lo")
        gatedT_ready = sem("gatedT_ready")
        gatedT_done = sem("gatedT_done")
        y_act = sem("y_act")
        y_dve = sem("y_dve")
        scatter_ready = sem("scatter_ready")
        scatter_done = sem("scatter_done")

        scratch = nc.dram_tensor("rel_tail", [DEPTH * H_B, 2 * P], F32, kind="Internal")
        rel_rows = rel_bias.rearrange("l h r -> (l h) r")
        R = 2 * REL_MAX + 1

        block = ctx.enter_context(nc.Block())

        def extra_experts(eng, work_on):
            eng.wait_ge(table_done, 1)
            many = eng.value_load(fulli[0:1, EXTRA:EXTRA + 1], min_val=0, max_val=EXTRA)
            for j in range(EXTRA):
                e = eng.value_load(fulli[0:1, j:j + 1], min_val=0, max_val=N_EXPERTS - 1)
                with eng.If(many > j):
                    work_on(e, N_EXPERTS + j)

        def used(eng, g):
            layer = g >= FIRST[1]
            i = g - FIRST[layer]
            if i >= len(PIECES):
                p, part = (i - len(PIECES) + 1) // 3, (i - len(PIECES) + 1) % 3
                if i == FIRST[1] - 1:
                    eng.wait_ge(ffn_down, PAIRS)
                elif i == len(PIECES):
                    eng.wait_ge(ffn_g, 1)
                elif i == len(PIECES) + 1:
                    eng.wait_ge(ffn_u, 1)
                elif part == 0:
                    eng.wait_ge(ffn_g, p + 1)
                elif part == 1:
                    eng.wait_ge(ffn_down, p)
                else:
                    eng.wait_ge(ffn_u, p + 1)
            elif PIECES[i][0] == "W":
                acc_ready.wait(eng, layer, (0 if PIECES[i][1] == "O" else 8) + 2 * int(PIECES[i][2]) + 2)
            else:
                tile_ready.wait(eng, layer, TILE_AT[PIECES[i]] + 1)

        def cut(t, g):
            s = g % SLOTS
            return t[:, s * PIECE:(s + 1) * PIECE]

        def is_small(g):
            return g in FIRST

        def columns(w, a, n):
            return w[:, a:a + n].rearrange("(t p) n -> p t n", p=P)

        def by_tiles(ap):
            return ap.rearrange("p (t n) -> p t n", t=KT)

        def by_rows(ap):
            return ap.rearrange("p (f n) -> p f n", n=D)

        @block.sync
        def _(sp):
            for b in range(TB):
                sp.dma_start(N[:, b, :], x[0, b * P:(b + 1) * P, :]).then_inc(s_x, 16)

            sp.wait_ge(rows_blank, 1)
            for i, (gg, bb) in enumerate([(ln3_g, ln3_b), (ln1_g, ln1_b), (ln2_g, ln2_b)]):
                r = i * 2 * KT
                first, layers = (KT, 1) if i == 0 else (0, DEPTH)
                for rows, src in ((rows_g, gg), (rows_b, bb)):
                    sp.dma_start(rows[r + first:r + 2 * KT, :],
                                 src[0:layers, :].rearrange("l (t p) -> (l t) p", p=P)).then_inc(s_rows, 16)
            sp.dma_start(stage_gain[0:DEPTH, :], diff_norm_g).then_inc(s_rows, 16)

            def load(slot, dst, src):
                sp.dma_start(dst, src).then_inc(raw_loaded[slot], 16)

            def layer_pieces(layer):
                where = {"QI": (w_in, C_QI), "QA": (w_in, C_QA), "KA": (w_in, C_KA), "QB": (w_in, C_QB),
                         "KB": (w_in, C_KB), "VB": (w_in, C_VB), "QC": (w_in, C_QC), "KC": (w_in, C_KC),
                         "VC": (w_in, C_VC), "VA": (w_in, C_VA), "KX": (xattn_wk, 0), "VX": (xattn_wv, 0),
                         "WO": (w_out, 0), "QX": (xattn_wq, 0), "WX": (xattn_wo, 0)}
                for i, name in enumerate(PIECES):
                    g = FIRST[layer] + i
                    if g == 2:
                        for b in range(TB):
                            sp.dma_start(E[:, b * D:(b + 1) * D], mem[0, b * P:(b + 1) * P, :]).then_inc(s_mem, 16)
                    if g >= SLOTS:
                        sp.wait_ge(lo_done, g - SLOTS + 1)
                    if name == "KI":
                        load(g % SLOTS, by_tiles(cut(RAW, g)[:, 0:KT * SMALL]), columns(w_in[layer], C_KI, SMALL))
                    else:
                        w, a = where[name[:2]]
                        a += 256 * int(name[2]) if name[2:] else 0
                        load(g % SLOTS, by_tiles(cut(RAW, g)), columns(w[layer], a, 256))

            def feed_forward():
                def piece(slot, w, k, held):
                    sp.wait_ge(lo_done, held)
                    dst = RAW[:, slot * PIECE:(slot + 1) * PIECE]
                    if w is ffn_w2:
                        load(slot, by_rows(dst), w[0][k, :].rearrange("(f p) n -> p f n", p=P))
                    else:
                        load(slot, by_tiles(dst), w[0][:, k].rearrange("(t p) n -> p t n", p=P))

                g = len(PIECES)
                piece(g % SLOTS, ffn_w1, slice(0, 2 * P), g - 2)
                piece((g + 1) % SLOTS, ffn_w3, slice(0, 2 * P), g - 1)
                with sp.Fori(1, PAIRS) as p:
                    now, one_before = bass.ds(p * (2 * P), 2 * P), bass.ds((p - 1) * (2 * P), 2 * P)
                    piece((g + 2) % SLOTS, ffn_w1, now, p * 3 + (g - 3))
                    piece((g + 3) % SLOTS, ffn_w2, one_before, p * 3 + (g - 2))
                    piece((g + 4) % SLOTS, ffn_w3, now, p * 3 + (g - 1))
                g = FIRST[1] - 1
                piece(g % SLOTS, ffn_w2, slice(D_FF - 2 * P, D_FF), g - 2)

            layer_pieces(0)
            feed_forward()
            layer_pieces(1)

            def expert_weights(e, n):
                def up(c, j):
                    col = bass.ds(j * (2 * FE) + (0 if c == "a" else FE), FE)
                    after(sp, lo1[c], n * STEPS + j)
                    sp.dma_start(by_tiles(flat["R1" + c][:]), moe_w1[0, e][:, col].rearrange("(t p) n -> p t n", p=P)
                                 ).then_inc(loaded1[c], 16)
                    after(sp, lo3[c], n * STEPS + j)
                    sp.dma_start(by_tiles(flat["R3" + c][:]), moe_w3[0, e][:, col].rearrange("(t p) n -> p t n", p=P)
                                 ).then_inc(loaded3[c], 16)

                def down(c, j):
                    col = bass.ds(j * (2 * FE) + (0 if c == "a" else FE), FE)
                    if c == "b":
                        sp.wait_ge(lo_done, ALL)
                    after(sp, w2_used[c], n * STEPS + j)
                    sp.dma_start(by_rows(R2[c][:]), moe_w2[0, e][col, :].rearrange("(f p) n -> p f n", p=P)
                                 ).then_inc(loaded2[c], 16)

                up("a", 0)
                with sp.Fori(0, STEPS - 1) as j:
                    up("b", j)
                    down("a", j)
                    up("a", j + 1)
                    down("b", j)
                up("b", STEPS - 1)
                down("a", STEPS - 1)
                down("b", STEPS - 1)

            tile_ready.wait(sp, 1, TILE_AT["OX3"] + 1)
            with sp.Fori(0, N_EXPERTS) as e:
                expert_weights(e, e)
            sp.wait_ge(table_done, 1)
            extra_experts(sp, lambda e, n: expert_weights(e, n))
            for b in range(TB):
                sp.wait_ge(out_ready, b + 1)
                sp.dma_start(out[0, b * P:(b + 1) * P, :], H[:, b, :]).then_inc(s_out, 16)
            sp.wait_ge(s_out, 16 * TB)

        @block.gpsimd
        def _(pool):
            o = Order(pool, order_pool)
            g = nc.gpsimd
            table = PT[0:DEPTH * H_B, 2 * P:2 * P + R]
            tail = PT[0:DEPTH * H_B, 768:768 + 2 * P]
            g.memset(rows_g, 1.0)
            g.memset(rows_b, 0.0).then_inc(rows_blank, 1)
            o.link(g.memset(iden[:], 0.0))
            g.affine_select(out=iden[:], in_=iden[:], compare_op=ALU.not_equal, fill=1.0, base=0,
                            pattern=[[-1, P]], channel_multiplier=1).then_inc(iden_ready, 1)
            pool.dma_start(table, rel_rows).then_inc(s_table, 16)
            for i, q in enumerate((lam_q1, lam_k1, lam_q2, lam_k2)):
                pool.dma_start(stage_lam[:, i * 128:(i + 1) * 128],
                               q.rearrange("l d -> (l d)").partition_broadcast(P)).then_inc(s_lam, 16)
            pool.dma_start(router[:], moe_router[0].rearrange("(t p) n -> p t n", p=P)).then_inc(s_router, 16)

            o.link(g.memset(flip8[:], 0.0))
            o.link(g.affine_select(out=flip8[:], in_=flip8[:], compare_op=ALU.not_equal, fill=1.0 / SCALE,
                                   base=1 - P, pattern=[[1, P]], channel_multiplier=1))
            o.link(g.memset(idenb[:], 0.0))
            o.link(g.affine_select(out=idenb[:], in_=idenb[:], compare_op=ALU.not_equal, fill=1.0, base=0,
                                   pattern=[[-1, P]], channel_multiplier=1))
            o.link(g.memset(slopeI[:], 0.0))
            for j, s in enumerate(slopes):
                o.link(g.affine_select(out=slopeI[:, j, :], in_=slopeI[:, j, :], compare_op=ALU.not_equal,
                                       fill=-s / SCALE, base=0, pattern=[[-1, P]], channel_multiplier=1))
            o.link(g.iota(stage_iota, pattern=[[-1, 2 * P]], base=P, channel_multiplier=1,
                          allow_small_or_imprecise_dtypes=True))
            o.link(g.iota(iota_s[:], pattern=[[1, 2 * P]], base=0, channel_multiplier=0,
                          allow_small_or_imprecise_dtypes=True))
            o.link(g.memset(maskI[:], 0.0))
            o.link(g.memset(maskI[0:CHUNK, P + CHUNK:2 * P], NEG_INF))
            o.link(g.memset(maskB[:], 0.0))
            o.link(g.memset(maskB[0:CHUNK, CHUNK:P], -FAR))
            o.link(g.memset(mhalf[:], -0.5))
            o.link(g.memset(ones[:], 1.0))
            o.link(g.memset(before[:], 1.0))
            o.link(g.affine_select(out=before[:], in_=before[:], compare_op=ALU.is_gt, fill=0.0, base=0,
                                   pattern=[[1, P]], channel_multiplier=-1))
            g.memset(top8[:], 0.0).then_inc(pool_done, 1)

            pool.wait_ge(tail_done, 1)
            pool.dma_start(scratch.ap(), tail).then_inc(s_table_out, 16)
            pool.wait_ge(s_table_out, 16)

            lns = ((ln1_g, ln1_b), (ln2_g, ln2_b), (ln3_g, ln3_b))

            def to_rstd(n, layer, v, out_, width):
                var_ready.wait(pool, layer, n)
                g.tensor_tensor(out_, v, mhalf[:, 0:width], ALU.pow).then_inc(rstd_ready.sem, 1)

            for layer in range(DEPTH):
                exp_done.wait(pool, layer, 0)
                near = bass.AP(rel_bias.tensor, 1, [[H_B * R, DEPTH], [1, P], [R, H_B], [1, P]])
                far = bass.AP(scratch, 0, [[H_B * 2 * P, DEPTH], [1, P], [2 * P, H_B], [1, P]])
                pool.dma_start(HK[:, 0], near[layer]).then_inc(hankel_loaded.sem, 16)
                pool.dma_start(HK[:, 1], far[layer]).then_inc(hankel_loaded.sem, 16)
                for i, (gg, bb) in enumerate(lns):
                    resid_done.wait(pool, layer, i)
                    pool.dma_start(GB[:, 0, :], gg[layer].partition_broadcast(P)).then_inc(gb_loaded.sem, 16)
                    pool.dma_start(GB[:, 1, :], bb[layer].partition_broadcast(P)).then_inc(gb_loaded.sem, 16)
                    if i == 0:
                        to_rstd(1, layer, ss[:], rms[:], 4)
                        to_rstd(2, layer, ss[:], rms[:], 4)
                    for b in range(TB):
                        to_rstd(3 + 2 * i + b, layer, var[:, b:b + 1], rstd[:, b:b + 1], 1)

        @block.tensor
        def _(pe):
            mm = pe.matmul

            def turn(dst, src, n=P):
                return pe.transpose(dst, src, iden[0:n, 0:n])

            def mm3(dst, wh, wl, xh, xl, start, stop):
                mm(dst, wh, xh, start=start, stop=False)
                mm(dst, wh, xl, start=False, stop=False)
                return mm(dst, wl, xh, start=False, stop=stop)

            for c in "ab":
                for signal in (g_ready, u_ready, turned_ready, w2_used):
                    pe.sem_inc(signal[c], 1)
            pe.sem_inc(gather_ready, 1)
            pe.sem_inc(gatedT_ready, 1)
            pe.wait_ge(iden_ready, 1)
            pe.wait_ge(s_rows, 16 * 7)
            turn(PS[:, 0, 0:6 * KT], rows_g, 6 * KT)
            turn(PS[:, 0, 64:64 + 6 * KT], rows_b, 6 * KT)
            turn(PS[:, 0, 128:128 + DEPTH], stage_gain[0:DEPTH, :], DEPTH).then_inc(columns_ready, 1)
            pe.wait_ge(s_x, 16 * TB)

            def turn_memory():
                pe.wait_ge(s_mem, 16 * TB)
                for t in range(KT):
                    for b in range(TB):
                        last = turn(PS[:, 1 + t // 2, (t % 2) * SEQ + b * P:(t % 2) * SEQ + (b + 1) * P],
                                    E[:, b * D + t * P:b * D + (t + 1) * P])
                last.then_inc(mem_ready, 1)

            def begin(name, layer):
                i = TILE_AT[name]
                if i >= 2:
                    taken(TILES[i - 2][0], layer)
                return tile_bank(name)

            def taken(name, layer):
                who = LAST[name]
                tile_taken[who].wait(pe, layer, TAKEN[who].index(name) + 1)

            def ready(ins):
                ins.then_inc(tile_ready.sem, 1)

            def parts(g):
                pe.wait_ge(lo_done, g + 1)
                return cut(SPH, g), cut(SPL, g)

            def turned_rows(name, layer):
                bank = begin(name, layer)
                k = int(name[2])
                for b in range(TB):
                    if k == 0 and (layer or name != "HT0"):
                        norm_done.wait(pe, layer, {"HT": -TB, "HX": 0, "HF": TB}[name[:2]] + b + 1)
                    for t in (2 * k, 2 * k + 1):
                        c = (t % 2) * SEQ + b * P
                        last = turn(bank[:, c:c + P], N[:, b, t * P:(t + 1) * P])
                ready(last)

            def fresh(count, t, layer):
                if t % 2 == 0:
                    turned_lo.wait(pe, layer, count + t // 2 + 1)

            def project_small(g, layer):
                bank = begin("KI", layer)
                WH, WL = [w[:, 0:KT * (P + 8)].rearrange("p (t n) -> p t n", t=KT) for w in parts(g)]
                for t in range(KT):
                    fresh(0, t, layer)
                    mm3(bank[:, 0:SEQ], WH[:, t, 0:P], WL[:, t, 0:P], XTH[:, t, :], XTL[:, t, :],
                        t == 0, t == KT - 1)
                for b in range(TB):
                    r = slice(b * P, (b + 1) * P)
                    for t in range(KT):
                        last = mm3(bank[:, SEQ + b * 8:SEQ + b * 8 + 8], XTH[:, t, r], XTL[:, t, r],
                                   WH[:, t, P:P + 8], WL[:, t, P:P + 8], t == 0, t == KT - 1)
                ready(last)

            def project_turned(name, g, XH, XL, layer):
                bank = begin(name, layer)
                WH, WL = [by_tiles(w) for w in parts(g)]
                for m in range(2):
                    c = slice(m * P, (m + 1) * P)
                    for t in range(KT):
                        if name == "QX0" and m == 0:
                            fresh(4, t, layer)
                        last = mm3(bank[:, m * SEQ:(m + 1) * SEQ], WH[:, t, c], WL[:, t, c], XH[:, t, :], XL[:, t, :],
                                   t == 0, t == KT - 1)
                ready(last)

            def rows_product(dsts, g, XH, XL):
                WH, WL = [by_tiles(w) for w in parts(g)]
                for b in range(TB):
                    r = slice(b * P, (b + 1) * P)
                    for t in range(KT):
                        last = mm3(dsts[b], XH[:, t, r], XL[:, t, r], WH[:, t, :], WL[:, t, :], t == 0, t == KT - 1)
                    yield last

            def project_rows(name, g, XH, XL, layer):
                bank = begin(name, layer)
                for last in rows_product([bank[:, 0:256], bank[:, 256:512]], g, XH, XL):
                    pass
                ready(last)

            def accumulate(name, layer):
                j = int(name[2])
                if name == "WO0":
                    for tile in ("YA0", "YB0", "YA1", "YB1"):
                        taken(tile, layer)
                if name == "WX0":
                    taken("OX2", layer)
                    taken("OX3", layer)
                    exp_done.wait(pe, layer, 8)
                c = slice((j % 2) * 256, (j % 2) * 256 + 256)
                dsts = [PS[:, 2 * (j // 2) + b, c] for b in range(TB)]
                for last in rows_product(dsts, FIRST[layer] + PIECE_AT[name], XTH, XTL):
                    last.then_inc(acc_ready.sem, 1)

            def group_free(group, layer):
                if group == "A0":
                    relu_done.wait(pe, layer, 2)
                elif group == "A1":
                    relu_done.wait(pe, layer, 1)
                elif group in ("B0", "C0"):
                    exp_done.wait(pe, layer, 1)
                elif group in ("B1", "C1"):
                    exp_done.wait(pe, layer, 2)
                elif group == "X0":
                    exp_done.wait(pe, layer, 4)
                else:
                    sum_done.wait(pe, layer, 4)

            def made(ins):
                ins.then_inc(scores_ready.sem, 1)

            def index_dots(b, layer):
                if b == 1:
                    for name in ("KI", "QI0", "QI1"):
                        taken(name, layer)
                    sum_done.wait(pe, layer, 0)
                    if layer == 0:
                        pe.wait_ge(columns_done, 3)
                        pe.wait_ge(mem_done, 1)
                for h in range(H_IDX):
                    r = slice(64 * (h % 2), 64 * (h % 2) + 64)
                    last = mm(DOTS[b][:, place(h, H_IDX), :], QK[r, M_QI + h // 2, b * P:(b + 1) * P],
                              QK[r, M_KI, 0:NKEYS[b]], start=True, stop=True)
                last.then_inc(dots_ready.sem, 1)

            def scores_a(b, layer):
                group = f"A{b}"
                if b == 0:
                    if layer == 0:
                        pe.wait_ge(pool_done, 1)
                        pe.wait_ge(dist_done, 1)
                    taken("KA0", layer)
                    taken("KA1", layer)
                group_free(group, layer)
                n = NKEYS[b]
                for i in range(2 * H_A):
                    h, m = i // 2, i % 2
                    r = slice(64 * m, 64 * m + 64)
                    S = score(group, m * H_A + h)
                    mm(S, QK[r, M_QA + h, b * P:(b + 1) * P], QK[r, M_KA + h, 0:n],
                       start=True, stop=False)
                    last = mm(S, slopeI[:, 2 * h, :], dist[:, 2 * P - n:], start=False, stop=True)
                made(last)

            def scores_b(b, layer):
                group = f"B{b}"
                if b == 0:
                    hankel_loaded.wait(pe, layer, 1)
                    taken("KB", layer)
                group_free(group, layer)
                n = NKEYS[b]
                for h in range(H_B):
                    S = score(group, place(h, H_B))
                    r = slice(64 * (h % 2), 64 * (h % 2) + 64)
                    mm(S, QK[r, M_QB + h // 2, b * P:(b + 1) * P], QK[r, M_KB + h // 2, 0:n],
                       start=True, stop=False)
                    for k in range(b + 1):
                        mm(S[:, k * P:(k + 1) * P], HK[:, b - k, h, :], flip8[:], start=False, stop=False)
                    last = mm(S[:, b * P:n], idenb[:], maskB[:], start=False, stop=True)
                made(last)

            def scores_c(b, layer):
                group = f"C{b}"
                group_free(group, layer)
                selected.wait(pe, layer, b + 1)
                if b == 0:
                    taken("KC", layer)
                n = NKEYS[b]
                chosen_keys = selb[:, 0:P] if b == 0 else selb[:, P:3 * P]
                for h in range(H_C):
                    S = score(group, place(h, H_C))
                    r = slice(64 * (h % 2), 64 * (h % 2) + 64)
                    mm(S, QK[r, M_QC + h // 2, b * P:(b + 1) * P], QK[r, M_KC + h // 2, 0:n],
                       start=True, stop=False)
                    mm(S, slopeI[:, 2 * h + 1, :], dist[:, 2 * P - n:], start=False, stop=False)
                    last = mm(S, idenb[:], chosen_keys, start=False, stop=True)
                made(last)

            def scores_x(b, layer):
                if b == 0:
                    for name in ("QX2", "QX3", "KX3"):
                        taken(name, layer)
                group_free(f"X{b}", layer)
                for h in range(H_X):
                    for c in range(2):
                        last = mm(score(f"X{b}", h), QK[:, 2 * h + c, b * P:(b + 1) * P], KX[:, 2 * h + c, :],
                                  start=(c == 0), stop=(c == 1))
                made(last)

            def turn_probs(name, group, k, layer):
                if group[0] == "A":
                    probs_ready.wait(pe, layer, 1 + int(group[1]))
                elif group[0] == "X":
                    probs_ready.wait(pe, layer, 3 + int(group[1]))
                else:
                    exp_done.wait(pe, layer, 4 if group[1] == "0" else 6)
                bank = begin(name, layer)
                for h in range(4):
                    i = place(h, 4) if group[0] in "BC" else h
                    src = EV[group][:, i, k * P:(k + 1) * P]
                    last = turn(bank[:, h * P:(h + 1) * P], src)
                ready(last)

            def values_a(b, layer):
                bank = begin(f"OA{b}", layer)
                halves = ["TA0"] if b == 0 else ["TA1", "TA2"]
                for name in ["VA0", "VA1"] + halves:
                    taken(name, layer)
                for h in range(H_A):
                    for k, part in enumerate(halves):
                        last = mm(bank[:, h * P:(h + 1) * P], PTV[part][:, h, :], VN[:, k, h * P:(h + 1) * P],
                                  start=(k == 0), stop=(k == len(halves) - 1))
                ready(last)

            def values_bc(b, layer):
                bank = begin(f"OBC{b}", layer)
                for name in ["VC"] + (["TB0", "TC0"] if b == 0 else ["TB1", "TB2", "TC1", "TC2"]):
                    taken(name, layer)
                for g, off in (("B", 512), ("C", 768)):
                    halves = [f"T{g}0"] if b == 0 else [f"T{g}1", f"T{g}2"]
                    for h in range(4):
                        c = off - 512 + h * 64
                        for k, part in enumerate(halves):
                            last = mm(bank[:, c:c + 64], PTV[part][:, h, :],
                                      VN[:, k, off + h * 64:off + (h + 1) * 64],
                                      start=(k == 0), stop=(k == len(halves) - 1))
                ready(last)

            def values_x(h, layer):
                if h == 0:
                    for name in ("TX2", "TX3", "VX2", "VX3"):
                        taken(name, layer)
                bank = begin(f"OX{h}", layer)
                for c in range(2):
                    for k in range(2):
                        last = mm(bank[:, c * SEQ:(c + 1) * SEQ], VX[:, k, (2 * h + c) * P:(2 * h + c + 1) * P],
                                  PX[:, k, h, :], start=(k == 0), stop=(k == 1))
                ready(last)

            def turn_outputs(name, layer):
                b, off = int(name[2]), 0 if name[1] == "A" else 4
                rows_done.wait(pe, layer, b + 1)
                bank = begin(name, layer)
                for m in range(4):
                    last = turn(bank[:, m * P:(m + 1) * P], N[:, b, (off + m) * P:(off + m + 1) * P])
                ready(last)

            def tile(name, layer):
                kind, i = name[:2], int(name[-1]) if name[-1].isdigit() else 0
                g = FIRST[layer] + PIECE_AT[name] if name in PIECE_AT else None
                if kind in ("HT", "HX", "HF"):
                    turned_rows(name, layer)
                elif name == "KI":
                    if layer == 0:
                        turn_memory()
                    project_small(g, layer)
                elif kind == "KX":
                    project_turned(name, g, YMH, YML, layer)
                elif kind in ("QI", "QA", "KA", "QB", "KB", "QC", "KC", "QX"):
                    project_turned(name, g, XTH, XTL, layer)
                elif kind == "VX":
                    project_rows(name, g, YMH, YML, layer)
                elif kind[0] == "V":
                    project_rows(name, g, XTH, XTL, layer)
                elif kind[0] == "T":
                    if kind == "TX":
                        turn_probs(name, f"X{i // 2}", i % 2, layer)
                    else:
                        turn_probs(name, f"{kind[1]}{min(i, 1)}", max(i - 1, 0), layer)
                elif kind == "OA":
                    values_a(i, layer)
                elif name[:3] == "OBC":
                    values_bc(i, layer)
                elif kind == "OX":
                    values_x(i, layer)
                else:
                    turn_outputs(name, layer)

            def body(layer):
                pe.wait_ge(ffn_hidden, layer * PAIRS)
                for step in PLAN:
                    kind, name = step[0], step[1]
                    if kind == "tile":
                        tile(name, layer)
                    elif kind == "dots":
                        index_dots(name, layer)
                    elif kind == "scores":
                        {"A": scores_a, "B": scores_b, "C": scores_c, "X": scores_x}[name[0]](int(name[1]), layer)
                    elif kind == "acc":
                        accumulate(f"{name}{step[2]}", layer)
                sum_done.wait(pe, layer, 8)

            def feed_forward():
                FIRST_FFN = len(PIECES)

                def up(slot, split, bank, signal, first=False):
                    pe.wait_ge(lo_done, split)
                    r = slice(slot * PIECE, (slot + 1) * PIECE)
                    WH, WL = by_tiles(SPH[:, r]), by_tiles(SPL[:, r])
                    for m in range(2):
                        c = slice(m * P, (m + 1) * P)
                        for t in range(KT):
                            if first and m == 0:
                                fresh(8, t, 0)
                            last = mm3(PS[:, bank, m * SEQ:(m + 1) * SEQ], WH[:, t, c], WL[:, t, c],
                                       XTH[:, t, :], XTL[:, t, :], t == 0, t == KT - 1)
                    last.then_inc(signal, 1)

                def down(slot, split, made_, first=False, final=False):
                    pe.wait_ge(lo_done, split)
                    pe.wait_ge(ffn_lo, made_)
                    r = slice(slot * PIECE, (slot + 1) * PIECE)
                    WH, WL = by_rows(SPH[:, r]), by_rows(SPL[:, r])
                    for b in range(TB):
                        for f in range(2):
                            for half in range(2):
                                c = slice(half * HALF, (half + 1) * HALF)
                                q = slice(b * P, (b + 1) * P)
                                last = mm3(PS[:, 2 * half + b, :], FHH[:, f, q], FHL[:, f, q], WH[:, f, c],
                                           WL[:, f, c], first and f == 0, final and f == 1)
                        if final and b == 0:
                            last.then_inc(ffn_first_rows, 1)
                    last.then_inc(ffn_down, 1)

                g = FIRST_FFN
                up(g % SLOTS, g + 1, 4, ffn_g, first=True)
                up((g + 1) % SLOTS, g + 2, 5, ffn_u)
                pe.wait_ge(ffn_silu, 1)
                up((g + 2) % SLOTS, g + 3, 4, ffn_g)
                down((g + 3) % SLOTS, g + 4, 1, first=True)
                pe.wait_ge(ffn_hidden, 1)
                up((g + 4) % SLOTS, g + 5, 5, ffn_u)
                with pe.Fori(2, PAIRS) as p:
                    pe.wait_ge(ffn_silu, p)
                    up((g + 2) % SLOTS, p * 3 + g, 4, ffn_g)
                    down((g + 3) % SLOTS, p * 3 + (g + 1), p)
                    pe.wait_ge(ffn_hidden, p)
                    up((g + 4) % SLOTS, p * 3 + (g + 2), 5, ffn_u)
                g = FIRST[1] - 1
                down(g % SLOTS, g + 1, PAIRS, final=True)

            def mixture():
                pe.wait_ge(router_lo, 1)
                for b in range(TB):
                    r = slice(b * P, (b + 1) * P)
                    for t in range(KT):
                        if b == 0:
                            fresh(8, t, 1)
                        last = mm3(PS[:, 4, b * 8:b * 8 + 8], XTH[:, t, r], XTL[:, t, r],
                                   routerh[:, t, :], routerl[:, t, :], t == 0, t == KT - 1)
                last.then_inc(router_ready, 1)
                pe.wait_ge(chosen_done, 1)
                mm(PS[:, 5, 0:8], before[:], chosen[:, 0, :], start=True, stop=True)
                mm(PS[:, 5, 8:16], before[:], chosen[:, 1, :], start=True, stop=False)
                mm(PS[:, 5, 8:16], ones[:], chosen[:, 0, :], start=False, stop=True)
                mm(PS[:, 5, 16:24], ones[:], chosen[:, 0, :], start=True, stop=False)
                mm(PS[:, 5, 16:24], ones[:], chosen[:, 1, :], start=False, stop=True).then_inc(rank_ready, 1)
                pe.wait_ge(table_done, 1)
                pe.wait_ge(rows_lo, 1)

                def gather(n, part):
                    rows = HRH if part == 0 else HRL
                    if part == 0:
                        pe.wait_ge(onehot_done, n * 2 + 1)
                    for q, bank in enumerate((2, 4) if part == 0 else (6, 3)):
                        if bank == 2:
                            after(pe, silu_done["a"], n * STEPS)
                        elif bank == 4:
                            after(pe, hidden_done["a"], n * STEPS)
                        elif bank == 6:
                            after(pe, turned_done["a"], n * STEPS)
                        else:
                            after(pe, silu_done["b"], n * STEPS)
                        for t in range(4):
                            c = slice((4 * q + t) * P, (4 * q + t + 1) * P)
                            for b in range(TB):
                                last = mm(PS[:, bank, t * P:(t + 1) * P], rows[:, b, c], ONE[:, b, :],
                                          start=(b == 0), stop=(b == 1))
                        last.then_inc(gather_ready, 1)

                def up(c, which, k):
                    after(pe, (lo1 if which == 0 else lo3)[c], k + 1)
                    if which == 0:
                        after(pe, silu_done[c], k)
                    else:
                        after(pe, hidden_done[c], k)
                    WH, WL = (S1H, S1L) if which == 0 else (S3H, S3L)
                    WH, WL = by_tiles(WH[c]), by_tiles(WL[c])
                    bank = 2 + 2 * which + (c == "b")
                    for t in range(KT):
                        last = mm3(PS[:, bank, 0:FE], XGH[:, t, :], XGL[:, t, :], WH[:, t, :], WL[:, t, :],
                                   t == 0, t == KT - 1)
                    last.then_inc((g_ready if which == 0 else u_ready)[c], 1)

                def turn_hidden(c, k):
                    after(pe, hidden_done[c], k + 1)
                    after(pe, turned_done[c], k)
                    for f in range(2):
                        last = turn(PS[:, 6 + (c == "b"), f * P:(f + 1) * P], HID[c][:, f * P:(f + 1) * P])
                    last.then_inc(turned_ready[c], 1)

                def down(c, k, first=False, final=False):
                    pe.wait_ge(lo2[c], k + 1)
                    after(pe, turned_done[c], k + 1)
                    WH, WL = by_rows(S2H[c]), by_rows(S2L[c])
                    for f in range(2):
                        r = slice(f * P, (f + 1) * P)
                        for half in range(2):
                            q = slice(half * HALF, (half + 1) * HALF)
                            last = mm3(PS[:, half, :], HTH[c][:, r], HTL[c][:, r], WH[:, f, q], WL[:, f, q],
                                       first and f == 0, final and f == 1)
                    last.then_inc(w2_used[c], 1)

                def start(n):
                    pe.wait_ge(gather_hi, n + 1)
                    pe.wait_ge(gather_lo, n + 1)
                    up("a", 0, n * STEPS)

                def item(n, ahead):
                    k0 = n * STEPS
                    up("a", 1, k0)
                    up("b", 0, k0)
                    after(pe, scatter_done, n * 4)
                    turn_hidden("a", k0)
                    pe.wait_ge(onehot_done, n * 2 + 2)
                    for b in range(TB):
                        last = turn(PS[:, 7, b * P:(b + 1) * P], GATED[:, b, :])
                    last.then_inc(gatedT_ready, 1)
                    up("b", 1, k0)
                    pe.wait_ge(gatedT_done, n + 1)
                    down("a", k0, first=True)
                    with pe.Fori(1, STEPS) as j:
                        k = k0 + j
                        up("a", 0, k)
                        turn_hidden("b", k - 1)
                        up("a", 1, k)
                        down("b", k - 1)
                        up("b", 0, k)
                        turn_hidden("a", k)
                        up("b", 1, k)
                        down("a", k)
                    k = k0 + (STEPS - 1)
                    if ahead:
                        gather(n + 1, 0)
                    turn_hidden("b", k)
                    if ahead:
                        gather(n + 1, 1)
                    down("b", k, final=True)
                    if ahead:
                        start(n + 1)
                    pe.wait_ge(y_act, n + 1)
                    pe.wait_ge(y_dve, n + 1)
                    for i, bank in enumerate((7, 0, 1, 6)):
                        half, b = i // 2, i % 2
                        mm(PS[:, bank, :], GATEDT[:, b * P:(b + 1) * P],
                           YE[:, half * HALF:(half + 1) * HALF], start=True, stop=True
                           ).then_inc(scatter_ready, 1)

                gather(0, 0)
                gather(0, 1)
                start(0)
                with pe.Fori(0, N_EXPERTS - 1) as e:
                    item(e, True)
                item(N_EXPERTS - 1, False)

                def extra(e, n):
                    after(pe, scatter_done, n * 4)
                    gather(n, 0)
                    gather(n, 1)
                    start(n)
                    item(n, False)

                extra_experts(pe, extra)

            for layer in range(DEPTH):
                body(layer)
                if layer == 0:
                    feed_forward()
                else:
                    mixture()

        def destination(name):
            bank = tile_bank(name)
            kind, i = name[:2], int(name[-1]) if name[-1].isdigit() else 0
            two = bank.rearrange("p (m t) -> p m t", t=SEQ)
            turned = {"QI": M_QI + 2 * i, "QA": M_QA + 2 * i, "KA": M_KA + 2 * i, "QB": M_QB, "KB": M_KB,
                      "QC": M_QC, "KC": M_KC}
            if kind in turned:
                return QK[:, turned[kind]:turned[kind] + 2, :], two
            if name == "VB":
                return VN[:, :, 512:768], two
            if name == "VC":
                return VN[:, :, 768:1024], two
            if kind == "VA":
                return VN[:, :, 256 * i:256 * (i + 1)], two
            if kind == "KX":
                return KX[:, 2 * i:2 * i + 2, :], two
            if kind == "QX":
                return QK[:, 2 * i:2 * i + 2, :], two
            if kind == "VX":
                return VX[:, :, 256 * i:256 * (i + 1)], two
            if kind == "TX":
                return PX[:, i % 2, :, i // 2 * P:(i // 2 + 1) * P], heads(bank)
            return PTV[name], heads(bank)

        def column(tile, row, layer, t):
            return tile[:].rearrange("p r t -> p (r t)")[:, bass.ds(layer * KT + (row * KT + t), 1)]

        NORM_ROW = {"HT": 0, "HX": 2, "HF": 4}

        def split_places(name):
            bank, kind, i = tile_bank(name), name[:2], int(name[2])
            if kind == "OX":
                return XTH[:, 2 * i:2 * i + 2, :], XTL[:, 2 * i:2 * i + 2, :], bank.rearrange("p (m t) -> p m t", t=SEQ)
            m = slice(0, 4) if kind == "YA" else slice(4, 8)
            q = slice(i * P, (i + 1) * P)
            return XTH[:, m, q], XTL[:, m, q], heads(bank)

        def turned_places(name):
            k = int(name[2])
            return [t[:, 2 * k:2 * k + 2, :].rearrange("p m t -> p (m t)") for t in (XTH, XTL)]

        def small_places(ring, g):
            w = cut(ring, g)[:, 0:KT * (P + 8)].rearrange("p (t n) -> p t n", t=KT)
            return w[:, :, 0:D_IDX], w[:, :, D_IDX:P + 8]

        def small_raw(g):
            w = cut(RAW, g)[:, 0:KT * SMALL].rearrange("p (t n) -> p t n", t=KT)
            return w[:, :, 0:D_IDX], w

        @block.scalar
        def _(act):
            a = nc.scalar
            for c in "ab":
                act.sem_inc(silu_done[c], 1)

            def high(dst, src):
                return a.activation(dst, src, ACT.Copy)

            def split(g):
                act.wait_ge(raw_loaded[g % SLOTS], 16 * (g // SLOTS + 1))
                if g >= SLOTS:
                    used(act, g - SLOTS)
                if is_small(g):
                    for dst, src in zip(small_places(SPH, g), small_raw(g)):
                        last = high(dst, src)
                else:
                    last = high(cut(SPH, g), cut(RAW, g))
                last.then_inc(hi_done, 1)

            split(0)
            act.wait_ge(columns_done, 3)

            def memory():
                split(1)
                act.wait_ge(mem_ready, 1)
                for i in range(KT // 2):
                    last = high(YMH[:, 2 * i:2 * i + 2, :].rearrange("p m t -> p (m t)"), PS[:, 1 + i, :])
                last.then_inc(mem_hi, 1)

            def lambda_and_router():
                act.wait_ge(lam_ready, 1)
                a.activation(lam_work[:, 2 * DEPTH:4 * DEPTH], lam_work[:, 0:2 * DEPTH], ACT.Exp).then_inc(lam_exp, 1)
                act.wait_ge(s_router, 16)
                high(routerh[:], router[:]).then_inc(router_hi, 1)

            def turned(kind, layer):
                def affine(k):
                    name = f"{kind}{k}"
                    tile_ready.wait(act, layer, TILE_AT[name] + 1)
                    for t in range(2):
                        last = a.activation(TURN[k][:, t * SEQ:(t + 1) * SEQ],
                                            tile_bank(name)[:, t * SEQ:(t + 1) * SEQ],
                                            ACT.Identity, bias=column(LB, NORM_ROW[kind], layer, 2 * k + t),
                                            scale=column(LG, NORM_ROW[kind], layer, 2 * k + t))
                    last.then_inc(tile_taken["a"].sem, 1)

                def split_rows(k):
                    name = f"{kind}{k}"
                    who = LAST[name]
                    tile_taken[who].wait(act, layer, TAKEN[who].index(name) + 1)
                    high(turned_places(name)[0], TURN[k]).then_inc(part_hi.sem, 1)

                affine(0)
                split_rows(0)
                affine(2)
                split_rows(1)
                split_rows(2)
                split_rows(3)

            def take(name, layer):
                if name == "TB0" and layer == 0:
                    act.wait_ge(s_table_out, 16)
                if name == "TA2":
                    selected.wait(act, layer, 2)
                tile_ready.wait(act, layer, TILE_AT[name] + 1)
                dst, src = destination(name)
                a.activation(dst, src, ACT.Copy).then_inc(tile_taken["a"].sem, 1)

            def take_high(name, layer):
                tile_ready.wait(act, layer, TILE_AT[name] + 1)
                dst, _, src = split_places(name)
                if name[:2] == "YA":
                    last = a.activation(dst, src, ACT.Copy, scale=gain[:, bass.ds(layer, 1)])
                else:
                    last = a.activation(dst, src, ACT.Copy)
                last.then_inc(part_hi.sem, 1)

            def exps(group, layer):
                i = GROUPS.index(group)
                max_done.wait(act, layer, max(through(group), i + 1))
                for m in range(maps_of(group)):
                    last = a.activation(EV[group][:, m, :], score(group, m), ACT.Exp, bias=nmx[:, i, m:m + 1],
                                        scale=SCALE_X if group[0] == "X" else SCALE,
                                        accum_out=sums[:, i, m:m + 1])
                last.then_inc(exp_done.sem, 1)

            def body(layer):
                for step in PLAN:
                    kind, name = step[0], step[1]
                    piece = f"{name}{step[2]}" if kind == "acc" else name
                    if piece in PIECE_AT:
                        g = FIRST[layer] + PIECE_AT[piece] + SLOTS - 1
                        if g < ALL:
                            split(g)
                    if kind == "tile":
                        if name[:2] in NORM_ROW:
                            if name[2] == "0":
                                turned(name[:2], layer)
                                if name == "HT0" and layer == 0:
                                    memory()
                        elif step[2] == "a":
                            take(name, layer)
                        elif step[2] == "s":
                            take_high(name, layer)
                    elif kind == "dots":
                        if name == 1 and layer == 0:
                            lambda_and_router()
                        dots_ready.wait(act, layer, 2 - name)
                        a.activation(DOT[name], DOTS[name], ACT.Relu).then_inc(relu_done.sem, 1)
                    elif kind == "exp":
                        exps(name, layer)

            def feed_forward():
                def split_ring(slot, loads, held, uses):
                    act.wait_ge(raw_loaded[slot], loads)
                    act.wait_ge(held, uses)
                    r = slice(slot * PIECE, (slot + 1) * PIECE)
                    high(SPH[:, r], RAW[:, r]).then_inc(hi_done, 1)

                def silu(p):
                    act.wait_ge(ffn_g, p + 1)
                    act.wait_ge(ffn_hidden, p)
                    a.activation(FSIL, PS[:, 4, :], ACT.Silu).then_inc(ffn_silu, 1)

                def split_hidden(p):
                    act.wait_ge(ffn_hidden, p + 1)
                    act.wait_ge(ffn_down, p)
                    high(FHH[:].rearrange("p f t -> p (f t)"), FHID).then_inc(ffn_hi, 1)

                g = len(PIECES)
                split(g + 2)
                silu(0)
                split(g + 3)
                split_hidden(0)
                split(g + 4)
                assert (g + 2) // SLOTS == (g + 3) // SLOTS == (g + 4) // SLOTS - 1
                first = 16 * ((g + 2) // SLOTS + 1)
                with act.Fori(1, PAIRS - 1) as p:
                    silu(p)
                    split_ring((g + 2) % SLOTS, p * 16 + first, ffn_g, p + 1)
                    split_ring((g + 3) % SLOTS, p * 16 + first, ffn_down, p)
                    split_hidden(p)
                    split_ring((g + 4) % SLOTS, p * 16 + (first + 16), ffn_u, p + 1)
                silu(PAIRS - 1)
                split(FIRST[1] - 1)
                split(FIRST[1])
                split_hidden(PAIRS - 1)
                split(FIRST[1] + 1)

            def mixture():
                def split1(c, k):
                    act.wait_ge(loaded1[c], (k + 1) * 16)
                    after(act, g_ready[c], k)
                    high(S1H[c], flat["R1" + c][:]).then_inc(hi1[c], 1)

                def split3(c, k):
                    act.wait_ge(loaded3[c], (k + 1) * 16)
                    after(act, u_ready[c], k)
                    high(S3H[c], flat["R3" + c][:]).then_inc(hi3[c], 1)

                def split2(c, k):
                    act.wait_ge(loaded2[c], (k + 1) * 16)
                    after(act, w2_used[c], k)
                    high(S2H[c], R2[c][:]).then_inc(hi2[c], 1)

                split1("a", 0)
                split3("a", 0)
                resid_done.wait(act, 1, 2)
                for b in range(TB):
                    last = high(HRH[:, b, :], H[:, b, :])
                last.then_inc(rows_hi, 1)
                act.wait_ge(logit_done, 1)
                a.activation(gw[:, :, 1:2], gw[:, :, 0:1], ACT.Exp).then_inc(exp2_done, 1)
                for b in range(TB):
                    last = a.activation(N[:, b, :], H[:, b, :], ACT.Copy, scale=ALPHA)
                last.then_inc(total_begun, 1)
                split1("b", 0)
                split3("b", 0)

                def gather(n):
                    for q, bank in enumerate((2, 4)):
                        after(act, gather_ready, n * 4 + (q + 1))
                        last = high(XGH[:, 4 * q:4 * q + 4, :], heads(PS[:, bank, :]))
                    last.then_inc(gather_hi, 1)

                def silu(c, k):
                    after(act, g_ready[c], k + 1)
                    after(act, hidden_done[c], k)
                    a.activation(SIL[c], PS[:, 2 + (c == "b"), 0:FE], ACT.Silu).then_inc(silu_done[c], 1)

                def take_turned(c, k):
                    after(act, turned_ready[c], k + 1)
                    after(act, w2_used[c], k)
                    high(HTH[c], PS[:, 6 + (c == "b"), 0:FE]).then_inc(turned_hi[c], 1)

                def item(n, ahead):
                    k0 = n * STEPS

                    def step(c, k, last_turned, following, gates=False):
                        silu(c, k)
                        if last_turned:
                            take_turned(*last_turned)
                        if gates:
                            act.wait_ge(gatedT_ready, n + 2)
                            a.activation(GATEDT, PS[:, 7, 0:TB * P], ACT.Copy).then_inc(gatedT_done, 1)
                        split1(*following)
                        split3(*following)
                        split2(c, k)

                    silu("a", k0)
                    split2("a", k0)
                    step("b", k0, ("a", k0), ("a", k0 + 1), gates=True)
                    with act.Fori(1, STEPS - 1) as j:
                        step("a", k0 + j, ("b", k0 + j - 1), ("b", k0 + j))
                        step("b", k0 + j, ("a", k0 + j), ("a", k0 + j + 1))
                    k = k0 + (STEPS - 1)
                    step("a", k, ("b", k - 1), ("b", k))
                    silu("b", k)
                    take_turned("a", k)
                    split2("b", k)
                    if ahead:
                        split1("a", k + 1)
                        gather(n + 1)
                    take_turned("b", k)
                    if ahead:
                        split3("a", k + 1)
                    after(act, w2_used["b"], k + 1)
                    a.activation(YE[:, 0:HALF], PS[:, 0, :], ACT.Copy).then_inc(y_act, 1)
                    if ahead:
                        split1("b", k + 1)
                        split3("b", k + 1)

                gather(0)
                with act.Fori(0, N_EXPERTS - 1) as e:
                    item(e, True)
                item(N_EXPERTS - 1, False)

                def extra(e, n):
                    for c in "ab":
                        split1(c, n * STEPS)
                        split3(c, n * STEPS)
                    gather(n)
                    item(n, False)

                extra_experts(act, extra)

            for layer in range(DEPTH):
                body(layer)
                if layer == 0:
                    feed_forward()
                else:
                    mixture()

        @block.vector
        def _(dve):
            v = nc.vector
            for c in "ab":
                for signal in (lo1, lo3, hidden_done, turned_done):
                    dve.sem_inc(signal[c], 1)
            dve.sem_inc(scatter_done, 1)
            o = Order(dve, order_dve)
            def low(dst, src, hi):
                return v.tensor_tensor(dst, src, hi, ALU.subtract)

            def split(g):
                dve.wait_ge(hi_done, g + 1)
                if is_small(g):
                    for dst, src, hi in zip(small_places(SPL, g), small_raw(g), small_places(SPH, g)):
                        last = low(dst, src, hi)
                else:
                    last = low(cut(SPL, g), cut(RAW, g), cut(SPH, g))
                last.then_inc(lo_done, 1)

            dve.wait_ge(columns_ready, 1)
            v.tensor_copy(LG[:].rearrange("p r t -> p (r t)"), PS[:, 0, 0:6 * KT]).then_inc(columns_done, 1)
            v.tensor_copy(LB[:].rearrange("p r t -> p (r t)"), PS[:, 0, 64:64 + 6 * KT]).then_inc(columns_done, 1)
            for l in range(DEPTH):
                last = v.tensor_scalar(gain[:, l:l + 1], PS[:, 0, 128 + l:129 + l], 1.0 - lam_inits[l], None, ALU.mult)
            last.then_inc(columns_done, 1)
            split(0)
            dve.wait_ge(columns_done, 3)
            lsum = lam_work[:, 0:2 * DEPTH].rearrange("p (i l) -> p i l", l=DEPTH)
            lexp = lam_work[:, 2 * DEPTH:4 * DEPTH].rearrange("p (i l) -> p i l", l=DEPTH)

            def tables():
                split(1)
                dve.wait_ge(mem_hi, 1)
                for i in range(KT // 2):
                    m = slice(2 * i, 2 * i + 2)
                    last = low(YML[:, m, :].rearrange("p m t -> p (m t)"), PS[:, 1 + i, :],
                               YMH[:, m, :].rearrange("p m t -> p (m t)"))
                last.then_inc(mem_done, 1)
                dve.wait_ge(s_lam, 16 * 4)
                lq = stage_lam.rearrange("p (i l d) -> p i l d", l=DEPTH, d=DQK_A)
                for i in range(2):
                    products = stage_sq[:, i * P:(i + 1) * P].rearrange("p (l d) -> p l d", l=DEPTH)
                    o.link(v.tensor_tensor(products, lq[:, 2 * i], lq[:, 2 * i + 1], ALU.mult))
                    last = v.tensor_reduce(lsum[:, i, :], products, AX, ALU.add)
                last.then_inc(lam_ready, 1)
                dve.wait_ge(s_table, 16)
                dve.wait_ge(pool_done, 1)
                t8 = slice(0, DEPTH * H_B)
                tail = PT[t8, 768:768 + 2 * P]
                v.tensor_copy(tail[:, 0:P], PT[t8, 2 * P + REL_MAX + 1:2 * P + R])
                v.tensor_scalar(tail[:, P:2 * P], maskI[t8, 0:P], PT[t8, 2 * P + R - 1:2 * P + R], None,
                                ALU.add).then_inc(tail_done, 1)
                o.link(v.scalar_tensor_tensor(out=dist[:], in0=stage_iota, scalar=-1.0, in1=stage_iota, op0=ALU.mult,
                                              op1=ALU.max))
                v.memset(dist[0:CHUNK, P + CHUNK:2 * P], FAR).then_inc(dist_done, 1)

            def residual_and_lambda():
                dve.wait_ge(lam_exp, 1)
                for l in range(DEPTH):
                    o.link(v.tensor_tensor(neglam[:, l:l + 1], lexp[:, 1, l:l + 1], lexp[:, 0, l:l + 1], ALU.subtract))
                    o.link(v.tensor_scalar(neglam[:, l:l + 1], neglam[:, l:l + 1], -lam_inits[l], None, ALU.add))
                dve.wait_ge(router_hi, 1)
                low(routerl[:], router[:], routerh[:]).then_inc(router_lo, 1)
                dve.wait_ge(s_x, 16 * TB)
                for b in range(TB):
                    o.link(v.tensor_copy(H[:, b, :], N[:, b, :]))

            def turned(kind, layer):
                def affine(k):
                    name = f"{kind}{k}"
                    tile_ready.wait(dve, layer, TILE_AT[name] + 1)
                    for t in range(2):
                        last = v.tensor_scalar(TURN[k][:, t * SEQ:(t + 1) * SEQ],
                                               tile_bank(name)[:, t * SEQ:(t + 1) * SEQ],
                                               column(LG, NORM_ROW[kind], layer, 2 * k + t),
                                               column(LB, NORM_ROW[kind], layer, 2 * k + t), ALU.mult, ALU.add)
                    last.then_inc(tile_taken["v"].sem, 1)

                def split_rows(k):
                    name = f"{kind}{k}"
                    part_hi.wait(dve, layer, PARTED.index(name) + 1)
                    hi, lo = turned_places(name)
                    low(lo, TURN[k], hi).then_inc(turned_lo.sem, 1)

                affine(1)
                split_rows(0)
                affine(3)
                split_rows(1)
                split_rows(2)
                split_rows(3)

            def take(name, layer):
                tile_ready.wait(dve, layer, TILE_AT[name] + 1)
                bank = tile_bank(name)
                if name == "KI":
                    v.tensor_copy(QK[:, M_KI, :], bank[:, 0:SEQ])
                    last = v.tensor_scalar(WI[:].rearrange("p b h -> p (b h)"), bank[:, SEQ:SEQ + TB * H_IDX],
                                           float(H_IDX ** -0.5 * D_IDX ** -0.5), None, ALU.mult)
                else:
                    dst, src = destination(name)
                    last = v.tensor_copy(dst, src)
                last.then_inc(tile_taken["v"].sem, 1)

            def take_low(name, layer):
                part_hi.wait(dve, layer, PARTED.index(name) + 1)
                hi, lo, src = split_places(name)
                if name[:2] == "YA":
                    last = v.scalar_tensor_tensor(out=lo, in0=src, scalar=gain[:, bass.ds(layer, 1)], in1=hi,
                                                  op0=ALU.mult, op1=ALU.subtract)
                else:
                    last = low(lo, src, hi)
                last.then_inc(tile_taken["v"].sem, 1)

            def select(b, part, layer):
                n = NKEYS[b]
                score, rest = isc[:, 0:n], work[:, 0:n]
                if part == 0:
                    relu_done.wait(dve, layer, 2 - b)
                    tile_taken["v"].wait(dve, layer, TAKEN["v"].index("KI") + 1)
                    selected.wait(dve, layer, b)
                    for h in range(H_IDX):
                        o.link(v.scalar_tensor_tensor(out=score, in0=DOT[b][:, place(h, H_IDX), :],
                                                      scalar=WI[:, b, h:h + 1],
                                                      in1=maskI[:, 2 * P - n:] if h == 0 else score,
                                                      op0=ALU.mult, op1=ALU.add))
                    return
                rounds = TOPK // 16
                for i in range((part - 1) * rounds, part * rounds):
                    o.link(v.max(top8[:], score if i == 0 else rest))
                    o.link(v.match_replace(rest, top8[:], score if i == 0 else rest, GONE))
                if part == 1:
                    return
                o.link(v.tensor_scalar(rest, rest, 0.5 * GONE, -FAR, ALU.is_gt, ALU.mult))
                o.link(v.tensor_scalar(score, score, 0.5 * NEG_INF, -FAR, ALU.is_le, ALU.mult))
                keys = selb[:, 0:P] if b == 0 else selb[:, P:3 * P]
                v.tensor_tensor(keys, rest, score, ALU.min).then_inc(selected.sem, 1)

            def maxima(group, layer):
                i = GROUPS.index(group)
                scores_ready.wait(dve, layer, max(through(group), i + 1))
                n = maps_of(group)
                o.link(v.tensor_reduce(mx[:, i, 0:n].rearrange("p (a m) -> p a m", a=2), scores(group), AX,
                                       ALU.max))
                v.tensor_scalar(nmx[:, i, 0:n], mx[:, i, 0:n], -(SCALE_X if group[0] == "X" else SCALE), None,
                                ALU.mult).then_inc(max_done.sem, 1)

            def inverse_sums(group, layer):
                i = GROUPS.index(group)
                exp_done.wait(dve, layer, i + 1)
                n = maps_of(group)
                o.link(v.reciprocal(rs[:, i, 0:n], sums[:, i, 0:n]))
                return i

            def mix_maps(b, layer):
                group = f"A{b}"
                i = inverse_sums(group, layer)
                pair = lambda t, m: t[:, i, m * H_A:(m + 1) * H_A]
                o.link(v.scalar_tensor_tensor(out=mix[:], in0=pair(sums, 0), scalar=neglam[:, bass.ds(layer, 1)],
                                              in1=pair(rs, 1), op0=ALU.mult, op1=ALU.mult))
                for h in range(H_A):
                    e0, e1 = EV[group][:, h, :], EV[group][:, H_A + h, :]
                    last = v.scalar_tensor_tensor(out=e0, in0=e1, scalar=mix[:, h:h + 1], in1=e0,
                                                  op0=ALU.mult, op1=ALU.add)
                last.then_inc(probs_ready.sem, 1)

            def rows_a(b, layer):
                name = f"OA{b}"
                tile_ready.wait(dve, layer, TILE_AT[name] + 1)
                i = GROUPS.index(f"A{b}")
                rows = N[:, b, 0:512].rearrange("p (h d) -> p h d", h=H_A)
                r0 = rs[:, i, 0:H_A].rearrange("p (h u) -> p h u", u=1).to_broadcast([P, H_A, DV_A])
                v.tensor_tensor(rows, heads(tile_bank(name)), r0, ALU.mult).then_inc(tile_taken["v"].sem, 1)
                taken = TAKEN["v"].index(name) + 1
                tile_taken["v"].wait(dve, layer, taken)
                o.link(v.tensor_tensor(sq, rows, rows, ALU.mult))
                o.link(v.tensor_reduce(ss[:], sq, AX, ALU.add))
                v.tensor_scalar(ss[:], ss[:], 1.0 / DV_A, RMS_EPS, ALU.mult, ALU.add).then_inc(var_ready.sem, 1)
                rstd_ready.wait(dve, layer, 1 + b)
                o.link(v.tensor_tensor(rows, rows, rms[:].rearrange("p (h u) -> p h u", u=1)
                                       .to_broadcast([P, H_A, DV_A]), ALU.mult))

            def rows_bc(b, layer):
                name = f"OBC{b}"
                for g in "BC":
                    inverse_sums(f"{g}{b}", layer)
                tile_ready.wait(dve, layer, TILE_AT[name] + 1)
                for g, c in (("B", 0), ("C", 256)):
                    i = GROUPS.index(f"{g}{b}")
                    r = rs[:, i, 0:4].rearrange("p (a c u) -> p c a u", a=2, u=1).to_broadcast([P, 2, 2, 64])
                    cut = lambda t: t.rearrange("p (c a d) -> p c a d", c=2, a=2)
                    last = v.tensor_tensor(cut(N[:, b, 512 + c:768 + c]), cut(tile_bank(name)[:, c:c + 256]), r,
                                           ALU.mult)
                    if g == "B":
                        o.link(last)
                last.then_inc(tile_taken["v"].sem, 1)
                tile_taken["v"].wait(dve, layer, TAKEN["v"].index(name) + 1)

            def half_statistics(o, z, b, half):
                o.link(v.bn_stats(st[:, b, half, :], z[:, b, half * HALF:(half + 1) * HALF]))

            def variance(o, b):
                o.link(v.bn_aggr(mv[:, b, :], st[:, b].rearrange("p c s -> p (c s)")))
                v.tensor_scalar(var[:, b:b + 1], mv[:, b, 1:2], LN_EPS, None, ALU.add).then_inc(var_ready.sem, 1)

            def statistics(o, z, b, layer):
                for half in range(2):
                    half_statistics(o, z, b, half)
                variance(o, b)

            def normalise(z, b, which, layer):
                rstd_ready.wait(dve, layer, 3 + 2 * which + b)
                v.tensor_scalar(N[:, b, :], z[:, b, :], mv[:, b, 0:1], rstd[:, b:b + 1], ALU.subtract, ALU.mult
                                ).then_inc(norm_done.sem, 1)

            def residual_sum(half, b, first, layer):
                z = H[:, b, half * HALF:(half + 1) * HALF]
                v.scalar_tensor_tensor(out=z, in0=z, scalar=ALPHA, in1=PS[:, 2 * half + b, :], op0=ALU.mult,
                                       op1=ALU.add).then_inc(sum_done.sem, 1)

            def residual_rows(o, which, layer):
                norm_done.wait(dve, layer, 2 * which + 2)
                gb_loaded.wait(dve, layer, which + 1)
                for b in range(TB):
                    o.link(v.tensor_tensor(H[:, b, :], N[:, b, :], GB[:, 0, :], ALU.mult))
                o.link(v.tensor_tensor(H[:, 0, :], H[:, 0, :], GB[:, 1, :], ALU.add))
                v.tensor_tensor(H[:, 1, :], H[:, 1, :], GB[:, 1, :], ALU.add).then_inc(resid_done.sem, 1)
                resid_done.wait(dve, layer, which + 1)

            def sublayer_norm(which, layer):
                for half in range(2):
                    for b in range(TB):
                        acc_ready.wait(dve, layer, 8 * which + 4 * half + 2 + b + 1)
                        residual_sum(half, b, 4 * which, layer)
                        sum_done.wait(dve, layer, 4 * which + 2 * half + b + 1)
                        half_statistics(o, H, b, half)
                        if half == 1:
                            variance(o, b)
                for b in range(TB):
                    normalise(H, b, which, layer)

            def normalise_probs(b, layer):
                group = f"X{b}"
                i = inverse_sums(group, layer)
                r = rs[:, i, 0:4].rearrange("p (h u) -> p h u", u=1).to_broadcast([P, 4, N_MEM])
                v.tensor_tensor(EV[group], EV[group], r, ALU.mult).then_inc(probs_ready.sem, 1)

            def body(layer):
                for step in PLAN:
                    kind, name = step[0], step[1]
                    piece = f"{name}{step[2]}" if kind == "acc" else name
                    if piece in PIECE_AT:
                        g = FIRST[layer] + PIECE_AT[piece] + SLOTS - 1
                        if g < ALL:
                            split(g)
                    if kind == "tile":
                        if name[:2] in NORM_ROW:
                            if name[2] == "0":
                                turned(name[:2], layer)
                                if name == "HT0" and layer == 0:
                                    tables()
                        elif name[:2] == "OA":
                            rows_a(int(name[2]), layer)
                        elif name[:3] == "OBC":
                            rows_bc(int(name[3]), layer)
                            dve.sem_inc(rows_done.sem, 1)
                        elif step[2] == "v":
                            take(name, layer)
                        elif step[2] == "s":
                            take_low(name, layer)
                    elif kind == "select":
                        select(name, step[2], layer)
                    elif kind == "max":
                        maxima(name, layer)
                    elif kind == "mix":
                        if name == 0 and layer == 0:
                            residual_and_lambda()
                        mix_maps(name, layer)
                    elif kind == "over":
                        normalise_probs(name, layer)
                    elif kind == "norm":
                        sublayer_norm(name, layer)
                    elif kind == "residual":
                        residual_rows(o, name, layer)

            def feed_forward(layer):
                o = Order(dve, order_ffn)

                def split_ring(slot, made_):
                    dve.wait_ge(hi_done, made_)
                    r = slice(slot * PIECE, (slot + 1) * PIECE)
                    low(SPL[:, r], RAW[:, r], SPH[:, r]).then_inc(lo_done, 1)

                def hidden(p):
                    dve.wait_ge(ffn_silu, p + 1)
                    dve.wait_ge(ffn_u, p + 1)
                    dve.wait_ge(ffn_lo, p)
                    v.tensor_tensor(FHID, FSIL, PS[:, 5, :], ALU.mult).then_inc(ffn_hidden, 1)
                    dve.wait_ge(ffn_hi, p + 1)
                    low(FHL[:].rearrange("p f t -> p (f t)"), FHID, FHH[:].rearrange("p f t -> p (f t)")
                        ).then_inc(ffn_lo, 1)

                g = len(PIECES)
                split(g + 2)
                split(g + 3)
                hidden(0)
                split(g + 4)
                with dve.Fori(1, PAIRS - 1) as p:
                    split_ring((g + 2) % SLOTS, p * 3 + (g + 3))
                    split_ring((g + 3) % SLOTS, p * 3 + (g + 4))
                    hidden(p)
                    split_ring((g + 4) % SLOTS, p * 3 + (g + 5))
                split(FIRST[1] - 1)
                split(FIRST[1])
                hidden(PAIRS - 1)
                split(FIRST[1] + 1)
                for b in range(TB):
                    if b == 0:
                        dve.wait_ge(ffn_first_rows, 1)
                    else:
                        dve.wait_ge(ffn_down, PAIRS)
                    for half in range(2):
                        residual_sum(half, b, 8, layer)
                        sum_done.wait(dve, layer, 8 + 2 * b + half + 1)
                        half_statistics(o, H, b, half)
                    variance(o, b)
                for b in range(TB):
                    normalise(H, b, 2, layer)
                residual_rows(o, 2, layer)

            def mixture(layer):
                o = Order(dve, order_moe)
                def split1(c, k):
                    dve.wait_ge(hi1[c], k + 1)
                    low(S1L[c], flat["R1" + c][:], S1H[c]).then_inc(lo1[c], 1)

                def split3(c, k):
                    dve.wait_ge(hi3[c], k + 1)
                    low(S3L[c], flat["R3" + c][:], S3H[c]).then_inc(lo3[c], 1)

                def split2(c, k):
                    dve.wait_ge(hi2[c], k + 1)
                    low(S2L[c], R2[c][:], S2H[c]).then_inc(lo2[c], 1)

                EIGHT = slice(0, N_EXPERTS)
                o.link(v.memset(logit[:], FILL))
                o.link(v.memset(take1[:], FILL))
                o.link(v.memset(take2[:], FILL))
                dve.wait_ge(router_ready, 1)
                o.link(v.tensor_copy(logit[:, :, EIGHT], PS[:, 4, 0:16].rearrange("p (b e) -> p b e", b=TB)))
                for b in range(TB):
                    o.link(v.max(best[:, b, :], logit[:, b, EIGHT]))
                v.tensor_tensor(gw[:, :, 0:1], best[:, :, 1:2], best[:, :, 0:1], ALU.subtract
                                ).then_inc(logit_done, 1)
                o.link(v.tensor_copy(take1[:, :, 0:1], best[:, :, 0:1]))
                o.link(v.tensor_copy(take2[:, :, 0:2], best[:, :, 0:2]))
                for b in range(TB):
                    o.link(v.match_replace(left1[:, b, :], take1[:, b, :], logit[:, b, :], GONE))
                    o.link(v.match_replace(left2[:, b, :], take2[:, b, :], logit[:, b, :], GONE))
                o.link(v.tensor_scalar(gtmp[:], left1[:, :, EIGHT], 0.5 * GONE, None, ALU.is_le))
                v.tensor_scalar(chosen[:], left2[:, :, EIGHT], 0.5 * GONE, None, ALU.is_le).then_inc(chosen_done, 1)
                dve.wait_ge(exp2_done, 1)
                dve.wait_ge(chosen_done, 1)
                o.link(v.tensor_scalar(gw[:, :, 2:3], gw[:, :, 1:2], 1.0, None, ALU.add))
                o.link(v.reciprocal(gw[:, :, 2:3], gw[:, :, 2:3]))
                o.link(v.tensor_tensor(gw[:, :, 3:4], gw[:, :, 1:2], gw[:, :, 2:3], ALU.mult))
                for b in range(TB):
                    o.link(v.tensor_tensor(gate[:, b, :], chosen[:, b, :], gtmp[:, b, :], ALU.subtract))
                    o.link(v.tensor_scalar(gtmp[:, b, :], gtmp[:, b, :], gw[:, b, 2:3], None, ALU.mult))
                    o.link(v.scalar_tensor_tensor(out=gate[:, b, :], in0=gate[:, b, :], scalar=gw[:, b, 3:4],
                                                  in1=gtmp[:, b, :], op0=ALU.mult, op1=ALU.add))
                dve.wait_ge(rank_ready, 1)
                o.link(v.tensor_copy(rank[:].rearrange("p b e -> p (b e)"), PS[:, 5, 0:16]))
                o.link(v.tensor_scalar(ctmp[:], PS[0:1, 5, 16:24], float(P), None, ALU.is_gt))
                o.link(v.tensor_reduce(full[:, 3:4], ctmp[:], AX, ALU.add))
                o.link(v.tensor_scalar(ctmp[:], ctmp[:], -64.0, 64.0, ALU.mult, ALU.add))
                o.link(v.tensor_tensor(cand[:], ctmp[:], iota_s[0:1, EIGHT], ALU.add))
                for j in range(EXTRA):
                    o.link(v.tensor_reduce(full[:, j:j + 1], cand[:], AX, ALU.min))
                    o.link(v.tensor_scalar(ctmp[:], cand[:], full[:, j:j + 1], 64.0, ALU.is_equal, ALU.mult))
                    o.link(v.tensor_tensor(cand[:], cand[:], ctmp[:], ALU.add))
                o.link(v.tensor_scalar(full[:, 0:EXTRA], full[:, 0:EXTRA], float(N_EXPERTS - 1), None, ALU.min))
                v.tensor_copy(fulli[:], full[:]).then_inc(table_done, 1)
                dve.wait_ge(rows_hi, 1)
                for b in range(TB):
                    last = low(HRL[:, b, :], H[:, b, :], HRH[:, b, :])
                last.then_inc(rows_lo, 1)

                def onehots(e, n, base):
                    after(dve, gather_ready, n * 4)
                    after(dve, gatedT_ready, n)
                    for table, rows in ((chosen, ONE), (gate, GATED)):
                        for b in range(TB):
                            pick = lambda t: t[:].rearrange("p b e -> p (b e)")[:, bass.ds(e + b * N_EXPERTS, 1)]
                            last = v.tensor_scalar(rows[:, b, :], iota_s[:, base:base + P], pick(rank), pick(table),
                                                   ALU.is_equal, ALU.mult)
                        last.then_inc(onehot_done, 1)

                def gather(n):
                    for q, bank in enumerate((6, 3)):
                        after(dve, gather_ready, n * 4 + (q + 3))
                        last = v.tensor_copy(XGL[:, 4 * q:4 * q + 4, :], heads(PS[:, bank, :]))
                    last.then_inc(gather_lo, 1)

                def hidden(c, k):
                    after(dve, u_ready[c], k + 1)
                    after(dve, silu_done[c], k + 1)
                    after(dve, turned_ready[c], k)
                    v.tensor_tensor(HID[c], SIL[c], PS[:, 4 + (c == "b"), 0:FE], ALU.mult
                                    ).then_inc(hidden_done[c], 1)

                def take_turned(c, k):
                    dve.wait_ge(turned_hi[c], k + 1)
                    low(HTL[c], PS[:, 6 + (c == "b"), 0:FE], HTH[c]).then_inc(turned_done[c], 1)

                def item(e, n, ahead):
                    def step(c, k, last_turned, following):
                        if last_turned:
                            take_turned(*last_turned)
                        split1(*following)
                        split3(*following)
                        hidden(c, k)
                        split2(c, k)

                    k0 = n * STEPS
                    hidden("a", k0)
                    split2("a", k0)
                    step("b", k0, ("a", k0), ("a", k0 + 1))
                    if ahead:
                        onehots(e + 1, n + 1, 0)
                    with dve.Fori(1, STEPS - 1) as j:
                        step("a", k0 + j, ("b", k0 + j - 1), ("b", k0 + j))
                        step("b", k0 + j, ("a", k0 + j), ("a", k0 + j + 1))
                    k = k0 + (STEPS - 1)
                    step("a", k, ("b", k - 1), ("b", k))
                    take_turned("a", k)
                    hidden("b", k)
                    split2("b", k)
                    if ahead:
                        split1("a", k + 1)
                    take_turned("b", k)
                    if ahead:
                        gather(n + 1)
                    after(dve, w2_used["b"], k + 1)
                    v.tensor_copy(YE[:, HALF:D], PS[:, 1, :]).then_inc(y_dve, 1)
                    if ahead:
                        split3("a", k + 1)
                    after(dve, scatter_done, n * 4)
                    for i, bank in enumerate((7, 0, 1, 6)):
                        half, b = i // 2, i % 2
                        z = N[:, b, half * HALF:(half + 1) * HALF]
                        dve.wait_ge(scatter_ready, n * 4 + (i + 1))
                        v.tensor_tensor(z, z, PS[:, bank, :], ALU.add).then_inc(scatter_done, 1)
                    if ahead:
                        split1("b", k + 1)
                        split3("b", k + 1)
                    else:
                        after(dve, scatter_done, n * 4 + 4)

                onehots(0, 0, 0)
                split1("a", 0)
                gather(0)
                split3("a", 0)
                turned_lo.wait(dve, 1, 12)
                split1("b", 0)
                split3("b", 0)
                dve.wait_ge(total_begun, 1)
                with dve.Fori(0, N_EXPERTS - 1) as e:
                    item(e, e, True)
                item(N_EXPERTS - 1, N_EXPERTS - 1, False)

                def extra(e, n):
                    onehots(e, n, P)
                    for c in "ab":
                        split1(c, n * STEPS)
                        split3(c, n * STEPS)
                    gather(n)
                    item(e, n, False)

                extra_experts(dve, extra)
                for b in range(TB):
                    statistics(o, N, b, layer)
                gb_loaded.wait(dve, layer, 3)
                for b in range(TB):
                    normalise(N, b, 2, layer)
                    norm_done.wait(dve, layer, 4 + b + 1)
                    o.link(v.tensor_tensor(H[:, b, :], N[:, b, :], GB[:, 0, :], ALU.mult))
                    v.tensor_tensor(H[:, b, :], H[:, b, :], GB[:, 1, :], ALU.add).then_inc(out_ready, 1)

            for layer in range(DEPTH):
                body(layer)
                if layer == 0:
                    feed_forward(layer)
                else:
                    mixture(layer)


_INS = ['x', 'mem', 'w_in', 'lam_q1', 'lam_k1', 'lam_q2', 'lam_k2', 'diff_norm_g', 'rel_bias', 'w_out',
        'ln1_g', 'ln1_b', 'xattn_wq', 'xattn_wk', 'xattn_wv', 'xattn_wo', 'ln2_g', 'ln2_b',
        'ffn_w1', 'ffn_w3', 'ffn_w2', 'moe_router', 'moe_w1', 'moe_w3', 'moe_w2', 'ln3_g', 'ln3_b']


def kernel(**inputs):
    import numpy as _np
    import concourse.bacc as _bacc
    from concourse import mybir as _mybir
    from concourse.bass_utils import run_bass_kernel_spmd as _run

    nc = _bacc.Bacc("TRN2", target_bir_lowering=False, num_devices=1)
    arrays, args = {}, []
    for name in _INS:
        a = _np.ascontiguousarray(inputs[name])
        arrays[f"in_{name}_dram"] = a
        args.append(nc.dram_tensor(f"in_{name}_dram", a.shape, _mybir.dt.from_np(a.dtype), kind="ExternalInput").ap())
    out = nc.dram_tensor("out_0_dram", inputs["x"].shape, _mybir.dt.float32, kind="ExternalOutput").ap()
    hybrid_encoder(nc, *args, out)
    r = _run(nc, [arrays], core_ids=[0])
    return r.results[0]["out_0_dram"]
```
